# Optimizing a Trainium2 kernel written in Bass

```python
import math
import jax, jax.numpy as jnp
from jax import lax
import numpy as np
import jax
import jax.numpy as jnp

D_MODEL = 1024
BATCH = 1
SEQ = 512
DEPTH = 2

N_MIXERS = 2
N_A_LAYERS = (DEPTH + N_MIXERS - 1) // N_MIXERS
N_B_LAYERS = DEPTH // N_MIXERS

D_FF = 4 * D_MODEL
RMS_EPS = 1e-6
ROPE_THETA = 10000.0
N_MOD = 6

D_RNN = 1280
LRU_BLOCKS = 5
LRU_BLOCK = D_RNN // LRU_BLOCKS
CONV_WIDTH = 4
LRU_C = 8.0

N_HEADS = 16
HEAD_DIM = D_MODEL // N_HEADS
KV_DIM = HEAD_DIM
IDX_HEADS = 8
IDX_DIM = 64
TOPK_MAX = 256
Q_BLOCK = 128
B_WIDTHS = (N_HEADS * HEAD_DIM, KV_DIM, KV_DIM, IDX_HEADS * IDX_DIM, IDX_DIM, IDX_HEADS)
B_IN = sum(B_WIDTHS)
B_SPLITS = tuple(int(v) for v in np.cumsum(B_WIDTHS)[:-1])


def rmsnorm(x, g):
    x32 = x.astype(jnp.float32)
    y = x32 * lax.rsqrt(jnp.mean(x32 * x32, axis=-1, keepdims=True) + RMS_EPS)
    return (y * g.astype(jnp.float32)).astype(x.dtype)

def rope_tables(seq, dim):
    inv = ROPE_THETA ** (-jnp.arange(0, dim, 2, dtype=jnp.float32) / dim)
    ang = jnp.arange(seq, dtype=jnp.float32)[:, None] * inv[None, :]
    return jnp.cos(ang), jnp.sin(ang)

def apply_rope(x, cos, sin):
    half = x.shape[-1] // 2
    cos = cos[:, None, :].astype(x.dtype)
    sin = sin[:, None, :].astype(x.dtype)
    x1, x2 = x[..., :half], x[..., half:]
    return jnp.concatenate([x1 * cos - x2 * sin, x2 * cos + x1 * sin], axis=-1)

def rglru_mixer(h, w_in, conv_w, conv_b, wr, br, wi, bi, lam, w_out):
    B, S, _ = h.shape
    u = h @ w_in
    xb, gb = jnp.split(u, 2, axis=-1)
    gate = jax.nn.gelu(gb)
    xc = lax.conv_general_dilated(
        xb, conv_w[:, None, :].astype(xb.dtype), window_strides=(1,),
        padding=[(CONV_WIDTH - 1, 0)], dimension_numbers=("NWC", "WIO", "NWC"),
        feature_group_count=D_RNN) + conv_b
    xr = xc.reshape(B, S, LRU_BLOCKS, LRU_BLOCK)
    r = jax.nn.sigmoid(jnp.einsum("bsnc,ncd->bsnd", xr, wr).reshape(B, S, D_RNN) + br)
    i = jax.nn.sigmoid(jnp.einsum("bsnc,ncd->bsnd", xr, wi).reshape(B, S, D_RNN) + bi)
    log_a = -LRU_C * r.astype(jnp.float32) * jax.nn.softplus(-lam.astype(jnp.float32))
    a = jnp.exp(log_a)
    b = jnp.sqrt(-jnp.expm1(2.0 * log_a)) * (i * xc).astype(jnp.float32)

    def combine(left, right):
        a_l, b_l = left
        a_r, b_r = right
        return a_l * a_r, a_r * b_l + b_r

    _, hs = lax.associative_scan(combine, (a, b), axis=1)
    y = hs.astype(h.dtype) * gate
    return y @ w_out

def dsa_mixer(h, w_in, q_g, k_g, w_out):
    B, S, _ = h.shape
    topk = min(TOPK_MAX, S // 4)
    cos, sin = rope_tables(S, HEAD_DIM)
    cos_i, sin_i = rope_tables(S, IDX_DIM)
    u = h @ w_in
    q, k, v, qi, ki, wi = jnp.split(u, B_SPLITS, axis=-1)
    q = apply_rope(rmsnorm(q.reshape(B, S, N_HEADS, HEAD_DIM), q_g), cos, sin)
    k = apply_rope(rmsnorm(k, k_g)[:, :, None, :], cos, sin)[:, :, 0]
    qi = apply_rope(qi.reshape(B, S, IDX_HEADS, IDX_DIM), cos_i, sin_i)
    ki = apply_rope(ki[:, :, None, :], cos_i, sin_i)[:, :, 0]
    wi = wi * (IDX_HEADS ** -0.5)
    pos = jnp.arange(S)
    nb = S // Q_BLOCK

    def to_blocks(t):
        return t.reshape((B, nb, Q_BLOCK) + t.shape[2:]).swapaxes(0, 1)

    def block_fn(args):
        qb, qib, wib, posb = args
        logits = jnp.einsum("bqhd,bsd->bqhs", qib, ki) * (IDX_DIM ** -0.5)
        score = jnp.einsum("bqh,bqhs->bqs", wib, jax.nn.relu(logits)).astype(jnp.float32)
        causal = pos[None, :] <= posb[:, None]
        score = jnp.where(causal[None], score, -jnp.inf)
        _, idx = lax.top_k(score, topk)
        kg = jax.vmap(lambda kk, ii: kk[ii])(k, idx)
        vg = jax.vmap(lambda vv, ii: vv[ii])(v, idx)
        valid = idx <= posb[None, :, None]
        s = jnp.einsum("bqhd,bqkd->bqhk", qb, kg).astype(jnp.float32) * (HEAD_DIM ** -0.5)
        s = jnp.where(valid[:, :, None, :], s, -jnp.inf)
        p = jax.nn.softmax(s, axis=-1).astype(vg.dtype)
        return jnp.einsum("bqhk,bqkd->bqhd", p, vg)

    out = lax.map(block_fn, (to_blocks(q), to_blocks(qi), to_blocks(wi), pos.reshape(nb, Q_BLOCK)))
    out = out.swapaxes(0, 1).reshape(B, S, N_HEADS * HEAD_DIM)
    return out @ w_out

def first_inputs(seed: int = 0) -> dict:
    key = jax.random.key(seed)
    ks = iter(jax.random.split(key, 32))
    f32 = jnp.float32

    def nrm(shape, scale):
        return jax.random.normal(next(ks), shape, f32) * scale

    x = nrm((BATCH, SEQ, D_MODEL), 1.0)
    c = nrm((BATCH, D_MODEL), 1.0)
    norm_mix_g = 1.0 + nrm((DEPTH, D_MODEL), 0.02)
    norm_ffn_g = 1.0 + nrm((DEPTH, D_MODEL), 0.02)
    ada_w = nrm((DEPTH, D_MODEL, N_MOD * D_MODEL), D_MODEL ** -0.5)
    ada_b = nrm((DEPTH, N_MOD * D_MODEL), 0.01)
    a_w_in = nrm((N_A_LAYERS, D_MODEL, 2 * D_RNN), D_MODEL ** -0.5)
    a_conv_w = nrm((N_A_LAYERS, CONV_WIDTH, D_RNN), CONV_WIDTH ** -0.5)
    a_conv_b = nrm((N_A_LAYERS, D_RNN), 0.01)
    a_gate_r_w = nrm((N_A_LAYERS, LRU_BLOCKS, LRU_BLOCK, LRU_BLOCK), LRU_BLOCK ** -0.5)
    a_gate_r_b = nrm((N_A_LAYERS, D_RNN), 0.01)
    a_gate_i_w = nrm((N_A_LAYERS, LRU_BLOCKS, LRU_BLOCK, LRU_BLOCK), LRU_BLOCK ** -0.5)
    a_gate_i_b = nrm((N_A_LAYERS, D_RNN), 0.01)
    a_pow = jax.random.uniform(next(ks), (N_A_LAYERS, D_RNN), f32, 0.9, 0.999)
    s = a_pow ** (1.0 / LRU_C)
    a_lambda = jnp.log(s) - jnp.log1p(-s)
    a_w_out = nrm((N_A_LAYERS, D_RNN, D_MODEL), D_RNN ** -0.5)
    b_w_in = nrm((N_B_LAYERS, D_MODEL, B_IN), D_MODEL ** -0.5)
    b_q_norm_g = 1.0 + nrm((N_B_LAYERS, HEAD_DIM), 0.02)
    b_k_norm_g = 1.0 + nrm((N_B_LAYERS, KV_DIM), 0.02)
    b_w_out = nrm((N_B_LAYERS, N_HEADS * HEAD_DIM, D_MODEL), (N_HEADS * HEAD_DIM) ** -0.5)
    ffn_w1 = nrm((DEPTH, D_MODEL, D_FF), D_MODEL ** -0.5)
    ffn_w2 = nrm((DEPTH, D_FF, D_MODEL), D_FF ** -0.5)
    return {"x": x, "c": c, "norm_mix_g": norm_mix_g, "norm_ffn_g": norm_ffn_g,
            "ada_w": ada_w, "ada_b": ada_b, "a_w_in": a_w_in, "a_conv_w": a_conv_w,
            "a_conv_b": a_conv_b, "a_gate_r_w": a_gate_r_w, "a_gate_r_b": a_gate_r_b,
            "a_gate_i_w": a_gate_i_w, "a_gate_i_b": a_gate_i_b, "a_lambda": a_lambda,
            "a_w_out": a_w_out, "b_w_in": b_w_in, "b_q_norm_g": b_q_norm_g,
            "b_k_norm_g": b_k_norm_g, "b_w_out": b_w_out, "ffn_w1": ffn_w1, "ffn_w2": ffn_w2}

def first_block(x, c, norm_mix_g, norm_ffn_g, ada_w, ada_b, a_w_in, a_conv_w, a_conv_b,
              a_gate_r_w, a_gate_r_b, a_gate_i_w, a_gate_i_b, a_lambda, a_w_out,
              b_w_in, b_q_norm_g, b_k_norm_g, b_w_out, ffn_w1, ffn_w2):
    cond = jax.nn.silu(c)
    for i in range(DEPTH):
        mod = (cond @ ada_w[i] + ada_b[i])[:, None, :]
        sh1, sc1, g1, sh2, sc2, g2 = jnp.split(mod, N_MOD, axis=-1)
        j = i // N_MIXERS
        h = rmsnorm(x, norm_mix_g[i]) * (1.0 + sc1) + sh1
        if i % N_MIXERS == 0:
            y = rglru_mixer(h, a_w_in[j], a_conv_w[j], a_conv_b[j], a_gate_r_w[j], a_gate_r_b[j],
                            a_gate_i_w[j], a_gate_i_b[j], a_lambda[j], a_w_out[j])
        else:
            y = dsa_mixer(h, b_w_in[j], b_q_norm_g[j], b_k_norm_g[j], b_w_out[j])
        x = x + g1 * y
        h = rmsnorm(x, norm_ffn_g[i]) * (1.0 + sc2) + sh2
        x = x + g2 * (jnp.square(jax.nn.relu(h @ ffn_w1[i])) @ ffn_w2[i])
    return x


GRID_W = 64
CTX_LEN = 256
NORM_EPS = 1e-6

GDN_HEADS = 8
GDN_DK = 64
GDN_DV = 64
GDN_CONV = 5
GDN_CHUNK = 64
GDN_QK_W = GDN_HEADS * GDN_DK
GDN_V_W = GDN_HEADS * GDN_DV

MLA_HEADS = 8
MLA_NOPE = 64
MLA_ROPE = 32
MLA_V = 64
MLA_Q_LORA = 256
MLA_KV_LORA = 128

NA_HEADS = 8
NA_DIM = 64
NA_WIN_H = 8
NA_WIN_W = 16
NA_W = NA_HEADS * NA_DIM

GQA_HEADS = 8
GQA_KV_HEADS = 2
GQA_DIM = 64

D_FF_2 = -(-(8 * D_MODEL) // (3 * 256)) * 256

EVEN_SPLITS = (2 * GDN_QK_W + GDN_V_W, GDN_V_W, 2 * GDN_HEADS, 2 * GDN_HEADS, MLA_Q_LORA, MLA_KV_LORA, MLA_ROPE)
ODD_SPLITS = (NA_W, NA_W, NA_W, GQA_HEADS * GQA_DIM, GQA_KV_HEADS * GQA_DIM, GQA_KV_HEADS * GQA_DIM)
IN_EVEN = sum(EVEN_SPLITS)
IN_ODD = sum(ODD_SPLITS)
MIX_EVEN = GDN_V_W + MLA_HEADS * MLA_V
MIX_ODD = NA_W + GQA_HEADS * GQA_DIM
N_EVEN = (DEPTH + 1) // 2
N_ODD = DEPTH // 2


def split_cols(z, sizes):
    offs = [int(o) for o in np.cumsum(sizes)[:-1]]
    return jnp.split(z, offs, axis=-1)

def to_heads(t, n):
    return t.reshape(t.shape[0], t.shape[1], n, -1)

def rms_norm(x, g):
    xf = x.astype(jnp.float32)
    y = xf * lax.rsqrt(jnp.mean(xf * xf, -1, keepdims=True) + NORM_EPS)
    return (y * g.astype(jnp.float32)).astype(x.dtype)

def l2_normalize(x):
    xf = x.astype(jnp.float32)
    return (xf * lax.rsqrt(jnp.sum(xf * xf, -1, keepdims=True) + NORM_EPS)).astype(x.dtype)

def modulate(h, shift, scale):
    return h * (1.0 + scale) + shift

def swiglu(u, w_gate, w_up, w_down):
    return (jax.nn.silu(u @ w_gate) * (u @ w_up)) @ w_down

def axial_rope(n_tokens, rot_dim):
    t = jnp.arange(n_tokens, dtype=jnp.int32)
    row = (t // GRID_W).astype(jnp.float32)
    col = (t % GRID_W).astype(jnp.float32)
    n_freq = rot_dim // 4
    inv_freq = ROPE_THETA ** (-jnp.arange(n_freq, dtype=jnp.float32) / n_freq)
    ang = jnp.concatenate([row[:, None] * inv_freq, col[:, None] * inv_freq], -1)
    return jnp.cos(ang), jnp.sin(ang)

def apply_rope_2(x, cos, sin):
    half = x.shape[-1] // 2
    x1, x2 = x[..., :half], x[..., half:]
    cs, sn = cos[None, :, None, :], sin[None, :, None, :]
    return jnp.concatenate([x1 * cs - x2 * sn, x2 * cs + x1 * sn], -1).astype(x.dtype)

def short_conv(x, w):
    n_tap = w.shape[0]
    pad = n_tap // 2
    t_len = x.shape[1]
    xp = jnp.pad(x, ((0, 0), (pad, pad), (0, 0)))
    out = xp[:, 0:t_len] * w[0]
    for j in range(1, n_tap):
        out = out + xp[:, j:j + t_len] * w[j]
    return out

def blocked_attention(q, k, v, scale):
    b, tq, h, d = q.shape
    hk = k.shape[2]
    grp = h // hk
    nb = tq // Q_BLOCK
    qb = q.reshape(b, nb, Q_BLOCK, hk, grp, d).transpose(1, 0, 2, 3, 4, 5)

    def one_block(q_i):
        s = jnp.einsum('bqkgd,bskd->bkgqs', q_i, k).astype(jnp.float32) * scale
        p = jax.nn.softmax(s, axis=-1).astype(v.dtype)
        return jnp.einsum('bkgqs,bskd->bqkgd', p, v)

    o = lax.map(one_block, qb)
    return o.transpose(1, 0, 2, 3, 4, 5).reshape(b, tq, h, v.shape[-1])

def delta_rule_chunked(q, k, v, g, beta, s0):
    f32 = jnp.float32
    b, t_len, h, dk = q.shape
    dv = v.shape[-1]
    n = t_len // GDN_CHUNK
    cl = GDN_CHUNK

    def chunks(t):
        return jnp.moveaxis(t.astype(f32).reshape(b, n, cl, h, *t.shape[3:]), 3, 1)

    qc, kc, vc, gch, bc = chunks(q), chunks(k), chunks(v), chunks(g), chunks(beta)
    gc = jnp.cumsum(gch, -1)
    tril = jnp.tril(jnp.ones((cl, cl), bool))
    strict = jnp.tril(jnp.ones((cl, cl), bool), -1)
    decay = jnp.exp(jnp.where(tril, gc[..., :, None] - gc[..., None, :], -jnp.inf))
    kb = kc * bc[..., None]
    vb = vc * bc[..., None]
    m = jnp.where(strict, jnp.einsum('bhncd,bhnsd->bhncs', kb, kc) * decay, 0.0)
    eye = jnp.eye(cl, dtype=f32)
    tmat = lax.linalg.triangular_solve(m + eye, jnp.broadcast_to(eye, m.shape), left_side=True,
                                       lower=True, unit_diagonal=True)
    u = jnp.einsum('bhncs,bhnsv->bhncv', tmat, vb)
    w = jnp.einsum('bhncs,bhnsk->bhnck', tmat, kb * jnp.exp(gc)[..., None])
    qk = jnp.einsum('bhncd,bhnsd->bhncs', qc, kc) * decay
    q_dec = qc * jnp.exp(gc)[..., None]
    k_dec = kc * jnp.exp(gc[..., -1:] - gc)[..., None]
    g_last = jnp.exp(gc[..., -1])
    xs = tuple(jnp.moveaxis(t, 2, 0) for t in (u, w, qk, q_dec, k_dec, g_last))

    def step(s, inp):
        u_i, w_i, qk_i, qd_i, kd_i, gl_i = inp
        v_new = u_i - jnp.einsum('bhck,bhkv->bhcv', w_i, s)
        o_i = jnp.einsum('bhck,bhkv->bhcv', qd_i, s) + jnp.einsum('bhcs,bhsv->bhcv', qk_i, v_new)
        s = s * gl_i[..., None, None] + jnp.einsum('bhck,bhcv->bhkv', kd_i, v_new)
        return s, o_i

    s_fin, o = lax.scan(step, s0.astype(f32), xs)
    return s_fin, o.transpose(1, 0, 3, 2, 4).reshape(b, t_len, h, dv)

def gdn_prepare(qkv, a, bt, conv_w, a_log, dt_bias):
    b, t_len, _ = qkv.shape
    qkv = jax.nn.silu(short_conv(qkv, conv_w))
    q, k, v = jnp.split(qkv, [GDN_QK_W, 2 * GDN_QK_W], axis=-1)
    q = l2_normalize(q.reshape(b, t_len, GDN_HEADS, GDN_DK)) * (GDN_DK ** -0.5)
    k = l2_normalize(k.reshape(b, t_len, GDN_HEADS, GDN_DK))
    v = v.reshape(b, t_len, GDN_HEADS, GDN_DV)
    a = a.reshape(b, t_len, 2, GDN_HEADS).astype(jnp.float32)
    bt = bt.reshape(b, t_len, 2, GDN_HEADS).astype(jnp.float32)
    g = -jnp.exp(a_log.astype(jnp.float32)) * jax.nn.softplus(a + dt_bias.astype(jnp.float32))
    return q, k, v, g, jax.nn.sigmoid(bt)

def gdn_bidirectional(lat, ctx):
    q_l, k_l, v_l, g_l, b_l = lat
    q_c, k_c, v_c, g_c, b_c = ctx
    s0 = jnp.zeros((q_l.shape[0], GDN_HEADS, GDN_DK, GDN_DV), jnp.float32)
    s_cf, oc_f = delta_rule_chunked(q_c, k_c, v_c, g_c[:, :, 0], b_c[:, :, 0], s0)
    _, ol_f = delta_rule_chunked(q_l, k_l, v_l, g_l[:, :, 0], b_l[:, :, 0], s_cf)
    fl = lambda t: jnp.flip(t, 1)
    s_cb, oc_b = delta_rule_chunked(fl(q_c), fl(k_c), fl(v_c), fl(g_c[:, :, 1]), fl(b_c[:, :, 1]), s0)
    _, ol_b = delta_rule_chunked(fl(q_l), fl(k_l), fl(v_l), fl(g_l[:, :, 1]), fl(b_l[:, :, 1]), s_cb)
    return ol_f + fl(ol_b), oc_f + fl(oc_b)

def gdn_output(o, gate, out_norm):
    b, t_len, h, dv = o.shape
    o = rms_norm(o.astype(gate.dtype), out_norm)
    return (o * jax.nn.silu(gate.reshape(b, t_len, h, dv))).reshape(b, t_len, h * dv)

def mla_q(q_down, q_norm, w_q_up, rope):
    b, t_len, _ = q_down.shape
    q = (rms_norm(q_down, q_norm) @ w_q_up).reshape(b, t_len, MLA_HEADS, MLA_NOPE + MLA_ROPE)
    if rope is None:
        return q
    return jnp.concatenate([q[..., :MLA_NOPE], apply_rope_2(q[..., MLA_NOPE:], *rope)], -1)

def mla_kv(kv_down, k_pe, kv_norm, w_kv_up, rope):
    b, t_len, _ = kv_down.shape
    kv = (rms_norm(kv_down, kv_norm) @ w_kv_up).reshape(b, t_len, MLA_HEADS, MLA_NOPE + MLA_V)
    k_pe = k_pe[:, :, None, :]
    if rope is not None:
        k_pe = apply_rope_2(k_pe, *rope)
    k = jnp.concatenate([kv[..., :MLA_NOPE], jnp.broadcast_to(k_pe, (b, t_len, MLA_HEADS, MLA_ROPE))], -1)
    return k, kv[..., MLA_NOPE:]

def neighbourhood_attention(q, k, v, k_ctx, v_ctx, rpb):
    b, s_len, h, d = q.shape
    rows = s_len // GRID_W
    kh = min(NA_WIN_H, rows)
    kw = NA_WIN_W
    nk = kh * kw
    r = jnp.arange(rows)
    col = jnp.arange(GRID_W)
    rs = jnp.clip(r - kh // 2, 0, rows - kh)
    cs = jnp.clip(col - kw // 2, 0, GRID_W - kw)
    kr = rs[:, None] + jnp.arange(kh)
    kc = cs[:, None] + jnp.arange(kw)
    idx = (kr[:, None, :, None] * GRID_W + kc[None, :, None, :]).reshape(rows, GRID_W * nk)
    dr = kr - r[:, None] + (NA_WIN_H - 1)
    dc = kc - col[:, None] + (NA_WIN_W - 1)
    bias = rpb[:, dr[:, None, :, None], dc[None, :, None, :]]
    bias = bias.reshape(h, rows, GRID_W, nk).transpose(1, 0, 2, 3).astype(jnp.float32)
    qr = q.reshape(b, rows, GRID_W, h, d).transpose(1, 0, 2, 3, 4)
    scale = d ** -0.5

    def row_block(inp):
        q_i, idx_i, b_i = inp
        kg = jnp.take(k, idx_i, axis=1).reshape(b, GRID_W, nk, h, d)
        vg = jnp.take(v, idx_i, axis=1).reshape(b, GRID_W, nk, h, d)
        s_loc = jnp.einsum('bqhd,bqnhd->bhqn', q_i, kg).astype(jnp.float32) * scale + b_i[None]
        s_ctx = jnp.einsum('bqhd,bshd->bhqs', q_i, k_ctx).astype(jnp.float32) * scale
        p = jax.nn.softmax(jnp.concatenate([s_loc, s_ctx], -1), axis=-1).astype(v.dtype)
        return (jnp.einsum('bhqn,bqnhd->bqhd', p[..., :nk], vg)
                + jnp.einsum('bhqs,bshd->bqhd', p[..., nk:], v_ctx))

    o = lax.map(row_block, (qr, idx, bias))
    return o.transpose(1, 0, 2, 3, 4).reshape(b, s_len, h, d)

def even_mixer(u_lat, u_ctx, need_ctx, w_in, w_out, conv_w, a_log, dt_bias, out_norm,
               q_norm, w_q_up, kv_norm, w_kv_up, rope):
    b, s_len, _ = u_lat.shape
    lat = split_cols(u_lat @ w_in, EVEN_SPLITS)
    ctx = split_cols(u_ctx @ w_in, EVEN_SPLITS)
    o_lat, o_ctx = gdn_bidirectional(gdn_prepare(lat[0], lat[2], lat[3], conv_w, a_log, dt_bias),
                                     gdn_prepare(ctx[0], ctx[2], ctx[3], conv_w, a_log, dt_bias))
    a_lat = gdn_output(o_lat, lat[1], out_norm)
    k_c, v_c = mla_kv(ctx[5], ctx[6], kv_norm, w_kv_up, None)
    k_l, v_l = mla_kv(lat[5], lat[6], kv_norm, w_kv_up, rope)
    q_l = mla_q(lat[4], q_norm, w_q_up, rope)
    scale = (MLA_NOPE + MLA_ROPE) ** -0.5
    b_lat = blocked_attention(q_l, jnp.concatenate([k_c, k_l], 1), jnp.concatenate([v_c, v_l], 1), scale)
    y_lat = jnp.concatenate([a_lat, b_lat.reshape(b, s_len, -1)], -1) @ w_out
    if not need_ctx:
        return y_lat, None
    l_len = u_ctx.shape[1]
    a_ctx = gdn_output(o_ctx, ctx[1], out_norm)
    b_ctx = blocked_attention(mla_q(ctx[4], q_norm, w_q_up, None), k_c, v_c, scale)
    y_ctx = jnp.concatenate([a_ctx, b_ctx.reshape(b, l_len, -1)], -1) @ w_out
    return y_lat, y_ctx

def odd_mixer(u_lat, u_ctx, need_ctx, w_in, w_out, rpb, q_norm, k_norm, rope):
    b, s_len, _ = u_lat.shape
    lat = split_cols(u_lat @ w_in, ODD_SPLITS)
    ctx = split_cols(u_ctx @ w_in, ODD_SPLITS)
    kn_c, vn_c = to_heads(ctx[1], NA_HEADS), to_heads(ctx[2], NA_HEADS)
    c_lat = neighbourhood_attention(to_heads(lat[0], NA_HEADS), to_heads(lat[1], NA_HEADS),
                                    to_heads(lat[2], NA_HEADS), kn_c, vn_c, rpb)
    kd_c = rms_norm(to_heads(ctx[4], GQA_KV_HEADS), k_norm)
    vd_c = to_heads(ctx[5], GQA_KV_HEADS)
    qd_l = apply_rope_2(rms_norm(to_heads(lat[3], GQA_HEADS), q_norm), *rope)
    kd_l = apply_rope_2(rms_norm(to_heads(lat[4], GQA_KV_HEADS), k_norm), *rope)
    scale = GQA_DIM ** -0.5
    d_lat = blocked_attention(qd_l, jnp.concatenate([kd_c, kd_l], 1),
                              jnp.concatenate([vd_c, to_heads(lat[5], GQA_KV_HEADS)], 1), scale)
    y_lat = jnp.concatenate([c_lat.reshape(b, s_len, -1), d_lat.reshape(b, s_len, -1)], -1) @ w_out
    if not need_ctx:
        return y_lat, None
    l_len = u_ctx.shape[1]
    c_ctx_o = blocked_attention(to_heads(ctx[0], NA_HEADS), kn_c, vn_c, NA_DIM ** -0.5)
    d_ctx = blocked_attention(rms_norm(to_heads(ctx[3], GQA_HEADS), q_norm), kd_c, vd_c, scale)
    y_ctx = jnp.concatenate([c_ctx_o.reshape(b, l_len, -1), d_ctx.reshape(b, l_len, -1)], -1) @ w_out
    return y_lat, y_ctx

def second_inputs(seed: int = 0) -> dict:
    key = jax.random.key(seed)
    ks = iter(jax.random.split(key, 40))
    f32 = jnp.float32

    def nrm(shape, scale):
        return jax.random.normal(next(ks), shape, f32) * scale

    def gain(shape):
        return 1.0 + 0.05 * jax.random.normal(next(ks), shape, f32)

    d = D_MODEL
    x = nrm((BATCH, SEQ, d), 1.0)
    c = nrm((BATCH, d), 1.0)
    ctx = nrm((BATCH, CTX_LEN, d), 1.0)
    c_ctx = nrm((d,), 1.0)
    w_mod = nrm((DEPTH, d, 6 * d), 0.5 * d ** -0.5)
    b_mod = nrm((DEPTH, 6 * d), 0.01)
    g_pre_mix = gain((DEPTH, d))
    g_post_mix = gain((DEPTH, d))
    g_pre_ffn = gain((DEPTH, d))
    g_post_ffn = gain((DEPTH, d))
    w_ffn_gate = nrm((DEPTH, d, D_FF_2), d ** -0.5)
    w_ffn_up = nrm((DEPTH, d, D_FF_2), d ** -0.5)
    w_ffn_down = nrm((DEPTH, D_FF_2, d), D_FF_2 ** -0.5)
    w_in_even = nrm((N_EVEN, d, IN_EVEN), d ** -0.5)
    w_out_even = nrm((N_EVEN, MIX_EVEN, d), MIX_EVEN ** -0.5)
    gdn_conv = nrm((N_EVEN, GDN_CONV, 2 * GDN_QK_W + GDN_V_W), GDN_CONV ** -0.5)
    gdn_a_log = jnp.log(jax.random.uniform(next(ks), (N_EVEN, 2, GDN_HEADS), f32, 1.0, 16.0))
    dt = jnp.exp(jax.random.uniform(next(ks), (N_EVEN, 2, GDN_HEADS), f32,
                                    float(np.log(1e-3)), float(np.log(1e-1))))
    gdn_dt_bias = dt + jnp.log(-jnp.expm1(-dt))
    gdn_out_norm = gain((N_EVEN, GDN_DV))
    mla_q_norm = gain((N_EVEN, MLA_Q_LORA))
    mla_w_q_up = nrm((N_EVEN, MLA_Q_LORA, MLA_HEADS * (MLA_NOPE + MLA_ROPE)), MLA_Q_LORA ** -0.5)
    mla_kv_norm = gain((N_EVEN, MLA_KV_LORA))
    mla_w_kv_up = nrm((N_EVEN, MLA_KV_LORA, MLA_HEADS * (MLA_NOPE + MLA_V)), MLA_KV_LORA ** -0.5)
    w_in_odd = nrm((N_ODD, d, IN_ODD), d ** -0.5)
    w_out_odd = nrm((N_ODD, MIX_ODD, d), MIX_ODD ** -0.5)
    na_rpb = nrm((N_ODD, NA_HEADS, 2 * NA_WIN_H - 1, 2 * NA_WIN_W - 1), 0.1)
    gqa_q_norm = gain((N_ODD, GQA_DIM))
    gqa_k_norm = gain((N_ODD, GQA_DIM))
    return {'x': x, 'c': c, 'ctx': ctx, 'c_ctx': c_ctx, 'w_mod': w_mod, 'b_mod': b_mod,
            'g_pre_mix': g_pre_mix, 'g_post_mix': g_post_mix, 'g_pre_ffn': g_pre_ffn,
            'g_post_ffn': g_post_ffn, 'w_ffn_gate': w_ffn_gate, 'w_ffn_up': w_ffn_up,
            'w_ffn_down': w_ffn_down, 'w_in_even': w_in_even, 'w_out_even': w_out_even,
            'gdn_conv': gdn_conv, 'gdn_a_log': gdn_a_log, 'gdn_dt_bias': gdn_dt_bias,
            'gdn_out_norm': gdn_out_norm, 'mla_q_norm': mla_q_norm, 'mla_w_q_up': mla_w_q_up,
            'mla_kv_norm': mla_kv_norm, 'mla_w_kv_up': mla_w_kv_up, 'w_in_odd': w_in_odd,
            'w_out_odd': w_out_odd, 'na_rpb': na_rpb, 'gqa_q_norm': gqa_q_norm, 'gqa_k_norm': gqa_k_norm}

def second_block(x, c, ctx, c_ctx, w_mod, b_mod, g_pre_mix, g_post_mix, g_pre_ffn, g_post_ffn,
              w_ffn_gate, w_ffn_up, w_ffn_down, w_in_even, w_out_even, gdn_conv, gdn_a_log,
              gdn_dt_bias, gdn_out_norm, mla_q_norm, mla_w_q_up, mla_kv_norm, mla_w_kv_up,
              w_in_odd, w_out_odd, na_rpb, gqa_q_norm, gqa_k_norm):
    s_len = x.shape[1]
    rope_mla = axial_rope(s_len, MLA_ROPE)
    rope_gqa = axial_rope(s_len, GQA_DIM)
    h, hc = x, ctx
    for i in range(DEPTH):
        last = i == DEPTH - 1
        mod = (jax.nn.silu(c) @ w_mod[i] + b_mod[i])[:, None, :]
        mod_c = (jax.nn.silu(c_ctx) @ w_mod[i] + b_mod[i])[None, None, :]
        sh_m, sc_m, gt_m, sh_f, sc_f, gt_f = jnp.split(mod, 6, axis=-1)
        csh_m, csc_m, cgt_m, csh_f, csc_f, cgt_f = jnp.split(mod_c, 6, axis=-1)
        u = modulate(rms_norm(h, g_pre_mix[i]), sh_m, sc_m)
        uc = modulate(rms_norm(hc, g_pre_mix[i]), csh_m, csc_m)
        j = i // 2
        if i % 2 == 0:
            y, yc = even_mixer(u, uc, not last, w_in_even[j], w_out_even[j], gdn_conv[j], gdn_a_log[j],
                               gdn_dt_bias[j], gdn_out_norm[j], mla_q_norm[j], mla_w_q_up[j],
                               mla_kv_norm[j], mla_w_kv_up[j], rope_mla)
        else:
            y, yc = odd_mixer(u, uc, not last, w_in_odd[j], w_out_odd[j], na_rpb[j],
                              gqa_q_norm[j], gqa_k_norm[j], rope_gqa)
        h = h + gt_m * rms_norm(y, g_post_mix[i])
        f = swiglu(modulate(rms_norm(h, g_pre_ffn[i]), sh_f, sc_f), w_ffn_gate[i], w_ffn_up[i], w_ffn_down[i])
        h = h + gt_f * rms_norm(f, g_post_ffn[i])
        if not last:
            hc = hc + cgt_m * rms_norm(yc, g_post_mix[i])
            fc = swiglu(modulate(rms_norm(hc, g_pre_ffn[i]), csh_f, csc_f), w_ffn_gate[i], w_ffn_up[i], w_ffn_down[i])
            hc = hc + cgt_f * rms_norm(fc, g_post_ffn[i])
    return h


def setup_inputs(seed=0):
    out = dict(first_inputs(seed))
    for name, value in second_inputs(seed + 1).items():
        if name != "x":
            out[name + "_2"] = value
    return out


def reference(
    x, c, norm_mix_g, norm_ffn_g, ada_w, ada_b, a_w_in, a_conv_w, a_conv_b, a_gate_r_w,
    a_gate_r_b, a_gate_i_w, a_gate_i_b, a_lambda, a_w_out, b_w_in, b_q_norm_g, b_k_norm_g,
    b_w_out, ffn_w1, ffn_w2, c_2, ctx_2, c_ctx_2, w_mod_2, b_mod_2, g_pre_mix_2, g_post_mix_2,
    g_pre_ffn_2, g_post_ffn_2, w_ffn_gate_2, w_ffn_up_2, w_ffn_down_2, w_in_even_2,
    w_out_even_2, gdn_conv_2, gdn_a_log_2, gdn_dt_bias_2, gdn_out_norm_2, mla_q_norm_2,
    mla_w_q_up_2, mla_kv_norm_2, mla_w_kv_up_2, w_in_odd_2, w_out_odd_2, na_rpb_2, gqa_q_norm_2,
    gqa_k_norm_2,
):
    x = first_block(
        x, c, norm_mix_g, norm_ffn_g, ada_w, ada_b, a_w_in, a_conv_w, a_conv_b, a_gate_r_w,
        a_gate_r_b, a_gate_i_w, a_gate_i_b, a_lambda, a_w_out, b_w_in, b_q_norm_g, b_k_norm_g,
        b_w_out, ffn_w1, ffn_w2,
    )
    return second_block(
        x, c_2, ctx_2, c_ctx_2, w_mod_2, b_mod_2, g_pre_mix_2, g_post_mix_2, g_pre_ffn_2,
        g_post_ffn_2, w_ffn_gate_2, w_ffn_up_2, w_ffn_down_2, w_in_even_2, w_out_even_2,
        gdn_conv_2, gdn_a_log_2, gdn_dt_bias_2, gdn_out_norm_2, mla_q_norm_2, mla_w_q_up_2,
        mla_kv_norm_2, mla_w_kv_up_2, w_in_odd_2, w_out_odd_2, na_rpb_2, gqa_q_norm_2,
        gqa_k_norm_2,
    )


_drawn_inputs = setup_inputs


def setup_inputs(seed=0):
    import zlib

    import numpy as np

    out = dict(_drawn_inputs(seed))
    spreads = {}
    factors = {'norm_mix_g': 3.137,
     'norm_ffn_g': 3.414,
     'a_conv_b': 3.861,
     'a_gate_r_b': 8.0,
     'a_gate_i_b': 8.0,
     'b_q_norm_g': 8.0,
     'b_k_norm_g': 8.0,
     'b_mod_2': 6.067,
     'g_pre_mix_2': 5.113,
     'g_post_mix_2': 7.026,
     'g_pre_ffn_2': 4.87,
     'g_post_ffn_2': 21.812,
     'gdn_a_log_2': 3.469,
     'gdn_out_norm_2': 8.0,
     'mla_q_norm_2': 8.0,
     'mla_w_q_up_2': 3.057,
     'mla_kv_norm_2': 8.0,
     'na_rpb_2': 64.0,
     'gqa_q_norm_2': 21.572,
     'gqa_k_norm_2': 8.0}
    for name, (base, spread) in spreads.items():
        noise = np.random.default_rng([zlib.crc32(name.encode()), seed]).standard_normal(out[name].shape)
        drawn = base * np.exp(spread * noise) if base else spread * noise
        out[name] = jnp.asarray(drawn.astype(out[name].dtype))
    for name, factor in factors.items():
        out[name] = (out[name] * factor).astype(out[name].dtype)
    return out
```

```python
from contextlib import ExitStack

import numpy as np

import concourse.bass as bass
from concourse import mybir

F32 = mybir.dt.float32
ALU = mybir.AluOpType
ACT = mybir.ActivationFunctionType
AXX = mybir.AxisListType.X

S, C, ST = 512, 256, 768
NEG = -1.0e30
GONE = -3.0e38
PANEL = 32


def weight_plan():
    plan = []

    def stat(name, nmt, nkt, mt0=0):
        for m in range(mt0, mt0 + nmt):
            plan.extend((name, k, m) for k in range(nkt))

    def mov(name, nkt, mt0, n):
        while len(plan) % n:
            plan.append(None)
        for k in range(nkt):
            plan.extend((name, k, mt0 + j) for j in range(n))

    def ada(name):
        for q in range(12):
            mov(name, 8, 4 * q, 4)

    ada("ada0")
    stat("a_in", 10, 8)
    for n in range(5):
        for d in range(2):
            for g in ("gr", "gi"):
                plan.extend((g, 2 * n + k, d) for k in range(2))
    stat("a_in", 10, 8, 10)
    stat("a_out", 8, 10)
    stat("f1_0", 32, 8)
    stat("f2_0", 8, 32)
    ada("ada1")
    stat("b_in", 14, 8)
    stat("b_in", 1, 8, 14)
    stat("b_out", 8, 8)
    stat("f1_1", 32, 8)
    stat("f2_1", 8, 32)
    ada("mod0")
    stat("e_in", 20, 8)
    stat("e_in", 1, 8, 20)
    mov("kvv", 1, 0, 4)
    for h in range(8):
        stat("qup", 1, 2, h)
        stat("kvk", 1, 1, h)
    stat("e_out", 8, 8)
    for i in range(2):
        if i:
            ada("mod1")
            stat("o_in", 14, 8)
            mov("nav", 8, 0, 4)
            stat("gv", 1, 8)
            stat("o_out", 8, 8)
        for m in range(22):
            stat(f"g_{i}", 1, 8, m)
            stat(f"u_{i}", 1, 8, m)
        stat(f"d_{i}", 8, 22)
    return plan


CONSTS = {}
for _n, _w in (("ident", 128), ("ones", 128), ("bd64", 128), ("rot64", 128), ("rot32", 128),
               ("triF", 128), ("triB", 128), ("negF", 128), ("negB", 128),
               ("lvF", 896), ("lvB", 896), ("causal", 128), ("namask", 64),
               ("cosM", 512), ("sinM", 512), ("eps", 1)):
    CONSTS[_n] = (sum(w for _, w in CONSTS.values()), _w)
NCONST = sum(w for _, w in CONSTS.values())
PARAMS = {}
for _n, _w in (("gmix", 16), ("gffn", 16), ("ada_b", 96), ("convw", 40), ("convb", 10), ("rb", 10), ("ib", 10),
               ("lam", 10), ("qg", 1), ("kg", 1), ("c1", 8), ("c2", 16), ("mod_b", 96), ("gpm", 16), ("gqm", 16),
               ("gpf", 16), ("gqf", 16), ("gconv", 60), ("alog", 16), ("dtb", 16), ("onorm", 1), ("mqn", 2),
               ("mkn", 1), ("gqn", 1), ("gkn", 1)):
    PARAMS[_n] = (sum(w for _, w in PARAMS.values()), _w)
NPARAM = sum(w for _, w in PARAMS.values())


def constants():
    p = np.arange(128)
    c = {"ident": np.eye(128), "ones": np.ones((128, 128)), "eps": np.full((128, 1), 1e-6)}
    c["bd64"] = (p[:, None] // 64 == p[None] // 64)

    def rot(base, head, half, n=128):
        m = np.zeros((128, 128))
        for o in range(base, n, head):
            for j in range(half):
                m[o + half + j, o + j] = -1.0
                m[o + j, o + half + j] = 1.0
        return m

    c["rot64"] = rot(0, 64, 32)
    c["rot32"] = rot(64, 64, 16, 96)
    c["triF"] = p[:, None] <= p[None]
    c["triB"] = p[:, None] >= p[None]
    c["negF"] = np.where(c["triF"], 0.0, NEG)
    c["negB"] = np.where(c["triB"], 0.0, NEG)
    lv = []
    for k in range(7):
        s = 1 << k
        i, j = p[:, None] // s, p[None] // s
        lv.append((i // 2 == j // 2) & (i == j + 1))
    c["lvF"] = np.concatenate(lv, 1)
    c["lvB"] = np.concatenate([m.T for m in lv], 1)
    c["causal"] = np.where(p[None] <= p[:, None], 0.0, NEG)
    col = p % 64
    cs = np.clip(col - 8, 0, 48)
    kc = np.arange(64)
    c["namask"] = np.where((kc[None] >= cs[:, None]) & (kc[None] < cs[:, None] + 16), 0.0, NEG)
    t = np.arange(S)

    def axial(rot_dim):
        n = rot_dim // 4
        inv = (np.float32(10000.0) ** (-np.arange(n, dtype=np.float32) / np.float32(n))).astype(np.float32)
        row, cl = (t // 64).astype(np.float32), (t % 64).astype(np.float32)
        return np.concatenate([row[:, None] * inv, cl[:, None] * inv], -1).astype(np.float32)

    a = axial(32).T
    c["cosM"] = np.zeros((128, S))
    c["sinM"] = np.zeros((128, S))
    c["cosM"][64:96] = np.cos(np.concatenate([a, a], 0))
    c["sinM"][64:96] = np.sin(np.concatenate([a, a], 0))
    inv = (np.float32(10000.0) ** (-np.arange(0, 64, 2, dtype=np.float32) / np.float32(64))).astype(np.float32)
    ang = (t.astype(np.float32)[:, None] * inv[None]).astype(np.float32).T
    ropes = []
    for a in (ang, axial(64).T):
        a4 = np.concatenate([a] * 4, 0)
        ropes += [np.cos(a4), np.sin(a4)]
    cst = np.concatenate([np.asarray(c[n], np.float32).reshape(128, w) for n, (_, w) in CONSTS.items()], 1)
    return np.ascontiguousarray(cst), np.ascontiguousarray(np.concatenate(ropes, 1).astype(np.float32))


class Op:
    __slots__ = ("eng", "fn", "waits", "marked", "sem", "val", "dma")

    def __init__(self, eng, fn, waits, dma):
        self.eng, self.fn, self.waits, self.dma = eng, fn, waits, dma
        self.marked = False
        self.sem = self.val = None


def flat(ws):
    for w in ws:
        if w is None:
            continue
        if isinstance(w, Op):
            yield w
        else:
            yield from flat(w)


class Queues:

    NDMA = 12

    def __init__(self):
        self.q = {e: [] for e in "pvagsd"}
        self.fence = {e: [] for e in self.q}

    def op(self, eng, fn, *waits, dma=False):
        ws = list(flat(waits)) + self.fence[eng]
        self.fence[eng] = []
        for w in ws:
            w.marked = True
        o = Op(eng, fn, ws, dma)
        self.q[eng].append(o)
        return o

    def barrier(self, engines="pvag"):
        last = [next((o for o in reversed(self.q[e]) if not o.dma), None) for e in "pvag"]
        last = [o for o in last if o]
        last += [o for o in self.q["a"][-40:] if o.dma]
        for e in engines:
            self.fence[e] = [o for o in last if o.eng != e or o.dma] + [o for o in last if o.eng == e]

    def number(self, sems, dsems):
        for e, ops in self.q.items():
            n = d = 0
            for o in ops:
                if o.dma:
                    o.sem, o.val = dsems[e][d % self.NDMA], 16 * (d // self.NDMA + 1)
                    d += 1
                elif o.marked:
                    n += 1
                    o.sem, o.val = sems[e], n

    def emit(self, e, eng):
        seen = {}

        def wait(sem, val):
            if seen.get(id(sem), 0) < val:
                eng.wait_ge(sem, val)
                seen[id(sem)] = val

        for o in self.q[e]:
            for w in o.waits:
                wait(w.sem, w.val)
            if o.dma:
                if o.val > 16:
                    wait(o.sem, o.val - 16)
                o.fn(eng).then_inc(o.sem, 16)
            else:
                ins = o.fn(eng)
                if o.marked:
                    ins.then_inc(o.sem, 1)
        last = {}
        for o in self.q[e]:
            if o.dma:
                last[id(o.sem)] = o
        for o in last.values():
            wait(o.sem, o.val)


class Slot:
    def __init__(self, ap):
        self.ap, self.free = ap, []


class Ring:

    def __init__(self, aps):
        self.slots, self.n = [Slot(a) for a in aps], 0

    def take(self):
        s = self.slots[self.n % len(self.slots)]
        self.n += 1
        return s


def program(nc, d_w, d_const, d_rope, d_par, d_rpb, d_x, d_ctx, d_out, d_dbg=None, stop=None):
    plan = weight_plan()
    npanel = -(-len(plan) // PANEL)
    Q = Queues()
    with ExitStack() as es:
        SB = es.enter_context(nc.sbuf_tensor("SB", [128, 52000], F32))
        PSB = es.enter_context(nc.psum_tensor("PSB", [128, 8 * 512], F32))
        pos = [0]

        def alloc(n):
            a = SB[:, pos[0]:pos[0] + n]
            pos[0] += n
            assert pos[0] <= 52000, pos[0]
            return a

        def tiles(n, w):
            a = alloc(n * w)
            return [a[:, i * w:(i + 1) * w] for i in range(n)]

        cst, par = alloc(NCONST), alloc(NPARAM)
        K = {n: cst[:, o:o + w] for n, (o, w) in CONSTS.items()}
        Pm = {n: par[:, o:o + w] for n, (o, w) in PARAMS.items()}
        ident, ones = K["ident"], K["ones"]
        X = tiles(8, S)
        XC = tiles(8, C)
        NSLOT = 2
        wslot = tiles(NSLOT, PANEL * 128)
        MOD1 = alloc(96)
        MOD2 = alloc(192)
        SMALL = alloc(1200)
        spos = [0]

        def small(n):
            a = SMALL[:, spos[0]:spos[0] + n]
            spos[0] += n
            assert spos[0] <= 1200
            return a

        banks = [PSB[:, i * 512:(i + 1) * 512] for i in range(8)]
        bank_slots = Ring(banks)

        def mm(out, lhsT, rhs, start, stop_, *w):
            return Q.op("p", lambda e: e.matmul(out, lhsT, rhs, start=start, stop=stop_), *w)

        def tr(out, in_, idn, *w):
            return Q.op("p", lambda e: e.transpose(out, in_, idn), *w)

        def act(out, in_, f, *w, scale=1.0, bias=0.0, accum=None):
            kw = {} if accum is None else {"accum_out": accum}
            if f == ACT.Copy:
                return Q.op("a", lambda e: e.activation(out, in_, f, scale=scale, **kw), *w)
            return Q.op("a", lambda e: e.activation(out, in_, f, bias=bias, scale=scale, **kw), *w)

        def tt(out, a, b, op, *w, eng="v"):
            return Q.op(eng, lambda e: e.tensor_tensor(out, a, b, op), *w)

        def ts(out, a, s1, s2, o0, o1, *w, eng="v"):
            if o1 is None:
                return Q.op(eng, lambda e: e.tensor_scalar(out, a, s1, None, o0), *w)
            return Q.op(eng, lambda e: e.tensor_scalar(out, a, s1, s2, o0, o1), *w)

        def stt(out, a, s, b, o0, o1, *w):
            return Q.op("v", lambda e: e.scalar_tensor_tensor(out=out, in0=a, scalar=s, in1=b, op0=o0, op1=o1), *w)

        def cp(out, a, *w, eng="v"):
            return Q.op(eng, lambda e: e.tensor_copy(out, a), *w)

        def rec(out, a, *w):
            return Q.op("v", lambda e: e.reciprocal(out, a), *w)

        def red(out, a, op, *w, negate=False):
            return Q.op("v", lambda e: e.tensor_reduce(out, a, AXX, op, negate=negate), *w)

        def memset(out, v, *w, eng="g"):
            return Q.op(eng, lambda e: e.memset(out, v), *w)

        def load(out, src, *w, eng="a"):
            return Q.op(eng, lambda e: e.dma_start(out, src), *w, dma=True)

        class Stream:
            i = 0
            loads = {}
            last = {}

            def fetch(self, p):
                if p < npanel:
                    self.loads[p] = Q.op("s", lambda e: e.dma_start(wslot[p % NSLOT], d_w[p, :, :]),
                                         self.last.get(p - NSLOT), dma=True)

            def take(self, name, n=1):
                while self.i % n or plan[self.i] is None:
                    assert plan[self.i] is None, (name, plan[self.i])
                    self.i += 1
                assert plan[self.i][0] == name, (name, plan[self.i])
                p, j = divmod(self.i, PANEL)
                assert j + n <= PANEL
                while max(self.loads) < p + NSLOT - 1 and max(self.loads) < npanel - 1:
                    self.fetch(max(self.loads) + 1)
                self.p = p
                self.i += n
                return wslot[p % NSLOT][:, j * 128:(j + n) * 128], self.loads[p]

            def used(self, op):
                self.last[self.p] = op

        W = Stream()
        for p in range(NSLOT):
            W.fetch(p)

        def linear(name, nmt, nkt, xs, chunks, evac, xw, m=128):
            for mt in range(nmt):
                bs = [bank_slots.take() for _ in chunks]
                for k in range(nkt):
                    t, tw = W.take(name)
                    for (lo, n), b in zip(chunks, bs):
                        o = mm(b.ap[0:m, 0:n], t[:, 0:m], xs[k][:, lo:lo + n], k == 0, k == nkt - 1,
                               tw, xw[k], b.free if k == 0 else None)
                    W.used(o)
                for (lo, n), b in zip(chunks, bs):
                    b.free = [evac(mt, lo, n, b.ap[0:m, 0:n], o)]

        LAT, BOTH = [(0, S)], [(0, S), (S, C)]

        l0 = [load(cst, d_const), load(par, d_par)]
        l0 += [load(X[f], d_x[f, :, :]) for f in range(8)] + [load(XC[f], d_ctx[f, :, :]) for f in range(8)]
        Q.barrier()
        for e in "pvag":
            Q.fence[e] = list(l0)
        for o in l0:
            o.marked = True
        arena0 = pos[0]

        def phase():
            Q.barrier()
            pos[0] = arena0

        cond1, cond2, ctmp = small(8), small(16), small(16)
        o = act(ctmp[:, 0:8], Pm["c1"], ACT.Tanh, scale=0.5)
        o = stt(ctmp[:, 0:8], ctmp[:, 0:8], 1.0, Pm["c1"], ALU.add, ALU.mult, o)
        oc1 = ts(cond1, ctmp[:, 0:8], 0.5, None, ALU.mult, None, o)
        o = act(ctmp, Pm["c2"], ACT.Tanh, oc1, scale=0.5)
        o = stt(ctmp, ctmp, 1.0, Pm["c2"], ALU.add, ALU.mult, o)
        oc2 = ts(cond2, ctmp, 0.5, None, ALU.mult, None, o)

        def modulation(name, cond, m, bias, MOD, w):
            row = alloc(6144)
            rows = []
            for q in range(12):
                b = bank_slots.take()
                for k in range(8):
                    t, tw = W.take(name, 4)
                    o = mm(b.ap[0:m, :], cond[:, k * m:(k + 1) * m], t, k == 0, k == 7, tw, w,
                           b.free if k == 0 else None)
                    W.used(o)
                o = act(row[0:m, q * 512:(q + 1) * 512], b.ap[0:m, :], ACT.Copy, o)
                b.free = [o]
                rows.append(o)
            b = bank_slots.take()
            for j in range(48):
                o = tr(b.ap[:, j * m:(j + 1) * m], row[0:m, j * 128:(j + 1) * 128], ident[0:m, 0:m], rows[j // 4],
                       b.free)
            o = tt(MOD.rearrange("p (j m) -> p j m", m=m), b.ap[:, 0:48 * m].rearrange("p (j m) -> p j m", m=m),
                   bias.unsqueeze(2).broadcast_to([128, 48, m]), ALU.add, o)
            b.free = [o]
            return o

        def part(MOD, s, m=1, which=0):
            v = MOD.rearrange("p (s f m) -> p s f m", f=8, m=m)
            return v[:, s, :, which]

        def scaled_gain(g, sc, w):
            gs = small(8)
            return gs, stt(gs, sc, 1.0, g, ALU.add, ALU.mult, w)

        def norm_stat(xs, n, count, tmp, out, w, lhs=None, key="ones", rows=128):
            b = bank_slots.take()
            for f, x in enumerate(xs):
                t = tmp.take()
                o = act(t.ap[0:rows, 0:n], x, ACT.Square, w[f], t.free)
                o = mm(b.ap[0:rows, 0:n], K[key][0:rows, 0:rows], t.ap[0:rows, 0:n], f == 0, f == len(xs) - 1, o,
                       b.free if f == 0 else None)
                t.free = [o]
            o = act(out, b.ap[0:rows, 0:n], ACT.Ln, o, scale=1.0 / count, bias=K["eps"][0:rows, :])
            b.free = [o]
            return act(out, out, ACT.Exp, o, scale=-0.5)

        def norm_mod(xs, n, H, lo, gs, sh, w, tmp, rst):
            ws = [w] * 8 if not isinstance(w, list) or len(w) != 8 else w
            o = norm_stat(xs, n, 1024.0, tmp, rst[:, 0:n], ws)
            out = []
            for f in range(8):
                h = H[f][:, lo:lo + n]
                q = stt(h, xs[f], gs[:, f:f + 1], rst[:, 0:n], ALU.mult, ALU.mult, o)
                out.append(ts(h, h, sh[:, f:f + 1], None, ALU.add, None, q, eng="g"))
            return out

        def residual(X, gate, w=None):
            def evac(mt, lo, n, ps, o):
                return stt(X[mt][:, 0:n], ps, gate[:, mt:mt + 1], X[mt][:, 0:n], ALU.mult, ALU.add, o, w)
            return evac

        def dump(aps):
            Q.barrier("a")
            for i, (a, r, n) in enumerate(aps):
                load(d_dbg[i, 0:r, 0:n], a)

        def ffn1(i, mod):
            phase()
            H, HID = tiles(8, S), tiles(32, S)
            tmp, rst = Ring(tiles(2, S)), alloc(S)
            gs, og = scaled_gain(Pm["gffn"][:, 8 * i:8 * i + 8], part(mod, 4), None)
            hw = norm_mod(X, S, H, 0, gs, part(mod, 3), og, tmp, rst)
            hid = [None] * 32

            def relu2(mt, lo, n, ps, o):
                o = act(HID[mt], ps, ACT.Relu, o)
                hid[mt] = tt(HID[mt], HID[mt], HID[mt], ALU.mult, o, eng="g")
                return o

            linear(f"f1_{i}", 32, 8, H, LAT, relu2, hw)
            linear(f"f2_{i}", 8, 32, HID, LAT, residual(X, part(mod, 5)), hid)

        def rglru(mod):
            phase()
            H = tiles(8, S)
            tmp, rst = Ring(tiles(2, S)), alloc(S)
            XB = tiles(10, S + 3)
            XCV, HS, A, M = tiles(10, S), tiles(10, S), tiles(10, S), tiles(10, S)
            gs, og = scaled_gain(Pm["gmix"][:, 0:8], part(mod, 1), None)
            hw = norm_mod(X, S, H, 0, gs, part(mod, 0), og, tmp, rst)
            pad = memset(SB[:, 0:1], 0.0) if False else None
            xbw, xcw = [None] * 10, [None] * 10
            c4, z, z2, s, m_ = small(10), small(10), small(10), small(10), small(10)
            hb = small(20)
            o1 = ts(hb[:, 0:10], Pm["rb"], 0.5, None, ALU.mult, None)
            o1 = ts(hb[:, 10:20], Pm["ib"], 0.5, None, ALU.mult, None, o1)
            osp = softplus(s, Pm["lam"], -1.0, z, z2, m_, o1)
            o4 = ts(c4, s, -4.0, None, ALU.mult, None, osp)
            n4 = small(10)
            o4 = ts(n4, s, 4.0, None, ALU.mult, None, o4)

            def conv(mt, lo, n, ps, o):
                xb = XB[mt]
                z0 = memset(xb[:, 0:3], 0.0)
                o = act(xb[:, 3:3 + S], ps, ACT.Copy, o)
                w = lambda j: Pm["convw"][:, j * 10 + mt:j * 10 + mt + 1]
                x = XCV[mt]
                q = ts(x, xb[:, 0:S], w(0), Pm["convb"][:, mt:mt + 1], ALU.mult, ALU.add, o, z0)
                for j in range(1, 4):
                    q = stt(x, xb[:, j:j + S], w(j), x, ALU.mult, ALU.add, q)
                xcw[mt] = q
                return o

            linear("a_in", 10, 8, H, LAT, conv, hw)
            ops = [None] * 10
            for n in range(5):
                for d in range(2):
                    f = 2 * n + d
                    got = []
                    for g, half in (("gr", hb[:, f:f + 1]), ("gi", hb[:, 10 + f:11 + f])):
                        b = bank_slots.take()
                        for k in range(2):
                            t, tw = W.take(g)
                            o = mm(b.ap, t, XCV[2 * n + k], k == 0, k == 1, tw, xcw[2 * n + k],
                                   b.free if k == 0 else None)
                            W.used(o)
                        dst = A[f] if g == "gr" else M[f]
                        o = act(dst, b.ap, ACT.Tanh, o, o1, scale=0.5, bias=half)
                        b.free = [o]
                        got.append(o)
                    o = stt(HS[f], M[f], 1.0, XCV[f], ALU.add, ALU.mult, got[1])
                    o2 = act(M[f], A[f], ACT.Tanh, got[0], o, o4, scale=n4[:, f:f + 1], bias=n4[:, f:f + 1])
                    o3 = act(A[f], A[f], ACT.Exp, o2, scale=c4[:, f:f + 1], bias=c4[:, f:f + 1])
                    ops[f] = [o, o2, o3]
            for f in range(10):
                o, o2, o3 = ops[f]
                t = tmp.take()
                q = tt(t.ap, A[f], A[f], ALU.mult, o3, t.free, eng="g")
                q = stt(M[f], t.ap, 1.0, M[f], ALU.add, ALU.mult, q, o2)
                t.free = [q]
                ops[f] = [o, o3, q]
            for f in range(10):
                o, o3, q = ops[f]
                q = act(M[f], M[f], ACT.Sqrt, q)
                q = stt(M[f], M[f], 0.5, HS[f], ALU.mult, ALU.mult, q, o)
                ops[f] = Q.op("v", (lambda f: lambda e: e.tensor_tensor_scan(HS[f], A[f], M[f], 0.0, ALU.mult,
                                                                             ALU.add))(f), q, o3)
            gt = Ring(XB)
            yw = [None] * 10

            def gelu(mt, lo, n, ps, o):
                t, u = A[mt], XCV[mt]
                q0 = act(u, ps, ACT.Copy, o, ops[mt])
                q = tt(t, u, u, ALU.mult, q0, ops[mt], eng="g")
                q = ts(t, t, 0.044715, 1.0, ALU.mult, ALU.add, q, eng="g")
                q = tt(t, t, u, ALU.mult, q, eng="g")
                q = act(t, t, ACT.Tanh, q, scale=0.7978845608028654)
                q = stt(t, t, 1.0, u, ALU.add, ALU.mult, q)
                yw[mt] = stt(HS[mt], t, 0.5, HS[mt], ALU.mult, ALU.mult, q)
                return q0

            linear("a_in", 10, 8, H, LAT, gelu, hw)
            linear("a_out", 8, 10, HS, LAT, residual(X, part(mod, 2)), yw)

        def softplus(out, x, sign, z, z2, mx, *w):
            o = ts(mx, x, sign, 0.0, ALU.mult, ALU.max, *w)
            o2 = ts(z, x, -1.0, None, ALU.mult, None, o)
            o2 = tt(z, z, x, ALU.min, o2)
            o = act(z, z, ACT.Exp, o2)
            o = ts(z2, z, 2.0, None, ALU.add, None, o)
            o = rec(z2, z2, o)
            o = tt(z, z, z2, ALU.mult, o)
            o = tt(z2, z, z, ALU.mult, o)
            n = 9
            o = ts(out, z2, 1.0 / (2 * n + 1), 1.0 / (2 * n - 1), ALU.mult, ALU.add, o)
            for k in range(n - 1, 0, -1):
                o = tt(out, out, z2, ALU.mult, o)
                o = ts(out, out, 1.0 / (2 * k - 1), None, ALU.add, None, o)
            o = tt(out, out, z, ALU.mult, o)
            return stt(out, out, 2.0, mx, ALU.mult, ALU.add, o)

        def rope(x, n, cos, sin, tmp, w, key="rot64", lo=0, hi=128, out=None):
            b = bank_slots.take()
            o = mm(b.ap[0:hi, 0:n], K[key][0:hi, 0:hi], x[0:hi, 0:n], True, True, w, b.free)
            t = tmp.take()
            q = tt(t.ap[lo:hi, 0:n], b.ap[lo:hi, 0:n], sin[lo:hi, 0:n], ALU.mult, o, t.free)
            b.free = [q]
            r = tt(x[lo:hi, 0:n], x[lo:hi, 0:n], cos[lo:hi, 0:n], ALU.mult, o, w, eng="g")
            r = tt(x[lo:hi, 0:n], x[lo:hi, 0:n], t.ap[lo:hi, 0:n], ALU.add, q, r, eng="g")
            t.free = [r]
            return r

        def attention(pairs, nqb, qT, kT, V, nkeys, mask, out, wq, tag):
            sring = Ring([PSB[:, 0:1024], PSB[:, 1024:2048]])
            tring = Ring([banks[4], banks[5]])
            oring = Ring([banks[6], banks[7]])
            held = [x.free for x in bank_slots.slots]
            for ring, at in ((sring, (0, 2)), (tring, (4, 5)), (oring, (6, 7))):
                for x, a in zip(ring.slots, at):
                    x.free = held[a:a + 2] if ring is sring else held[a]
            nk_max = max(nkeys(b) for b in range(nqb))
            sb = Ring(tiles(2, nk_max))
            pt = Ring(tiles(2, nk_max))
            st = Ring(tiles(4, 4))
            done = []
            for p in range(pairs):
                ob = oring.take()
                for hh in range(2):
                    h = 2 * p + hh
                    for b in range(nqb):
                        nk = nkeys(b)
                        s = sring.take()
                        o = None
                        for lo in range(0, nk, 512):
                            n = min(512, nk - lo)
                            o = mm(s.ap[:, lo:lo + n], qT(h, b), kT(h, lo, n), True, True, wq(h), s.free)
                        pb, stt_ = sb.take(), st.take()
                        mx, sm, rc = (stt_.ap[:, j:j + 1] for j in range(3))
                        parts = mask(h, b)
                        src = s.ap[:, 0:nk]
                        if parts:
                            lasts = []
                            for lo, n, m_, mw in parts:
                                shape = None
                                if m_ is None:
                                    lasts.append(act(pb.ap[:, lo:lo + n], s.ap[:, lo:lo + n], ACT.Copy, o, pb.free))
                                else:
                                    lasts.append(tt(pb.ap[:, lo:lo + n], s.ap[:, lo:lo + n], m_, ALU.add, o, pb.free,
                                                    mw))
                            s.free = lasts
                            src = pb.ap[:, 0:nk]
                            o = lasts
                        o = red(mx, src, ALU.max, o, stt_.free, pb.free, negate=True)
                        e_ = act(pb.ap[:, 0:nk], src, ACT.Exp, o, pb.free, bias=mx, accum=sm)
                        if not parts:
                            s.free = [e_]
                        o = rec(rc, sm, e_)
                        o = ts(pb.ap[:, 0:nk], pb.ap[:, 0:nk], rc, None, ALU.mult, None, o, e_, eng="g")
                        stt_.free = [o]
                        ptb = pt.take()
                        evs = []
                        for lo in range(0, nk, 512):
                            n = min(512, nk - lo)
                            t = tring.take()
                            for j in range(0, n, 128):
                                q = tr(t.ap[:, j:j + 128], pb.ap[:, lo + j:lo + j + 128], ident, o, t.free)
                            ev = act(ptb.ap[:, lo:lo + n], t.ap[:, 0:n], ACT.Copy, q, ptb.free)
                            t.free = [ev]
                            evs.append(ev)
                        pb.free = [q]
                        nt = nk // 128
                        for j in range(nt):
                            vap, vw = V(h, j)
                            q = mm(ob.ap[64 * hh:64 * hh + 64, b * 128:b * 128 + 128], vap,
                                   ptb.ap[:, j * 128:j * 128 + 128], j == 0, j == nt - 1, evs, vw, ob.free)
                        ptb.free = [q]
                o = act(out(p), ob.ap[:, 0:nqb * 128], ACT.Copy, q)
                ob.free = [o]
                done.append(o)
            for b in range(8):
                bank_slots.slots[b].free = []
            Q.barrier()
            return done

        def head_norm(x, n, gcol, scale, tmp, rst, w):
            r = rst.take()
            o = norm_stat([x], n, 64.0, tmp, r.ap[:, 0:n], [[w, r.free]], key="bd64")
            q = stt(x, x, gcol, r.ap[:, 0:n], ALU.mult, ALU.mult, o, w)
            r.free = [q]
            if scale != 1.0:
                q = ts(x, x, scale, None, ALU.mult, None, q, eng="g")
            return q

        def dsa(mod):
            phase()
            H = tiles(8, S)
            QT, QI, KK, KI = tiles(8, S), tiles(4, S), alloc(S), alloc(S)
            VW = tiles(4, 72)
            RP = tiles(2, S)
            AO = tiles(8, S)
            MK = [alloc(128 * (b + 1)) for b in range(4)]
            tmp, rst = Ring(tiles(2, S)), Ring(tiles(2, S))
            lr = load(RP[0], d_rope[:, 0:S]), load(RP[1], d_rope[:, S:2 * S])
            Q.barrier("a")
            gs, og = scaled_gain(Pm["gmix"][:, 8:16], part(mod, 1), None)
            hw = norm_mod(X, S, H, 0, gs, part(mod, 0), og, tmp, rst.slots[0].ap)
            rst.slots[0].free = [hw]
            dst = QT + [KK] + QI + [KI]
            rdy = [None] * 14

            def ev(mt, lo, n, ps, o):
                o = act(dst[mt], ps, ACT.Copy, o)
                w = o
                if mt < 8:
                    w = head_norm(dst[mt], S, Pm["qg"], 0.125, tmp, rst, o)
                elif mt == 8:
                    w = head_norm(dst[mt], S, Pm["kg"], 1.0, tmp, rst, o)
                rdy[mt] = rope(dst[mt], S, RP[0], RP[1], tmp, [w, lr])
                return o

            linear("b_in", 14, 8, H, LAT, ev, hw)
            bs = [bank_slots.take() for _ in range(4)]
            for k in range(8):
                t, tw = W.take("b_in")
                for b in range(4):
                    o = mm(bs[b].ap[:, 0:72], H[k][:, b * 128:(b + 1) * 128], t[:, 0:72], k == 0, k == 7, tw, hw[k],
                           bs[b].free if k == 0 else None)
                W.used(o)
            vw = []
            for b in range(4):
                o1 = act(VW[b], bs[b].ap[:, 0:72], ACT.Copy, o)
                bs[b].free = [o1]
                o1 = ts(VW[b][:, 64:72], VW[b][:, 64:72], 8.0 ** -0.5, None, ALU.mult, None, o1, eng="g")
                vw.append(o1)
            SC = tiles(2, S)
            m8 = alloc(8)
            lt = Ring(tiles(3, S))
            mk = []
            for b in range(4):
                nk = 128 * (b + 1)
                if b == 0:
                    mk.append(cp(MK[0], K["causal"]))
                    continue
                sc = SC[0][:, 0:nk]
                prev = None
                for h in range(8):
                    bk = bank_slots.take()
                    r = 64 * (h % 2)
                    o = mm(bk.ap[:, 0:nk], QI[h // 2][r:r + 64, b * 128:(b + 1) * 128], KI[r:r + 64, 0:nk], True, True,
                           rdy[9 + h // 2], rdy[13], bk.free)
                    l = lt.take()
                    o = act(l.ap[:, 0:nk], bk.ap[:, 0:nk], ACT.Relu, o, l.free, scale=0.125)
                    bk.free = [o]
                    wcol = VW[b][:, 64 + h:65 + h]
                    if h == 0:
                        prev = ts(sc, l.ap[:, 0:nk], wcol, None, ALU.mult, None, o, vw[b], mk[-1])
                    else:
                        prev = stt(sc, l.ap[:, 0:nk], wcol, sc, ALU.mult, ALU.add, o, prev)
                    l.free = [prev]
                o = tt(sc[:, nk - 128:nk], sc[:, nk - 128:nk], K["causal"], ALU.add, prev)
                cur, nxt = SC
                for r in range(16):
                    a, z = cur[:, 0:nk], nxt[:, 0:nk]
                    o = Q.op("v", (lambda a: lambda e: e.max(m8, a))(a), o)
                    o = Q.op("v", (lambda a, z: lambda e: e.match_replace(z, m8, a, GONE))(a, z), o)
                    cur, nxt = nxt, cur
                mk.append(ts(MK[b], cur[:, 0:nk], 0.5 * GONE, NEG, ALU.is_gt, ALU.mult, o))

            done = attention(8, 4,
                      lambda h, b: QT[h // 2][64 * (h % 2):64 * (h % 2) + 64, b * 128:(b + 1) * 128],
                      lambda h, lo, n: KK[64 * (h % 2):64 * (h % 2) + 64, lo:lo + n],
                      lambda h, j: (VW[j][:, 0:64], vw[j]),
                      lambda b: 128 * (b + 1),
                      lambda h, b: [(0, 128 * (b + 1), MK[b], mk[b])],
                      lambda p: AO[p], lambda h: [rdy[h // 2], rdy[8]], "dsa")
            linear("b_out", 8, 8, AO, LAT, residual(X, part(mod, 2)), done)

        def mods2(i):
            return [(part(MOD2, s, 2, 0), part(MOD2, s, 2, 1)) for s in range(6)]

        def pre2(i, m, gname, s_sh, s_sc, H, tmp, rst, both):
            gl, o1 = scaled_gain(Pm[gname][:, 8 * i:8 * i + 8], m[s_sc][0], None)
            hw = norm_mod(X, S, H, 0, gl, m[s_sh][0], o1, tmp, rst)
            hw = [[w] for w in hw]
            if both:
                gc, o2 = scaled_gain(Pm[gname][:, 8 * i:8 * i + 8], m[s_sc][1], None)
                hc = norm_mod(XC, C, H, S, gc, m[s_sh][1], [o2, hw], tmp, rst)
                hw = [a + [b] for a, b in zip(hw, hc)]
            return hw

        def post2(i, m, gname, s_gt, Y, yw, tmp, rst, both):
            for which, (lo, n, xs) in enumerate([(0, S, X), (S, C, XC)][:2 if both else 1]):
                gg = small(8)
                og = tt(gg, m[s_gt][which], Pm[gname][:, 8 * i:8 * i + 8], ALU.mult)
                o = norm_stat([y[:, lo:lo + n] for y in Y], n, 1024.0, tmp, rst[:, 0:n],
                              [[w, og] for w in yw])
                for f in range(8):
                    y = Y[f][:, lo:lo + n]
                    q = stt(y, y, gg[:, f:f + 1], rst[:, 0:n], ALU.mult, ALU.mult, o, og)
                    last = tt(xs[f], xs[f], y, ALU.add, q, eng="g")
                Q.barrier()

        def ffn2(i, m, both):
            phase()
            chunks = BOTH if both else LAT
            wdt = ST if both else S
            H, Y, HID = tiles(8, wdt), tiles(8, wdt), tiles(22, wdt)
            tmp, rst = Ring(tiles(2, S)), alloc(S)
            hw = pre2(i, m, "gpf", 3, 4, H, tmp, rst, both)
            hid = [[] for _ in range(22)]
            gr = Ring([y[:, 0:S] for y in Y[0:4]])
            for mt in range(22):
                bs = {}
                for name in ("g", "u"):
                    bs[name] = [bank_slots.take() for _ in chunks]
                    for k in range(8):
                        t, tw = W.take(f"{name}_{i}")
                        for (lo, n), b in zip(chunks, bs[name]):
                            o = mm(b.ap[:, 0:n], t, H[k][:, lo:lo + n], k == 0, k == 7, tw, hw[k],
                                   b.free if k == 0 else None)
                        W.used(o)
                for (lo, n), bg, bu in zip(chunks, bs["g"], bs["u"]):
                    t = gr.take()
                    q = act(t.ap[:, 0:n], bg.ap[:, 0:n], ACT.Tanh, o, t.free, scale=0.5)
                    q = stt(t.ap[:, 0:n], t.ap[:, 0:n], 1.0, bg.ap[:, 0:n], ALU.add, ALU.mult, q)
                    bg.free = [q]
                    q = stt(HID[mt][:, lo:lo + n], t.ap[:, 0:n], 0.5, bu.ap[:, 0:n], ALU.mult, ALU.mult, q)
                    bu.free = t.free = [q]
                    hid[mt].append(q)
            yw = [[] for _ in range(8)]

            def ev(mt, lo, n, ps, o):
                o = act(Y[mt][:, lo:lo + n], ps, ACT.Copy, o)
                yw[mt].append(o)
                return o

            linear(f"d_{i}", 8, 22, HID, chunks, ev, hid)
            post2(i, m, "gqf", 5, Y, yw, tmp, rst, both)

        def silu_half(out, x, t, *w):
            o = act(t, x, ACT.Tanh, *w)
            return stt(out, t, 1.0, x, ALU.add, ALU.mult, o)

        def even(m):
            phase()
            QKV, GT = tiles(12, ST), tiles(4, ST)
            MIXb = alloc(8 * ST)
            H = [MIXb[:, f * ST:(f + 1) * ST] for f in range(8)]
            RAW = tiles(4, ST)
            AB = alloc(6 * 32)
            mark = pos[0]
            tmp, rst = Ring(tiles(2, S)), alloc(S)
            hw = pre2(0, m, "gpm", 0, 1, H, tmp, rst, True)
            pads = Ring(tiles(2, 776))
            cw = small(60)
            ocw = ts(cw, Pm["gconv"], 0.5, None, ALU.mult, None)
            z = []
            for sl in pads.slots:
                for lo in (0, 514, 516, 774):
                    z.append(memset(sl.ap[:, lo:lo + 2], 0.0))
            qw = [None] * 12
            rw = [[] for _ in range(4)]
            gw = [[] for _ in range(4)]
            l2 = Ring([rst, tmp.slots[1].ap])
            tmp1 = Ring([tmp.slots[0].ap])
            cur = {}

            def ev(mt, lo, n, ps, o):
                if mt >= 16:
                    o = act(RAW[mt - 16][:, lo:lo + n], ps, ACT.Copy, o)
                    rw[mt - 16].append(o)
                    return o
                if mt >= 12:
                    g = GT[mt - 12][:, lo:lo + n]
                    q = act(g, ps, ACT.Tanh, o, scale=0.5)
                    q = stt(g, g, 1.0, ps, ALU.add, ALU.mult, q)
                    gw[mt - 12].append(q)
                    return q
                if lo == 0:
                    cur["p"] = pads.take()
                    cur["q"] = []
                pd = cur["p"]
                off = 2 if lo == 0 else 518
                o = act(pd.ap[:, off:off + n], ps, ACT.Copy, o, pd.free, z)
                x = QKV[mt][:, lo:lo + n]
                w = lambda j: cw[:, j * 12 + mt:j * 12 + mt + 1]
                q = ts(x, pd.ap[:, off - 2:off - 2 + n], w(0), None, ALU.mult, None, o, ocw)
                for j in range(1, 5):
                    q = stt(x, pd.ap[:, off - 2 + j:off - 2 + j + n], w(j), x, ALU.mult, ALU.add, q)
                q = silu_half(x, x, pd.ap[:, off:off + n], q)
                cur["q"].append(q)
                if lo:
                    pd.free = list(cur["q"])
                    qw[mt] = list(cur["q"])
                return o

            linear("e_in", 20, 8, H, BOTH, ev, hw)
            bs = bank_slots.take()
            for blk in range(6):
                pass
            b6 = [bs] + [bank_slots.take() for _ in range(5)]
            for k in range(8):
                t, tw = W.take("e_in")
                for blk in range(6):
                    o = mm(b6[blk].ap[:, 0:32], H[k][:, blk * 128:(blk + 1) * 128], t[:, 0:32], k == 0, k == 7, tw, hw[k],
                           b6[blk].free if k == 0 else None)
                W.used(o)
            for blk in range(6):
                q = act(AB[:, blk * 32:(blk + 1) * 32], b6[blk].ap[:, 0:32], ACT.Copy, o)
                b6[blk].free = [q]
            Q.barrier()
            for f in range(8):
                for lo, n in BOTH:
                    x = QKV[f][:, lo:lo + n]
                    t = l2.take()
                    o = norm_stat([x], n, 1.0, tmp1, t.ap[:, 0:n], [[qw[f], t.free]], key="bd64")
                    o = tt(x, x, t.ap[:, 0:n], ALU.mult, o)
                    t.free = [o]
                    if f < 4:
                        ts(x, x, 0.125, None, ALU.mult, None, o, eng="g")
            Q.barrier()
            pos[0] = mark
            mla(RAW, MIXb)
            Q.barrier()
            pos[0] = mark - 6 * 32 - 4 * ST
            ab = alloc(192)
            gdn(QKV, GT, MIXb[:, 0:4 * ST], AB, ab)
            phase_keep = MIXb
            MIX = [QKV[f] for f in range(4)] + [MIXb[:, (4 + f) * ST:(5 + f) * ST] for f in range(4)]
            Q.barrier()
            pos[0] = mark - 6 * 32 - 4 * ST
            Y = tiles(8, ST)
            yw = [[] for _ in range(8)]
            tmp, rst = Ring(tiles(2, S)), alloc(S)

            def evy(mt, lo, n, ps, o):
                o = act(Y[mt][:, lo:lo + n], ps, ACT.Copy, o)
                yw[mt].append(o)
                return o

            linear("e_out", 8, 8, MIX, BOTH, evy, [None] * 8)
            post2(0, m, "gqm", 2, Y, yw, tmp, rst, True)

        def mla(RAW, MIXb):
            QD, KVD, KPE = RAW[0:2], RAW[2], RAW[3]
            OUT = [MIXb[:, (4 + f) * ST:(5 + f) * ST] for f in range(4)]
            VT = [MIXb[:, b * 512:(b + 1) * 512] for b in range(6)]
            save = pos[0]
            tmp, rst = Ring(tiles(1, S)), alloc(S)
            for lo, n in BOTH:
                o = norm_stat([q[:, lo:lo + n] for q in QD], n, 256.0, tmp, rst[:, 0:n], [None, None])
                for j in range(2):
                    x = QD[j][:, lo:lo + n]
                    q = stt(x, x, Pm["mqn"][:, j:j + 1], rst[:, 0:n], ALU.mult, ALU.mult, o)
                    ts(x, x, 96.0 ** -0.5, None, ALU.mult, None, q, eng="g")
                Q.barrier()
                o = norm_stat([KVD[:, lo:lo + n]], n, 128.0, tmp, rst[:, 0:n], [None])
                stt(KVD[:, lo:lo + n], KVD[:, lo:lo + n], Pm["mkn"], rst[:, 0:n], ALU.mult, ALU.mult, o)
                Q.barrier()
            rope(KPE, S, K["cosM"], K["sinM"], tmp, None, key="rot32", lo=64, hi=96)
            Q.barrier()
            t, tw = W.take("kvv", 4)
            for b in range(6):
                bk = bank_slots.take()
                o = mm(bk.ap, KVD[:, b * 128:(b + 1) * 128], t, True, True, tw, bk.free)
                bk.free = [act(VT[b], bk.ap, ACT.Copy, o)]
            W.used(o)
            pos[0] = save
            QH, KH = tiles(1, ST)[0], tiles(1, ST)[0]
            cp(KH[64:96, :], KPE[64:96, :], eng="g")
            Q.barrier()
            save = pos[0]
            QH2, KH2 = alloc(ST), alloc(ST)
            cp(KH2[64:96, :], KPE[64:96, :], eng="g")
            rt = Ring(tiles(1, S))
            Q.barrier()
            base = pos[0]
            for p in range(4):
                for hh, (qh, kh) in enumerate(((QH, KH), (QH2, KH2))):
                    h = 2 * p + hh
                    bsq = [bank_slots.take() for _ in BOTH]
                    for k in range(2):
                        t, tw = W.take("qup")
                        for (lo, n), b in zip(BOTH, bsq):
                            o = mm(b.ap[0:96, 0:n], t[:, 0:96], QD[k][:, lo:lo + n], k == 0, k == 1, tw,
                                   b.free if k == 0 else None)
                        W.used(o)
                    for (lo, n), b in zip(BOTH, bsq):
                        oq = act(qh[0:96, lo:lo + n], b.ap[0:96, 0:n], ACT.Copy, o)
                        b.free = [oq]
                    rope(qh, S, K["cosM"], K["sinM"], rt, oq, key="rot32", lo=64, hi=96)
                    bsk = [bank_slots.take() for _ in BOTH]
                    t, tw = W.take("kvk")
                    for (lo, n), b in zip(BOTH, bsk):
                        o = mm(b.ap[0:64, 0:n], t[:, 0:64], KVD[:, lo:lo + n], True, True, tw, b.free)
                    W.used(o)
                    for (lo, n), b in zip(BOTH, bsk):
                        b.free = [act(kh[0:64, lo:lo + n], b.ap[0:64, 0:n], ACT.Copy, o)]
                Q.barrier()
                qk = ((QH, KH), (QH2, KH2))
                for lo, nqb, klo, nk in ((0, 4, 0, ST), (S, 2, S, C)):
                    pos[0] = base
                    attention(1, nqb,
                              lambda h, b: qk[h][0][0:96, lo + b * 128:lo + (b + 1) * 128],
                              lambda h, l, n: qk[h][1][0:96, klo + l:klo + l + n],
                              lambda h, j: (VT[klo // 128 + j][:, (2 * p + h) * 64:(2 * p + h) * 64 + 64], None),
                              lambda b: nk, lambda h, b: None,
                              lambda _: OUT[p][:, lo:lo + nqb * 128], lambda h: None, "mla")

        def gdn(QKV, GT, Ob, AB0, AB):
            QT, KT, VT_ = QKV[0:4], QKV[4:8], QKV[8:12]
            O = [Ob[:, b * 512:(b + 1) * 512] for b in range(6)]
            o = cp(AB, AB0)
            Q.barrier()
            G, B = alloc(96), alloc(96)
            z, z2, mx, spx = alloc(96), alloc(96), alloc(96), alloc(96)
            ea = alloc(16)
            v3 = lambda a: a.rearrange("p (b c) -> p b c", b=6)
            o = tt(v3(spx), v3(AB)[:, :, 0:16], Pm["dtb"].unsqueeze(1).broadcast_to([128, 6, 16]), ALU.add)
            o = softplus(G, spx, 1.0, z, z2, mx, o)
            o2 = act(ea, Pm["alog"], ACT.Exp)
            o = stt(v3(G), v3(G), -1.0, ea.unsqueeze(1).broadcast_to([128, 6, 16]), ALU.mult, ALU.mult, o, o2)
            o = act(v3(B), v3(AB)[:, :, 16:32], ACT.Tanh, scale=0.5)
            o = ts(B, B, 0.5, 0.5, ALU.mult, ALU.add, o)
            Q.barrier()
            NG, EG, FT, GL, GLP = alloc(96), alloc(96), alloc(96), alloc(96), alloc(48)
            bg, bt = bank_slots.take(), bank_slots.take()
            for c in range(6):
                for d, tri in enumerate(("triF", "triB")):
                    j = c * 16 + d * 8
                    mm(bg.ap[:, j:j + 8], K[tri], G[:, j:j + 8], True, True, bg.free)
                    o = mm(bt.ap[:, j:j + 8], ones, G[:, j:j + 8], True, True, bt.free)
            o1 = act(NG, bg.ap[:, 0:96], ACT.Copy, o, scale=-1.0)
            o2 = act(EG, bg.ap[:, 0:96], ACT.Exp, o)
            o3 = act(GL, bt.ap[:, 0:96], ACT.Exp, o)
            q = tt(FT, bt.ap[:, 0:96], NG, ALU.add, o1, o3)
            bg.free, bt.free = [o2], [o3, q]
            act(FT, FT, ACT.Exp, q)
            gl2 = GL.rearrange("p (x two) -> p x two", two=2)
            cp(GLP[0:64, :], gl2[0:64, :, 0], o3)
            cp(GLP[64:128, :], gl2[64:128, :, 1], o3)
            ST_ = tiles(2, 256)
            for d in range(2):
                memset(ST_[d], 0.0)
            Q.barrier()
            for b in range(6):
                memset(O[b], 0.0)
            KTOK, VTOK, U, WT, KD = ({0: t, 1: t} for t in tiles(5, 512))
            AT = {0: alloc(1024)}
            AT[1] = AT[0]
            D, DT, MT, Y = tiles(2, 512), tiles(2, 512), tiles(2, 512), tiles(2, 512)
            h3 = lambda a: a.rearrange("p (h d) -> p h d", d=64)
            g3 = lambda a: a.rearrange("p (h d) -> p h d", d=128)
            tok = (4, 5, 0, 1, 2, 3), (5, 4, 3, 2, 1, 0)
            for step, d in [(i, j) for i in range(6) for j in range(2)]:
                Q.barrier()
                cols = {}
                for d in [d]:
                    c = tok[d][step]
                    j0 = c * 16 + d * 8
                    cl = slice(c * 128, (c + 1) * 128)
                    cols[d] = (c, j0, cl)
                    for src, dst in ((KT, KTOK[d]), (VT_, VTOK[d])):
                        b = bank_slots.take()
                        for f in range(4):
                            o = tr(b.ap[:, f * 128:(f + 1) * 128], src[f][:, cl], ident, b.free)
                        b.free = [act(dst, b.ap, ACT.Copy, o)]
                Q.barrier()
                bc = lambda a, n: a.unsqueeze(2).broadcast_to([128, a.shape[1], n])
                for d in [d]:
                    c, j0, cl = cols[d]
                    tt(h3(KD[d]), h3(KTOK[d]), bc(FT[:, j0:j0 + 8], 64), ALU.mult)
                    o = tt(h3(VTOK[d]), h3(VTOK[d]), bc(B[:, j0:j0 + 8], 64), ALU.mult, eng="g")
                    o = tt(h3(KTOK[d]), h3(KTOK[d]), bc(B[:, j0:j0 + 8], 64), ALU.mult, Q.q["v"][-1], eng="g")
                    o = tt(h3(KTOK[d]), h3(KTOK[d]), bc(EG[:, j0:j0 + 8], 64), ALU.mult, o, eng="g")
                grp = [(d, hg) for hg in range(2)]
                mt_op = {}
                for gi, (d, hg) in enumerate(grp):
                    c, j0, cl = cols[d]
                    tri, neg = (("triF", "negF"), ("triB", "negB"))[d]
                    b = bank_slots.take()
                    for x in range(4):
                        j = j0 + 2 * x + hg
                        o = mm(b.ap[:, x * 128:(x + 1) * 128], G[:, j:j + 1].broadcast_to([128, 128]), K[tri], True, True,
                               b.free)
                    o = tt(g3(Y[gi]), g3(b.ap), K[neg].unsqueeze(1).broadcast_to([128, 4, 128]), ALU.add, o)
                    b.free = [o]
                    for x in range(4):
                        j = j0 + 2 * x + hg
                        od = act(Y[gi][:, x * 128:(x + 1) * 128], Y[gi][:, x * 128:(x + 1) * 128], ACT.Exp, o,
                                 bias=NG[:, j:j + 1])
                    bk, bq, bb = bank_slots.take(), bank_slots.take(), bank_slots.take()
                    for x in range(4):
                        h = 2 * x + hg
                        r = slice(64 * (h % 2), 64 * (h % 2) + 64)
                        sl = slice(x * 128, (x + 1) * 128)
                        mm(bk.ap[:, sl], KT[h // 2][r, cl], KT[h // 2][r, cl], True, True, bk.free)
                        mm(bq.ap[:, sl], KT[h // 2][r, cl], QT[h // 2][r, cl], True, True, bq.free)
                        o = mm(bb.ap[:, sl], B[:, j0 + h:j0 + h + 1].broadcast_to([128, 128]), ident, True, True, bb.free)
                    a1 = tt(AT[d].rearrange("p (x two c) -> p x two c", two=2, c=128)[:, :, hg, :], g3(bq.ap), g3(Y[gi]), ALU.mult, o,
                            od)
                    a2 = tt(MT[gi], bk.ap, Y[gi], ALU.mult, o, od)
                    a3 = tt(MT[gi], bb.ap, MT[gi], ALU.mult, a2)
                    bq.free, bk.free, bb.free = [a1], [a2], [a3]
                    mt_op[gi] = a3
                idb = ident.unsqueeze(1).broadcast_to([128, 4, 128])
                d_op, dt_op, y_free = {}, {}, {}
                for gi in range(2):
                    d_op[gi] = cp(g3(D[gi]), idb, eng="g")
                    dt_op[gi] = cp(g3(DT[gi]), idb, eng="g")
                    y_free[gi] = mt_op[gi]
                for lv in range(7):
                    for gi, (d, hg) in enumerate(grp):
                        mask = K[("lvF", "lvB")[d]][:, lv * 128:(lv + 1) * 128].unsqueeze(1).broadcast_to([128, 4, 128])
                        b = bank_slots.take()
                        for x in range(4):
                            sl = slice(x * 128, (x + 1) * 128)
                            o = mm(b.ap[:, sl], MT[gi][:, sl], D[gi][:, sl], True, True, mt_op[gi], d_op[gi], b.free)
                        oy = tt(g3(Y[gi]), g3(b.ap), mask, ALU.mult, o, y_free[gi])
                        b.free = [oy]
                        if lv < 6:
                            b = bank_slots.take()
                            for x in range(4):
                                sl = slice(x * 128, (x + 1) * 128)
                                oz = mm(b.ap[:, sl], DT[gi][:, sl], Y[gi][:, sl], True, True, oy, dt_op[gi], b.free)
                            bz = b
                        b = bank_slots.take()
                        for x in range(4):
                            sl = slice(x * 128, (x + 1) * 128)
                            o = mm(b.ap[:, sl], Y[gi][:, sl], DT[gi][:, sl], True, True, oy, dt_op[gi], b.free)
                        y_free[gi] = o
                        if lv < 6:
                            d_op[gi] = tt(D[gi], D[gi], bz.ap, ALU.subtract, oz, o)
                            bz.free = [d_op[gi]]
                        dt_op[gi] = tt(DT[gi], DT[gi], b.ap, ALU.subtract, o)
                        b.free = [dt_op[gi]]
                Q.barrier()
                for d in [d]:
                    b = bank_slots.take()
                    for h in range(8):
                        gi, x = h % 2, h // 2
                        o = mm(b.ap[:, h * 64:(h + 1) * 64], DT[gi][:, x * 128:(x + 1) * 128],
                               VTOK[d][:, h * 64:(h + 1) * 64], True, True, b.free)
                    b.free = [act(U[d], b.ap, ACT.Copy, o)]
                    b = bank_slots.take()
                    for h in range(8):
                        gi, x = h % 2, h // 2
                        r = slice(64 * (h % 2), 64 * (h % 2) + 64)
                        o = mm(b.ap[r, (h // 2) * 128:(h // 2 + 1) * 128], KTOK[d][:, h * 64:(h + 1) * 64],
                               DT[gi][:, x * 128:(x + 1) * 128], True, True, b.free)
                    b.free = [act(WT[d], b.ap, ACT.Copy, o)]
                Q.barrier()
                vnew, tq = {d: Y[0]}, {d: Y[1]}
                for d in [d]:
                    c, j0, cl = cols[d]
                    two = lambda a, y: a.rearrange("p (x two c) -> p x two c", two=2, c=64)[:, :, y, :]
                    q4 = lambda a: a.rearrange("p (x c) -> p x c", c=64)
                    ov, oq = [], []
                    for y in range(2):
                        b = bank_slots.take()
                        r = slice(64 * y, 64 * y + 64)
                        for x in range(4):
                            s_ = ST_[d][r, x * 64:x * 64 + 64]
                            mm(b.ap[:, x * 64:(x + 1) * 64], WT[d][r, x * 128:(x + 1) * 128], s_, True, True, b.free)
                            o = mm(b.ap[:, 256 + x * 64:256 + (x + 1) * 64], QT[x][r, cl], s_, True, True, b.free)
                        ov.append(tt(two(vnew[d], y), two(U[d], y), q4(b.ap[:, 0:256]), ALU.subtract, o))
                        eg = EG[:, j0:j0 + 8].rearrange("p (x two) -> p x two", two=2)[:, :, y]
                        oq.append(tt(two(tq[d], y), q4(b.ap[:, 256:512]), eg.unsqueeze(2).broadcast_to([128, 4, 64]),
                                     ALU.mult, o))
                        b.free = [ov[-1], oq[-1]]
                    bo = bank_slots.take()
                    for h in range(8):
                        o = mm(bo.ap[:, h * 64:(h + 1) * 64], AT[d][:, h * 128:(h + 1) * 128],
                               vnew[d][:, h * 64:(h + 1) * 64], True, True, ov, bo.free)
                    oq = tt(tq[d], tq[d], bo.ap, ALU.add, oq, o)
                    bo.free = [oq]
                    tt(O[c], O[c], tq[d], ALU.add, oq, eng="g")
                    if step < 5:
                        b = bank_slots.take()
                        for h in range(8):
                            r = slice(64 * (h % 2), 64 * (h % 2) + 64)
                            o = mm(b.ap[r, (h // 2) * 64:(h // 2) * 64 + 64], KD[d][:, h * 64:(h + 1) * 64],
                                   vnew[d][:, h * 64:(h + 1) * 64], True, True, ov, b.free)
                        s3 = ST_[d].rearrange("p (h d) -> p h d", d=64)
                        q = tt(s3, s3, bc(GLP[:, j0 // 2:j0 // 2 + 4], 64), ALU.mult, o)
                        q = tt(ST_[d], ST_[d], b.ap[:, 0:256], ALU.add, q)
                        b.free = [q]
            Q.barrier()
            hg_ = small(1)
            oh = ts(hg_, Pm["onorm"], 0.5, None, ALU.mult, None)
            sq = Ring([U[0], KTOK[0]])
            rr = Ring([WT[0][:, 0:8], WT[0][:, 8:16]])
            for b in range(6):
                t, r = sq.take(), rr.take()
                o = act(t.ap, O[b], ACT.Square, t.free)
                o = red(r.ap, h3(t.ap), ALU.add, o, r.free)
                t.free = [o]
                o = act(r.ap, r.ap, ACT.Ln, o, scale=1.0 / 64, bias=K["eps"])
                o = act(r.ap, r.ap, ACT.Exp, o, scale=-0.5)
                o = tt(h3(O[b]), h3(O[b]), bc(r.ap, 64), ALU.mult, o)
                r.free = [o]
                bk = bank_slots.take()
                for f in range(4):
                    q = tr(bk.ap[:, f * 128:(f + 1) * 128], O[b][:, f * 128:(f + 1) * 128], ident, o, bk.free)
                for f in range(4):
                    sl = slice(b * 128, (b + 1) * 128)
                    q2 = stt(QKV[f][:, sl], bk.ap[:, f * 128:(f + 1) * 128], hg_, GT[f][:, sl], ALU.mult, ALU.mult, q, oh)
                bk.free = [q2]

        def odd(m):
            phase()
            H = tiles(8, ST)
            NQ, NK_, NV = tiles(4, S), tiles(4, ST), tiles(6, 512)
            GQ, GK, GV = tiles(4, S), tiles(2, ST), tiles(6, 128)
            RP = tiles(2, S)
            lr = load(RP[0], d_rope[:, 2 * S:3 * S]), load(RP[1], d_rope[:, 3 * S:4 * S])
            Q.barrier("a")
            tmp, rst = Ring(tiles(1, S)), Ring(tiles(2, S))
            mark = pos[0]
            hw = pre2(1, m, "gpm", 0, 1, H, tmp, rst.slots[0].ap, True)
            rst.slots[0].free = [hw]

            def ev(mt, lo, n, ps, o):
                if mt < 4:
                    return act(NQ[mt], ps, ACT.Copy, o, scale=0.125)
                if mt < 8:
                    return act(NK_[mt - 4][:, lo:lo + n], ps, ACT.Copy, o)
                x = GQ[mt - 8] if mt < 12 else GK[mt - 12][:, lo:lo + n]
                o = act(x, ps, ACT.Copy, o)
                w = head_norm(x, n, Pm["gqn" if mt < 12 else "gkn"], 0.125 if mt < 12 else 1.0, tmp, rst, o)
                if lo == 0:
                    rope(x, S, RP[0], RP[1], tmp, [w, lr])
                return o

            linear("o_in", 4, 8, H, LAT, ev, hw)
            linear("o_in", 4, 8, H, BOTH, lambda mt, *a: ev(mt + 4, *a), hw)
            linear("o_in", 4, 8, H, LAT, lambda mt, *a: ev(mt + 8, *a), hw)
            linear("o_in", 2, 8, H, BOTH, lambda mt, *a: ev(mt + 12, *a), hw)
            for name, n, dst in (("nav", 4, NV), ("gv", 1, GV)):
                b6 = [bank_slots.take() for _ in range(6)]
                for k in range(8):
                    t, tw = W.take(name, n)
                    for b in range(6):
                        o = mm(b6[b].ap[:, 0:n * 128], H[k][:, b * 128:(b + 1) * 128], t, k == 0, k == 7, tw, hw[k],
                               b6[b].free if k == 0 else None)
                    W.used(o)
                for b in range(6):
                    b6[b].free = [act(dst[b], b6[b].ap[:, 0:n * 128], ACT.Copy, o)]
            Q.barrier()
            OUT = tiles(8, 512) if False else [H[f][:, 0:S] for f in range(8)]
            pos[0] = mark
            TB = Ring(tiles(2, 896))
            base = pos[0]
            for p in range(4):
                pos[0] = base
                tb, tw = [], []
                for hh in range(2):
                    t = TB.slots[hh].ap
                    Q.barrier("a")
                    l = load(t, d_rpb[2 * p + hh, :, :])
                    t3 = t.rearrange("p (e k) -> p e k", k=64)
                    tw.append(tt(t3, t3, K["namask"].unsqueeze(1).broadcast_to([128, 14, 64]), ALU.add, l, eng="g"))
                    tb.append(t)
                attention(1, 4,
                          lambda h, b: NQ[p][64 * h:64 * h + 64, b * 128:(b + 1) * 128],
                          lambda h, l, n: NK_[p][64 * h:64 * h + 64, l:l + n],
                          lambda h, j: (NV[j][:, (2 * p + h) * 64:(2 * p + h) * 64 + 64], None),
                          lambda b: ST,
                          lambda h, b: [(0, 512, tb[h][:, (6 - 2 * b) * 64:(14 - 2 * b) * 64], tw[h]), (512, 256, None, None)],
                          lambda _: OUT[p], lambda h: None, "na")
            pos[0] = mark
            attention(4, 4,
                      lambda h, b: GQ[h // 2][64 * (h % 2):64 * (h % 2) + 64, b * 128:(b + 1) * 128],
                      lambda h, l, n: GK[h // 4][64 * (h % 2):64 * (h % 2) + 64, l:l + n],
                      lambda h, j: (GV[j][:, (h // 4) * 64:(h // 4) * 64 + 64], None),
                      lambda b: ST, lambda h, b: None,
                      lambda p: OUT[4 + p], lambda h: None, "gqa")
            pos[0] = mark
            Y = [a for a in NK_] + [alloc(S)[:, 0:S] for _ in range(4)]
            Y = [y[:, 0:S] for y in Y]
            yw = [None] * 8
            tmp, rst = Ring(tmp.slots[0:1] and [tmp.slots[0].ap]), rst.slots[0].ap

            def evy(mt, lo, n, ps, o):
                yw[mt] = act(Y[mt], ps, ACT.Copy, o)
                return yw[mt]

            linear("o_out", 8, 8, OUT, LAT, evy, [None] * 8)
            post2(1, m, "gqm", 2, Y, yw, tmp, rst, False)

        def body():
            def xdump():
                dump([(X[f], 128, S) for f in range(8)] + [(XC[f], 128, C) for f in range(8)])

            modulation("ada0", cond1, 1, Pm["ada_b"][:, 0:48], MOD1[:, 0:48], oc1)
            rglru(MOD1[:, 0:48])
            if stop == 1:
                return xdump()
            ffn1(0, MOD1[:, 0:48])
            if stop == 2:
                return xdump()
            phase()
            modulation("ada1", cond1, 1, Pm["ada_b"][:, 48:96], MOD1[:, 48:96], oc1)
            dsa(MOD1[:, 48:96])
            if stop == 3:
                return xdump()
            ffn1(1, MOD1[:, 48:96])
            if stop == 4:
                return xdump()
            for i in range(2):
                phase()
                modulation(f"mod{i}", cond2, 2, Pm["mod_b"][:, 48 * i:48 * i + 48], MOD2[:, 96 * i:96 * i + 96], oc2)
                m = [(part(MOD2[:, 96 * i:96 * i + 96], s, 2, 0), part(MOD2[:, 96 * i:96 * i + 96], s, 2, 1))
                     for s in range(6)]
                if i == 0:
                    even(m)
                else:
                    odd(m)
                if stop == 5 + 2 * i:
                    return xdump()
                ffn2(i, m, i == 0)
                if stop == 6 + 2 * i:
                    return xdump()
            Q.barrier("a")
            for f in range(8):
                load(d_out[f, :, :], X[f])

        body()

        sems = {e: es.enter_context(nc.semaphore(f"s_{n}")) for e, n in
                zip("pvagsd", ("tensor", "vector", "scalar", "gpsimd", "sync", "none"))}
        dsems = {e: [es.enter_context(nc.semaphore(f"d_{e}{i}")) for i in range(Q.NDMA)] for e in "as"}
        Q.number(sems, dsems)
        block = es.enter_context(nc.Block())

        @block.sync
        def _(e):
            Q.emit("s", e)

        @block.scalar
        def _(e):
            Q.emit("a", e)

        @block.tensor
        def _(e):
            Q.emit("p", e)

        @block.vector
        def _(e):
            Q.emit("v", e)

        @block.gpsimd
        def _(e):
            Q.emit("g", e)


def pack_weights(a):
    def pad(w, m):
        return np.pad(w, ((0, 0), (0, m - w.shape[1])))

    b, e, o = a["b_w_in"][0], a["w_in_even_2"][0], a["w_in_odd_2"][0]
    up, kv = a["mla_w_q_up_2"][0], a["mla_w_kv_up_2"][0].reshape(128, 8, 128)
    mats = {
        "ada0": a["ada_w"][0], "ada1": a["ada_w"][1], "mod0": a["w_mod_2"][0], "mod1": a["w_mod_2"][1],
        "a_in": a["a_w_in"][0], "a_out": a["a_w_out"][0],
        "gr": a["a_gate_r_w"][0].reshape(1280, 256), "gi": a["a_gate_i_w"][0].reshape(1280, 256),
        "b_in": np.concatenate([b[:, 0:1024], b[:, 1024:1088], b[:, 1024:1088], b[:, 1152:1664], b[:, 1664:1728],
                                b[:, 1664:1728], pad(np.concatenate([b[:, 1088:1152], b[:, 1728:1736]], 1), 128)], 1),
        "b_out": a["b_w_out"][0],
        "e_in": np.concatenate([e[:, 0:2048], e[:, 2080:2464], np.pad(e[:, 2464:2496], ((0, 0), (64, 32))),
                                pad(e[:, 2048:2080], 128)], 1),
        "e_out": a["w_out_even_2"][0],
        "kvv": kv[:, :, 64:].reshape(128, 512),
        "kvk": np.pad(kv[:, :, :64], ((0, 0), (0, 0), (0, 64))).reshape(128, 1024),
        "qup": np.pad(up.reshape(256, 8, 96), ((0, 0), (0, 0), (0, 32))).reshape(256, 1024),
        "o_in": np.concatenate([o[:, 0:1024], o[:, 1536:2048], o[:, 2048:2112], o[:, 2048:2112], o[:, 2112:2176],
                                o[:, 2112:2176]], 1),
        "nav": o[:, 1024:1536], "gv": o[:, 2176:2304], "o_out": a["w_out_odd_2"][0],
    }
    for i in range(2):
        mats[f"f1_{i}"], mats[f"f2_{i}"] = a["ffn_w1"][i], a["ffn_w2"][i]
        mats[f"g_{i}"], mats[f"u_{i}"], mats[f"d_{i}"] = (a["w_ffn_gate_2"][i], a["w_ffn_up_2"][i],
                                                          a["w_ffn_down_2"][i])
    plan = weight_plan()
    npanel = -(-len(plan) // PANEL)
    w = np.zeros((npanel, 128, PANEL, 128), np.float32)
    for i, t in enumerate(plan):
        if t is not None:
            name, k, m = t
            w[i // PANEL, :, i % PANEL, :] = mats[name][k * 128:(k + 1) * 128, m * 128:(m + 1) * 128]
    return w.reshape(npanel, 128, PANEL * 128)


def pack_params(a):
    def cols(v):
        return np.asarray(v).reshape(-1, 128).T

    def rows(v):
        return np.broadcast_to(np.asarray(v).reshape(1, -1), (128, v.size))

    def two(v):
        return np.concatenate([v, v]).reshape(128, 1)

    p = {
        "gmix": cols(a["norm_mix_g"]), "gffn": cols(a["norm_ffn_g"]), "ada_b": cols(a["ada_b"]),
        "convw": cols(a["a_conv_w"]), "convb": cols(a["a_conv_b"]), "rb": cols(a["a_gate_r_b"]),
        "ib": cols(a["a_gate_i_b"]), "lam": cols(a["a_lambda"]), "qg": two(a["b_q_norm_g"][0]),
        "kg": two(a["b_k_norm_g"][0]), "c1": cols(a["c"]),
        "c2": np.stack([cols(a["c_2"]), cols(a["c_ctx_2"])], 2).reshape(128, 16),
        "mod_b": cols(a["b_mod_2"]), "gpm": cols(a["g_pre_mix_2"]), "gqm": cols(a["g_post_mix_2"]),
        "gpf": cols(a["g_pre_ffn_2"]), "gqf": cols(a["g_post_ffn_2"]), "gconv": cols(a["gdn_conv_2"]),
        "alog": rows(a["gdn_a_log_2"]), "dtb": rows(a["gdn_dt_bias_2"]), "onorm": two(a["gdn_out_norm_2"][0]),
        "mqn": cols(a["mla_q_norm_2"]), "mkn": cols(a["mla_kv_norm_2"]), "gqn": two(a["gqa_q_norm_2"][0]),
        "gkn": two(a["gqa_k_norm_2"][0]),
    }
    return np.ascontiguousarray(np.concatenate([p[n] for n in PARAMS], 1))


def pack_rpb(rpb):
    t = np.pad(rpb, ((0, 0), (0, 0), (48, 48)))
    out = np.empty((8, 2, 64, 14, 64), np.float32)
    for rr in range(2):
        for col in range(64):
            out[:, rr, col] = t[:, 1 - rr:15 - rr, 63 - col:127 - col]
    return out.reshape(8, 128, 896)


def arrays_of(a):
    cst, ropes = constants()
    return {
        "in_w": pack_weights(a), "in_const": cst, "in_rope": ropes, "in_par": pack_params(a),
        "in_rpb": pack_rpb(a["na_rpb_2"][0]),
        "in_x": np.ascontiguousarray(a["x"][0].T.reshape(8, 128, S)),
        "in_ctx": np.ascontiguousarray(a["ctx_2"][0].T.reshape(8, 128, C)),
    }


def build(nc, arrays, stop=None):
    aps = [nc.dram_tensor(n, list(v.shape), F32, kind="ExternalInput").ap() for n, v in arrays.items()]
    out = nc.dram_tensor("out_y", [8, 128, S], F32, kind="ExternalOutput").ap()
    dbg = nc.dram_tensor("dbg", [16, 128, ST], F32, kind="ExternalOutput").ap() if stop else None
    program(nc, *aps, out, dbg, stop)


def kernel(**inputs):
    import concourse.bacc as bacc
    from concourse.bass_utils import run_bass_kernel_spmd as run

    arrays = arrays_of({k: np.asarray(v) for k, v in inputs.items()})
    nc = bacc.Bacc("TRN2", target_bir_lowering=False, num_devices=1)
    build(nc, arrays)
    r = run(nc, [arrays], core_ids=[0])
    y = r.results[0]["out_y"]
    return np.ascontiguousarray(y.reshape(1024, S).T).reshape(1, S, 1024)
```

```python
from contextlib import ExitStack

import numpy as np

import concourse.bass as bass
from concourse import mybir

F32 = mybir.dt.float32
ALU = mybir.AluOpType
ACT = mybir.ActivationFunctionType
AXX = mybir.AxisListType.X

S, C, ST = 512, 256, 768
NEG = -1.0e30
GONE = -3.0e38
PANEL = 32


def weight_plan():
    plan = []

    def stat(name, nmt, nkt, mt0=0):
        for m in range(mt0, mt0 + nmt):
            plan.extend((name, k, m) for k in range(nkt))

    def mov(name, nkt, mt0, n):
        while len(plan) % n:
            plan.append(None)
        for k in range(nkt):
            plan.extend((name, k, mt0 + j) for j in range(n))

    stat("a_in", 10, 8)
    for n in range(5):
        for d in range(2):
            for g in ("gr", "gi"):
                plan.extend((g, 2 * n + k, d) for k in range(2))
    stat("a_in", 10, 8, 10)
    stat("a_out", 8, 10)
    stat("f1_0", 32, 8)
    stat("f2_0", 8, 32)
    stat("b_in", 14, 8)
    stat("b_in", 1, 8, 14)
    stat("b_out", 8, 8)
    stat("f1_1", 32, 8)
    stat("f2_1", 8, 32)
    stat("e_in", 20, 8)
    stat("e_in", 1, 8, 20)
    mov("kvv", 1, 0, 4)
    for h in range(8):
        stat("qup", 1, 2, h)
        stat("kvk", 1, 1, h)
    stat("e_out", 8, 8)
    for i in range(2):
        if i:
            stat("o_in", 14, 8)
            mov("nav", 8, 0, 4)
            stat("gv", 1, 8)
            stat("o_out", 8, 8)
        for m in range(22):
            stat(f"g_{i}", 1, 8, m)
            stat(f"u_{i}", 1, 8, m)
        stat(f"d_{i}", 8, 22)
    return plan


CONSTS = {}
for _n, _w in (("ident", 128), ("ones", 128), ("bd64", 128), ("rot64", 128), ("rot32", 128),
               ("triF", 128), ("triB", 128), ("negF", 128), ("negB", 128),
               ("lvF", 896), ("lvB", 896), ("causal", 128), ("namask", 64),
               ("cosM", 512), ("sinM", 512), ("eps", 1)):
    CONSTS[_n] = (sum(w for _, w in CONSTS.values()), _w)
NCONST = sum(w for _, w in CONSTS.values())
PARAMS = {}
for _n, _w in (("gmix", 16), ("gffn", 16), ("ada_b", 96), ("convw", 40), ("convb", 10), ("rb", 10), ("ib", 10),
               ("lam", 10), ("qg", 1), ("kg", 1), ("c1", 8), ("c2", 16), ("mod_b", 96), ("gpm", 16), ("gqm", 16),
               ("gpf", 16), ("gqf", 16), ("gconv", 60), ("alog", 16), ("dtb", 16), ("onorm", 1), ("mqn", 2),
               ("mkn", 1), ("gqn", 1), ("gkn", 1)):
    PARAMS[_n] = (sum(w for _, w in PARAMS.values()), _w)
NPARAM = sum(w for _, w in PARAMS.values())


def constants():
    p = np.arange(128)
    c = {"ident": np.eye(128), "ones": np.ones((128, 128)), "eps": np.full((128, 1), 1e-6)}
    c["bd64"] = (p[:, None] // 64 == p[None] // 64)

    def rot(base, head, half, n=128):
        m = np.zeros((128, 128))
        for o in range(base, n, head):
            for j in range(half):
                m[o + half + j, o + j] = -1.0
                m[o + j, o + half + j] = 1.0
        return m

    c["rot64"] = rot(0, 64, 32)
    c["rot32"] = rot(64, 64, 16, 96)
    c["triF"] = p[:, None] <= p[None]
    c["triB"] = p[:, None] >= p[None]
    c["negF"] = np.where(c["triF"], 0.0, NEG)
    c["negB"] = np.where(c["triB"], 0.0, NEG)
    lv = []
    for k in range(7):
        s = 1 << k
        i, j = p[:, None] // s, p[None] // s
        lv.append((i // 2 == j // 2) & (i == j + 1))
    c["lvF"] = np.concatenate(lv, 1)
    c["lvB"] = np.concatenate([m.T for m in lv], 1)
    c["causal"] = np.where(p[None] <= p[:, None], 0.0, NEG)
    col = p % 64
    cs = np.clip(col - 8, 0, 48)
    kc = np.arange(64)
    c["namask"] = np.where((kc[None] >= cs[:, None]) & (kc[None] < cs[:, None] + 16), 0.0, NEG)
    t = np.arange(S)

    def axial(rot_dim):
        n = rot_dim // 4
        inv = (np.float32(10000.0) ** (-np.arange(n, dtype=np.float32) / np.float32(n))).astype(np.float32)
        row, cl = (t // 64).astype(np.float32), (t % 64).astype(np.float32)
        return np.concatenate([row[:, None] * inv, cl[:, None] * inv], -1).astype(np.float32)

    a = axial(32).T
    c["cosM"] = np.zeros((128, S))
    c["sinM"] = np.zeros((128, S))
    c["cosM"][64:96] = np.cos(np.concatenate([a, a], 0))
    c["sinM"][64:96] = np.sin(np.concatenate([a, a], 0))
    inv = (np.float32(10000.0) ** (-np.arange(0, 64, 2, dtype=np.float32) / np.float32(64))).astype(np.float32)
    ang = (t.astype(np.float32)[:, None] * inv[None]).astype(np.float32).T
    ropes = []
    for a in (ang, axial(64).T):
        a4 = np.concatenate([a] * 4, 0)
        ropes += [np.cos(a4), np.sin(a4)]
    cst = np.concatenate([np.asarray(c[n], np.float32).reshape(128, w) for n, (_, w) in CONSTS.items()], 1)
    return np.ascontiguousarray(cst), np.ascontiguousarray(np.concatenate(ropes, 1).astype(np.float32))


class Op:
    __slots__ = ("eng", "fn", "waits", "marked", "sem", "val", "dma")

    def __init__(self, eng, fn, waits, dma):
        self.eng, self.fn, self.waits, self.dma = eng, fn, waits, dma
        self.marked = False
        self.sem = self.val = None


def flat(ws):
    for w in ws:
        if w is None:
            continue
        if isinstance(w, Op):
            yield w
        else:
            yield from flat(w)


class Queues:

    NDMA = 12

    def __init__(self):
        self.q = {e: [] for e in "pvagsd"}
        self.fence = {e: [] for e in self.q}

    def op(self, eng, fn, *waits, dma=False):
        ws = list(flat(waits)) + self.fence[eng]
        self.fence[eng] = []
        for w in ws:
            w.marked = True
        o = Op(eng, fn, ws, dma)
        self.q[eng].append(o)
        return o

    def barrier(self, engines="pvag"):
        last = [next((o for o in reversed(self.q[e]) if not o.dma), None) for e in "pvag"]
        last = [o for o in last if o]
        last += [o for o in self.q["a"][-40:] if o.dma]
        self.last = last
        for e in engines:
            self.fence[e] = [o for o in last if o.eng != e or o.dma] + [o for o in last if o.eng == e]

    def number(self, sems, dsems):
        for e, ops in self.q.items():
            n = d = 0
            for o in ops:
                if o.dma:
                    o.sem, o.val = dsems[e][d % self.NDMA], 16 * (d // self.NDMA + 1)
                    d += 1
                elif o.marked:
                    n += 1
                    o.sem, o.val = sems[e], n

    def emit(self, e, eng):
        seen = {}

        def wait(sem, val):
            if seen.get(id(sem), 0) < val:
                eng.wait_ge(sem, val)
                seen[id(sem)] = val

        for o in self.q[e]:
            for w in o.waits:
                wait(w.sem, w.val)
            if o.dma:
                if o.val > 16:
                    wait(o.sem, o.val - 16)
                o.fn(eng).then_inc(o.sem, 16)
            else:
                ins = o.fn(eng)
                if o.marked:
                    ins.then_inc(o.sem, 1)
        last = {}
        for o in self.q[e]:
            if o.dma:
                last[id(o.sem)] = o
        for o in last.values():
            wait(o.sem, o.val)


class Slot:
    def __init__(self, ap):
        self.ap, self.free = ap, []


class Ring:

    def __init__(self, aps):
        self.slots, self.n = [Slot(a) for a in aps], 0

    def take(self):
        s = self.slots[self.n % len(self.slots)]
        self.n += 1
        return s


def program(nc, d_w, d_ada, d_const, d_rope, d_par, d_rpb, d_x, d_ctx, d_out, d_dbg=None, stop=None):
    plan = weight_plan()
    npanel = -(-len(plan) // PANEL)
    Q = Queues()
    with ExitStack() as es:
        SB = es.enter_context(nc.sbuf_tensor("SB", [128, 52000], F32))
        PSB = es.enter_context(nc.psum_tensor("PSB", [128, 8 * 512], F32))
        pos = [0]

        def alloc(n):
            a = SB[:, pos[0]:pos[0] + n]
            pos[0] += n
            assert pos[0] <= 52000, pos[0]
            return a

        def tiles(n, w):
            a = alloc(n * w)
            return [a[:, i * w:(i + 1) * w] for i in range(n)]

        cst, par = alloc(NCONST), alloc(NPARAM)
        K = {n: cst[:, o:o + w] for n, (o, w) in CONSTS.items()}
        Pm = {n: par[:, o:o + w] for n, (o, w) in PARAMS.items()}
        ident, ones = K["ident"], K["ones"]
        x0 = pos[0]
        X = tiles(8, S)
        XC = tiles(8, C)
        XREG = SB[:, x0:x0 + 8 * ST]
        spill = nc.dram_tensor("spill", [128, 8 * ST], F32, kind="Internal").ap()
        NSLOT = 2
        wslot = tiles(NSLOT, PANEL * 128)
        MOD1 = alloc(96)
        MOD2 = alloc(192)
        SMALL = alloc(1200)
        spos = [0]

        def small(n):
            a = SMALL[:, spos[0]:spos[0] + n]
            spos[0] += n
            assert spos[0] <= 1200
            return a

        banks = [PSB[:, i * 512:(i + 1) * 512] for i in range(8)]
        bank_slots = Ring(banks)

        def mm(out, lhsT, rhs, start, stop_, *w):
            return Q.op("p", lambda e: e.matmul(out, lhsT, rhs, start=start, stop=stop_), *w)

        def tr(out, in_, idn, *w):
            return Q.op("p", lambda e: e.transpose(out, in_, idn), *w)

        def act(out, in_, f, *w, scale=1.0, bias=0.0, accum=None):
            kw = {} if accum is None else {"accum_out": accum}
            if f == ACT.Copy:
                return Q.op("a", lambda e: e.activation(out, in_, f, scale=scale, **kw), *w)
            return Q.op("a", lambda e: e.activation(out, in_, f, bias=bias, scale=scale, **kw), *w)

        def tt(out, a, b, op, *w, eng="v"):
            return Q.op(eng, lambda e: e.tensor_tensor(out, a, b, op), *w)

        def ts(out, a, s1, s2, o0, o1, *w, eng="v"):
            if o1 is None:
                return Q.op(eng, lambda e: e.tensor_scalar(out, a, s1, None, o0), *w)
            return Q.op(eng, lambda e: e.tensor_scalar(out, a, s1, s2, o0, o1), *w)

        def stt(out, a, s, b, o0, o1, *w):
            return Q.op("v", lambda e: e.scalar_tensor_tensor(out=out, in0=a, scalar=s, in1=b, op0=o0, op1=o1), *w)

        def cp(out, a, *w, eng="v"):
            return Q.op(eng, lambda e: e.tensor_copy(out, a), *w)

        def rec(out, a, *w):
            return Q.op("v", lambda e: e.reciprocal(out, a), *w)

        def red(out, a, op, *w, negate=False):
            return Q.op("v", lambda e: e.tensor_reduce(out, a, AXX, op, negate=negate), *w)

        def ttr_max(out, a, b, first, mx, *w):
            return Q.op("v", lambda e: e.tensor_tensor_reduce(out, a, b, 1.0, first, ALU.add, ALU.max, mx), *w)

        def memset(out, v, *w, eng="g"):
            return Q.op(eng, lambda e: e.memset(out, v), *w)

        def load(out, src, *w, eng="a"):
            return Q.op(eng, lambda e: e.dma_start(out, src), *w, dma=True)

        class Stream:
            i = 0
            loads = {}
            last = {}

            def fetch(self, p):
                if p < npanel:
                    self.loads[p] = Q.op("s", lambda e: e.dma_start(wslot[p % NSLOT], d_w[p, :, :]),
                                         self.last.get(p - NSLOT), dma=True)

            def take(self, name, n=1):
                while self.i % n or plan[self.i] is None:
                    assert plan[self.i] is None, (name, plan[self.i])
                    self.i += 1
                assert plan[self.i][0] == name, (name, plan[self.i])
                p, j = divmod(self.i, PANEL)
                assert j + n <= PANEL
                while max(self.loads) < p + NSLOT - 1 and max(self.loads) < npanel - 1:
                    self.fetch(max(self.loads) + 1)
                self.p = p
                self.i += n
                return wslot[p % NSLOT][:, j * 128:(j + n) * 128], self.loads[p]

            def used(self, op):
                self.last[self.p] = op

        W = Stream()
        for p in range(NSLOT):
            W.fetch(p)

        def linear(name, nmt, nkt, xs, chunks, evac, xw, m=128, each=None):
            for mt in range(nmt):
                if each:
                    each(mt)
                bs = [bank_slots.take() for _ in chunks]
                for k in range(nkt):
                    t, tw = W.take(name)
                    for (lo, n), b in zip(chunks, bs):
                        o = mm(b.ap[0:m, 0:n], t[:, 0:m], xs[k][:, lo:lo + n], k == 0, k == nkt - 1,
                               tw, xw[k], b.free if k == 0 else None)
                    W.used(o)
                for (lo, n), b in zip(chunks, bs):
                    b.free = [evac(mt, lo, n, b.ap[0:m, 0:n], o)]

        LAT, BOTH = [(0, S)], [(0, S), (S, C)]

        l0 = [load(cst, d_const), load(par, d_par)]
        l0 += [load(X[f], d_x[f, :, :]) for f in range(8)] + [load(XC[f], d_ctx[f, :, :]) for f in range(8)]
        Q.barrier()
        for e in "pvag":
            Q.fence[e] = list(l0)
        for o in l0:
            o.marked = True
        arena0 = pos[0]

        def phase():
            Q.barrier()
            pos[0] = arena0

        cond1, cond2, ctmp = small(8), small(16), small(16)
        o = act(ctmp[:, 0:8], Pm["c1"], ACT.Tanh, scale=0.5)
        o = stt(ctmp[:, 0:8], ctmp[:, 0:8], 1.0, Pm["c1"], ALU.add, ALU.mult, o)
        oc1 = ts(cond1, ctmp[:, 0:8], 0.5, None, ALU.mult, None, o)
        o = act(ctmp, Pm["c2"], ACT.Tanh, oc1, scale=0.5)
        o = stt(ctmp, ctmp, 1.0, Pm["c2"], ALU.add, ALU.mult, o)
        oc2 = ts(cond2, ctmp, 0.5, None, ALU.mult, None, o)

        class Filler:

            def begin(self, jobs):
                self.jobs, self.left, self.ready = list(jobs), [], None
                self.ring = Ring(tiles(2, 2048))
                self.acc = [Ring(tiles(2, 512)) for _ in range(max(j[2] for j in jobs))]
                self.at, self.loaded, self.fence = 0, [], Q.last
                self.load()

            def load(self):
                if self.at < len(self.jobs):
                    for half in range(2):
                        sl = self.ring.take()
                        src = d_ada[self.jobs[self.at][0], :, half * 2048:(half + 1) * 2048]
                        o = Q.op("s", (lambda d, x: lambda e: e.dma_start(d, x))(sl.ap, src), sl.free, self.fence,
                                 dma=True)
                        self.loaded.append((sl, o))
                    self.at += 1

            def sums(self):
                if self.ready is None:
                    return
                (_, cond, m, bias, MOD, key), accs, last = self.ready
                self.ready = None
                b = bank_slots.take()
                for j in range(4):
                    for v in range(m):
                        o = mm(b.ap[:, j * m + v:j * m + v + 1], accs[v].ap[:, j * 128:(j + 1) * 128], ones[:, 0:1], True,
                               True, last, b.free)
                for v in range(m):
                    accs[v].free = [o]
                v3 = lambda a: a.rearrange("p (j m) -> p j m", m=m)
                o = tt(v3(MOD), v3(b.ap[:, 0:4 * m]), bias.unsqueeze(2).broadcast_to([128, 4, m]), ALU.add, o)
                b.free = [o]
                mod_ready.setdefault(key, []).append(o)

            def step(self):
                self.sums()
                if not self.loaded:
                    return
                job = self.jobs[self.at - 1]
                m, cond = job[2], job[1]
                accs = [self.acc[v].take() for v in range(m)]
                last = [None] * m
                for half in range(2):
                    sl, l = self.loaded.pop(0)
                    for k in range(4):
                        w = sl.ap[:, k * 512:(k + 1) * 512]
                        for v in range(m):
                            c = cond[:, (4 * half + k) * m + v:(4 * half + k) * m + v + 1]
                            if half == k == 0:
                                last[v] = ts(accs[v].ap, w, c, None, ALU.mult, None, l, accs[v].free, oc1, oc2)
                            else:
                                last[v] = stt(accs[v].ap, w, c, accs[v].ap, ALU.mult, ALU.add, last[v], l)
                    sl.free = list(last)
                self.ready = job, accs, last
                self.load()

            def flush(self):
                while self.loaded or self.ready:
                    self.step()

        fill = Filler()
        mod_ready = {}

        def mod_jobs(i, first=0, end=12):
            cond, m = (cond1, 1) if i < 2 else (cond2, 2)
            MOD = MOD1[:, 48 * i:48 * i + 48] if i < 2 else MOD2[:, 96 * (i - 2):96 * (i - 2) + 96]
            bias = Pm["ada_b"][:, 48 * i:48 * i + 48] if i < 2 else Pm["mod_b"][:, 48 * (i - 2):48 * (i - 2) + 48]
            return [(12 * i + q, cond, m, bias[:, 4 * q:4 * q + 4], MOD[:, 4 * q * m:4 * (q + 1) * m], i)
                    for q in range(first, end)]

        def part(MOD, s, m=1, which=0):
            v = MOD.rearrange("p (s f m) -> p s f m", f=8, m=m)
            return v[:, s, :, which]

        def scaled_gain(g, sc, w):
            gs = small(8)
            return gs, stt(gs, sc, 1.0, g, ALU.add, ALU.mult, w)

        def norm_stat(xs, n, count, tmp, out, w, lhs=None, key="ones", rows=128):
            b = bank_slots.take()
            for f, x in enumerate(xs):
                t = tmp.take()
                o = act(t.ap[0:rows, 0:n], x, ACT.Square, w[f], t.free)
                o = mm(b.ap[0:rows, 0:n], K[key][0:rows, 0:rows], t.ap[0:rows, 0:n], f == 0, f == len(xs) - 1, o,
                       b.free if f == 0 else None)
                t.free = [o]
            o = act(out, b.ap[0:rows, 0:n], ACT.Ln, o, scale=1.0 / count, bias=K["eps"][0:rows, :])
            b.free = [o]
            return act(out, out, ACT.Exp, o, scale=-0.5)

        def norm_mod(xs, n, H, lo, gs, sh, w, tmp, rst):
            ws = [w] * 8 if not isinstance(w, list) or len(w) != 8 else w
            o = norm_stat(xs, n, 1024.0, tmp, rst[:, 0:n], ws)
            out = []
            for f in range(8):
                h = H[f][:, lo:lo + n]
                q = stt(h, xs[f], gs[:, f:f + 1], rst[:, 0:n], ALU.mult, ALU.mult, o)
                out.append(ts(h, h, sh[:, f:f + 1], None, ALU.add, None, q, eng="g"))
            return out

        def residual(X, gate, w=None):
            def evac(mt, lo, n, ps, o):
                return stt(X[mt][:, 0:n], ps, gate[:, mt:mt + 1], X[mt][:, 0:n], ALU.mult, ALU.add, o, w)
            return evac

        def dump(aps):
            Q.barrier("a")
            for i, (a, r, n) in enumerate(aps):
                load(d_dbg[i, 0:r, 0:n], a)

        def ffn1(i, mod):
            phase()
            H, HID = tiles(8, S), tiles(32, S)
            tmp, rst = Ring(tiles(2, S)), alloc(S)
            fill.begin(mod_jobs(1) + mod_jobs(2) if i == 0 else mod_jobs(3))
            gs, og = scaled_gain(Pm["gffn"][:, 8 * i:8 * i + 8], part(mod, 4), None)
            hw = norm_mod(X, S, H, 0, gs, part(mod, 3), og, tmp, rst)
            hid = [None] * 32

            def relu2(mt, lo, n, ps, o):
                o = act(HID[mt], ps, ACT.Relu, o)
                hid[mt] = tt(HID[mt], HID[mt], HID[mt], ALU.mult, o, eng="g")
                return o

            linear(f"f1_{i}", 32, 8, H, LAT, relu2, hw, each=lambda mt: fill.step() if mt % 2 == 1 else None)
            linear(f"f2_{i}", 8, 32, HID, LAT, residual(X, part(mod, 5)), hid, each=lambda mt: fill.step())
            fill.flush()

        def rglru(mod):
            phase()
            H = tiles(8, S)
            tmp, rst = Ring(tiles(2, S)), alloc(S)
            XB = tiles(10, S + 3)
            XCV, HS, M = tiles(10, S), tiles(10, S), tiles(10, S)
            A = [x[:, 0:S] for x in XB]
            fill.begin(mod_jobs(0))
            for _ in range(4):
                fill.step()
            fill.sums()
            gs, og = scaled_gain(Pm["gmix"][:, 0:8], part(mod, 1), mod_ready[0])
            hw = norm_mod(X, S, H, 0, gs, part(mod, 0), og, tmp, rst)
            xcw = [None] * 10
            c4, z, z2, s, m_ = small(10), small(10), small(10), small(10), small(10)
            hb = small(20)
            o1 = ts(hb[:, 0:10], Pm["rb"], 0.5, None, ALU.mult, None)
            o1 = ts(hb[:, 10:20], Pm["ib"], 0.5, None, ALU.mult, None, o1)
            osp = softplus(s, Pm["lam"], -1.0, z, z2, m_, o1)
            o4 = ts(c4, s, -4.0, None, ALU.mult, None, osp)
            n4 = small(10)
            o4 = ts(n4, s, 4.0, None, ALU.mult, None, o4)

            def conv(mt, lo, n, ps, o):
                xb = XB[mt]
                z0 = memset(xb[:, 0:3], 0.0)
                o = act(xb[:, 3:3 + S], ps, ACT.Copy, o)
                w = lambda j: Pm["convw"][:, j * 10 + mt:j * 10 + mt + 1]
                x = XCV[mt]
                q = ts(x, xb[:, 0:S], w(0), Pm["convb"][:, mt:mt + 1], ALU.mult, ALU.add, o, z0)
                for j in range(1, 4):
                    q = stt(x, xb[:, j:j + S], w(j), x, ALU.mult, ALU.add, q)
                xcw[mt] = q
                return o

            linear("a_in", 10, 8, H, LAT, conv, hw, each=lambda mt: fill.step())
            fill.flush()
            ops = [None] * 10
            for n in range(5):
                for d in range(2):
                    f = 2 * n + d
                    got = []
                    for g, half in (("gr", hb[:, f:f + 1]), ("gi", hb[:, 10 + f:11 + f])):
                        b = bank_slots.take()
                        for k in range(2):
                            t, tw = W.take(g)
                            o = mm(b.ap, t, XCV[2 * n + k], k == 0, k == 1, tw, xcw[2 * n + k],
                                   b.free if k == 0 else None)
                            W.used(o)
                        dst = A[f] if g == "gr" else M[f]
                        o = act(dst, b.ap, ACT.Tanh, o, o1, scale=0.5, bias=half)
                        b.free = [o]
                        got.append(o)
                    o = stt(HS[f], M[f], 1.0, XCV[f], ALU.add, ALU.mult, got[1])
                    o2 = act(M[f], A[f], ACT.Tanh, got[0], o, o4, scale=n4[:, f:f + 1], bias=n4[:, f:f + 1])
                    o3 = act(A[f], A[f], ACT.Exp, o2, scale=c4[:, f:f + 1], bias=c4[:, f:f + 1])
                    ops[f] = [o, o2, o3]
            for f in range(10):
                o, o2, o3 = ops[f]
                t = tmp.take()
                q = tt(t.ap, A[f], A[f], ALU.mult, o3, t.free, eng="g")
                q = stt(M[f], t.ap, 1.0, M[f], ALU.add, ALU.mult, q, o2)
                t.free = [q]
                ops[f] = [o, o3, q]
            for f in range(10):
                o, o3, q = ops[f]
                q = act(M[f], M[f], ACT.Sqrt, q)
                q = stt(M[f], M[f], 0.5, HS[f], ALU.mult, ALU.mult, q, o)
                ops[f] = Q.op("v", (lambda f: lambda e: e.tensor_tensor_scan(HS[f], A[f], M[f], 0.0, ALU.mult,
                                                                             ALU.add))(f), q, o3)
            yw = [None] * 10

            def gelu(mt, lo, n, ps, o):
                t, u = A[mt], XCV[mt]
                q0 = act(u, ps, ACT.Copy, o, ops[mt])
                q = tt(t, u, u, ALU.mult, q0, ops[mt], eng="g")
                q = ts(t, t, 0.044715, 1.0, ALU.mult, ALU.add, q, eng="g")
                q = tt(t, t, u, ALU.mult, q, eng="g")
                q = act(t, t, ACT.Tanh, q, scale=0.7978845608028654)
                q = stt(t, t, 1.0, u, ALU.add, ALU.mult, q)
                yw[mt] = stt(HS[mt], t, 0.5, HS[mt], ALU.mult, ALU.mult, q)
                return q0

            linear("a_in", 10, 8, H, LAT, gelu, hw)
            linear("a_out", 8, 10, HS, LAT, residual(X, part(mod, 2), mod_ready[0]), yw)

        def softplus(out, x, sign, z, z2, mx, *w):
            o = ts(mx, x, sign, 0.0, ALU.mult, ALU.max, *w)
            o2 = ts(z, x, -1.0, None, ALU.mult, None, o)
            o2 = tt(z, z, x, ALU.min, o2)
            o = act(z, z, ACT.Exp, o2)
            o = ts(z2, z, 2.0, None, ALU.add, None, o)
            o = rec(z2, z2, o)
            o = tt(z, z, z2, ALU.mult, o)
            o = tt(z2, z, z, ALU.mult, o)
            n = 9
            o = ts(out, z2, 1.0 / (2 * n + 1), 1.0 / (2 * n - 1), ALU.mult, ALU.add, o)
            for k in range(n - 1, 0, -1):
                o = tt(out, out, z2, ALU.mult, o)
                o = ts(out, out, 1.0 / (2 * k - 1), None, ALU.add, None, o)
            o = tt(out, out, z, ALU.mult, o)
            return stt(out, out, 2.0, mx, ALU.mult, ALU.add, o)

        def rope(x, n, cos, sin, tmp, w, key="rot64", lo=0, hi=128, ring=None):
            b = (ring or bank_slots).take()
            o = mm(b.ap[0:hi, 0:n], K[key][0:hi, 0:hi], x[0:hi, 0:n], True, True, w, b.free)
            t = tmp.take()
            q = tt(t.ap[lo:hi, 0:n], b.ap[lo:hi, 0:n], sin[lo:hi, 0:n], ALU.mult, o, t.free)
            b.free = [q]
            r = tt(x[lo:hi, 0:n], x[lo:hi, 0:n], cos[lo:hi, 0:n], ALU.mult, o, w, eng="g")
            r = tt(x[lo:hi, 0:n], x[lo:hi, 0:n], t.ap[lo:hi, 0:n], ALU.add, q, r, eng="g")
            t.free = [r]
            return r

        def attention(pairs, nqb, qT, kT, V, nkeys, mask, out, wq, hook=None):
            held = [x.free for x in bank_slots.slots]
            nk_max = max(nkeys(b) for b in range(nqb))
            wide = nk_max > 512
            sring = Ring([PSB[:, 0:1024], PSB[:, 1024:2048]] if wide else banks[0:4])
            for j, x in enumerate(sring.slots):
                x.free = held[2 * j:2 * j + 2] if wide else held[j]
            tring, oring = Ring(banks[4:6]), Ring(banks[6:8])
            for j in range(2):
                tring.slots[j].free, oring.slots[j].free = held[4 + j], held[6 + j]
            sb, pt, st = Ring(tiles(3, nk_max)), Ring(tiles(2, nk_max)), Ring(tiles(6, 8))
            ov = Ring(tiles(2, 128 * nqb))
            items = [(p, hh, b) for p in range(pairs) for hh in range(2) for b in range(nqb)]
            state, pair, done = {}, {}, []

            def scores(i):
                p, hh, b = items[i]
                h, nk = 2 * p + hh, nkeys(b)
                s = sring.take()
                o = None
                for lo in range(0, nk, 512):
                    n = min(512, nk - lo)
                    o = mm(s.ap[:, lo:lo + n], qT(h, b), kT(h, b, lo, n), True, True, wq(h), s.free)
                pb, sc = sb.take(), st.take()
                mx, m2, s1, s2, rc = (sc.ap[:, j:j + 1] for j in range(5))
                masked = mask(h, b)
                free = [pb.free, sc.free]
                if masked is None:
                    o = red(mx, s.ap[:, 0:nk], ALU.max, o, free, negate=True)
                    e_ = act(pb.ap[:, 0:nk], s.ap[:, 0:nk], ACT.Exp, o, bias=mx, accum=s1)
                    s.free = [e_]
                    o = rec(rc, s1, e_)
                else:
                    n, m_, mw = masked
                    first = -3.0e38
                    if n < nk:
                        o = red(m2, s.ap[:, n:nk], ALU.max, o, free)
                        first = m2
                    o = ttr_max(pb.ap[:, 0:n], s.ap[:, 0:n], m_, first, mx, o, mw, free)
                    om = o
                    o = ts(mx, mx, -1.0, None, ALU.mult, None, o)
                    e_ = act(pb.ap[:, 0:n], pb.ap[:, 0:n], ACT.Exp, o, bias=mx, accum=s1)
                    s.free = [om]
                    if n < nk:
                        e2 = act(pb.ap[:, n:nk], s.ap[:, n:nk], ACT.Exp, o, bias=mx, accum=s2)
                        s.free = [om, e2]
                        o = tt(s1, s1, s2, ALU.add, e_, e2)
                        e_ = [e_, e2]
                    else:
                        o = e_
                    o = rec(rc, s1, o)
                state[i] = pb, sc, rc, e_, o

            def transposed(i):
                p, hh, b = items[i]
                nk = nkeys(b)
                pb, sc, rc, e_, o = state[i]
                ptb = pt.take()
                evs = []
                for lo in range(0, nk, 512):
                    n = min(512, nk - lo)
                    t = tring.take()
                    for j in range(0, n, 128):
                        q = tr(t.ap[:, j:j + 128], pb.ap[:, lo + j:lo + j + 128], ident, e_, t.free)
                    ev = act(ptb.ap[:, lo:lo + n], t.ap[:, 0:n], ACT.Copy, q, ptb.free)
                    t.free = [ev]
                    evs.append(ev)
                pb.free = [q]
                state[i] = sc, rc, o, ptb, evs

            def values(i):
                p, hh, b = items[i]
                h = 2 * p + hh
                sc, rc, orc, ptb, evs = state.pop(i)
                if p not in pair:
                    pair[p] = ov.take(), []
                osb, ops = pair[p]
                ob = oring.take()
                nt = nkeys(b) // 128
                for j in range(nt):
                    vap, vw = V(h, b, j)
                    q = mm(ob.ap[:, 0:64], ptb.ap[:, j * 128:j * 128 + 128], vap, j == 0, j == nt - 1, evs, vw, ob.free)
                ptb.free = [q]
                at = b * 128 + hh * 64
                o = ts(osb.ap[:, at:at + 64], ob.ap[:, 0:64], rc, None, ALU.mult, None, q, orc, osb.free)
                ob.free = sc.free = [o]
                ops.append(o)

            def gathered(p):
                osb, ops = pair.pop(p)
                for b0 in range(0, nqb, 4):
                    t, nb = tring.take(), min(4, nqb - b0)
                    for b in range(nb):
                        q = tr(t.ap[:, b * 128:(b + 1) * 128], osb.ap[:, (b0 + b) * 128:(b0 + b + 1) * 128], ident, ops,
                               t.free)
                    o = act(out(p)[:, b0 * 128:(b0 + nb) * 128], t.ap[:, 0:nb * 128], ACT.Copy, q)
                    t.free = [o]
                    done.append(o)
                osb.free = [q]

            n = len(items)
            for i in range(n + 4):
                if hook:
                    hook(i, tring)
                if i < n:
                    scores(i)
                if 1 <= i <= n:
                    transposed(i - 1)
                if 2 <= i <= n + 1:
                    values(i - 2)
                if i >= 4 and (i - 3) % (2 * nqb) == 0:
                    gathered((i - 3) // (2 * nqb) - 1)
            for x in bank_slots.slots:
                x.free = []
            Q.barrier()
            return done

        def head_norm(x, n, gcol, scale, tmp, rst, w):
            r = rst.take()
            o = norm_stat([x], n, 64.0, tmp, r.ap[:, 0:n], [[w, r.free]], key="bd64")
            q = stt(x, x, gcol, r.ap[:, 0:n], ALU.mult, ALU.mult, o, w)
            r.free = [q]
            if scale != 1.0:
                q = ts(x, x, scale, None, ALU.mult, None, q, eng="g")
            return q

        def dsa(mod):
            phase()
            H = tiles(8, S)
            QT, QI, KK, KI = tiles(8, S), tiles(4, S), alloc(S), alloc(S)
            VW = tiles(4, 72)
            RP = tiles(2, S)
            AO = tiles(8, S)
            MK = [alloc(128 * (b + 1)) for b in range(4)]
            tmp, rst = Ring(tiles(2, S)), Ring(tiles(2, S))
            lr = load(RP[0], d_rope[:, 0:S]), load(RP[1], d_rope[:, S:2 * S])
            Q.barrier("a")
            gs, og = scaled_gain(Pm["gmix"][:, 8:16], part(mod, 1), None)
            hw = norm_mod(X, S, H, 0, gs, part(mod, 0), og, tmp, rst.slots[0].ap)
            rst.slots[0].free = [hw]
            dst = QT + [KK] + QI + [KI]
            rdy = [None] * 14

            def ev(mt, lo, n, ps, o):
                o = act(dst[mt], ps, ACT.Copy, o)
                w = o
                if mt < 8:
                    w = head_norm(dst[mt], S, Pm["qg"], 0.125, tmp, rst, o)
                elif mt == 8:
                    w = head_norm(dst[mt], S, Pm["kg"], 1.0, tmp, rst, o)
                rdy[mt] = rope(dst[mt], S, RP[0], RP[1], tmp, [w, lr])
                return o

            linear("b_in", 14, 8, H, LAT, ev, hw)
            bs = [bank_slots.take() for _ in range(4)]
            for k in range(8):
                t, tw = W.take("b_in")
                for b in range(4):
                    o = mm(bs[b].ap[:, 0:72], H[k][:, b * 128:(b + 1) * 128], t[:, 0:72], k == 0, k == 7, tw, hw[k],
                           bs[b].free if k == 0 else None)
                W.used(o)
            vw = []
            for b in range(4):
                o1 = act(VW[b], bs[b].ap[:, 0:72], ACT.Copy, o)
                bs[b].free = [o1]
                o1 = ts(VW[b][:, 64:72], VW[b][:, 64:72], 8.0 ** -0.5, None, ALU.mult, None, o1, eng="g")
                vw.append(o1)
            SC = tiles(2, S)
            m8 = alloc(8)
            lt = Ring(tiles(3, S))
            mk = []
            for b in range(4):
                nk = 128 * (b + 1)
                if b == 0:
                    mk.append(cp(MK[0], K["causal"]))
                    continue
                sc = SC[0][:, 0:nk]
                prev = None
                for h in range(8):
                    bk = bank_slots.take()
                    r = 64 * (h % 2)
                    o = mm(bk.ap[:, 0:nk], QI[h // 2][r:r + 64, b * 128:(b + 1) * 128], KI[r:r + 64, 0:nk], True, True,
                           rdy[9 + h // 2], rdy[13], bk.free)
                    l = lt.take()
                    o = act(l.ap[:, 0:nk], bk.ap[:, 0:nk], ACT.Relu, o, l.free, scale=0.125)
                    bk.free = [o]
                    wcol = VW[b][:, 64 + h:65 + h]
                    if h == 0:
                        prev = ts(sc, l.ap[:, 0:nk], wcol, None, ALU.mult, None, o, vw[b], mk[-1])
                    else:
                        prev = stt(sc, l.ap[:, 0:nk], wcol, sc, ALU.mult, ALU.add, o, prev)
                    l.free = [prev]
                o = tt(sc[:, nk - 128:nk], sc[:, nk - 128:nk], K["causal"], ALU.add, prev)
                cur, nxt = SC
                for r in range(16):
                    a, z = cur[:, 0:nk], nxt[:, 0:nk]
                    o = Q.op("v", (lambda a: lambda e: e.max(m8, a))(a), o)
                    o = Q.op("v", (lambda a, z: lambda e: e.match_replace(z, m8, a, GONE))(a, z), o)
                    cur, nxt = nxt, cur
                mk.append(ts(MK[b], cur[:, 0:nk], 0.5 * GONE, NEG, ALU.is_gt, ALU.mult, o))

            done = attention(8, 4,
                      lambda h, b: QT[h // 2][64 * (h % 2):64 * (h % 2) + 64, b * 128:(b + 1) * 128],
                      lambda h, b, lo, n: KK[64 * (h % 2):64 * (h % 2) + 64, lo:lo + n],
                      lambda h, b, j: (VW[j][:, 0:64], vw[j]),
                      lambda b: 128 * (b + 1),
                      lambda h, b: (128 * (b + 1), MK[b], mk[b]),
                      lambda p: AO[p], lambda h: [rdy[h // 2], rdy[8]])
            linear("b_out", 8, 8, AO, LAT, residual(X, part(mod, 2)), done)

        def mods2(i):
            return [(part(MOD2, s, 2, 0), part(MOD2, s, 2, 1)) for s in range(6)]

        def pre2(i, m, gname, s_sh, s_sc, H, tmp, rst, both):
            gl, o1 = scaled_gain(Pm[gname][:, 8 * i:8 * i + 8], m[s_sc][0], None)
            hw = norm_mod(X, S, H, 0, gl, m[s_sh][0], o1, tmp, rst)
            hw = [[w] for w in hw]
            if both:
                gc, o2 = scaled_gain(Pm[gname][:, 8 * i:8 * i + 8], m[s_sc][1], None)
                hc = norm_mod(XC, C, H, S, gc, m[s_sh][1], [o2, hw], tmp, rst)
                hw = [a + [b] for a, b in zip(hw, hc)]
            return hw

        def post2(i, m, gname, s_gt, Y, yw, tmp, rst, both):
            for which, (lo, n, xs) in enumerate([(0, S, X), (S, C, XC)][:2 if both else 1]):
                gg = small(8)
                og = tt(gg, m[s_gt][which], Pm[gname][:, 8 * i:8 * i + 8], ALU.mult)
                o = norm_stat([y[:, lo:lo + n] for y in Y], n, 1024.0, tmp, rst[:, 0:n],
                              [[w, og] for w in yw])
                for f in range(8):
                    y = Y[f][:, lo:lo + n]
                    q = stt(y, y, gg[:, f:f + 1], rst[:, 0:n], ALU.mult, ALU.mult, o, og)
                    last = tt(xs[f], xs[f], y, ALU.add, q, eng="g")
                Q.barrier()

        def ffn2(i, m, both):
            phase()
            chunks = BOTH if both else LAT
            wdt = ST if both else S
            H, Y, HID = tiles(8, wdt), tiles(8, wdt), tiles(22, wdt)
            tmp, rst = Ring(tiles(2, S)), alloc(S)
            hw = pre2(i, m, "gpf", 3, 4, H, tmp, rst, both)
            hid = [[] for _ in range(22)]
            gr = Ring([y[:, 0:S] for y in Y[0:4]])
            for mt in range(22):
                bs = {}
                for name in ("g", "u"):
                    bs[name] = [bank_slots.take() for _ in chunks]
                    for k in range(8):
                        t, tw = W.take(f"{name}_{i}")
                        for (lo, n), b in zip(chunks, bs[name]):
                            o = mm(b.ap[:, 0:n], t, H[k][:, lo:lo + n], k == 0, k == 7, tw, hw[k],
                                   b.free if k == 0 else None)
                        W.used(o)
                for (lo, n), bg, bu in zip(chunks, bs["g"], bs["u"]):
                    t = gr.take()
                    q = act(t.ap[:, 0:n], bg.ap[:, 0:n], ACT.Tanh, o, t.free, scale=0.5)
                    q = stt(t.ap[:, 0:n], t.ap[:, 0:n], 1.0, bg.ap[:, 0:n], ALU.add, ALU.mult, q)
                    bg.free = [q]
                    q = stt(HID[mt][:, lo:lo + n], t.ap[:, 0:n], 0.5, bu.ap[:, 0:n], ALU.mult, ALU.mult, q)
                    bu.free = t.free = [q]
                    hid[mt].append(q)
            yw = [[] for _ in range(8)]

            def ev(mt, lo, n, ps, o):
                o = act(Y[mt][:, lo:lo + n], ps, ACT.Copy, o)
                yw[mt].append(o)
                return o

            linear(f"d_{i}", 8, 22, HID, chunks, ev, hid)
            post2(i, m, "gqf", 5, Y, yw, tmp, rst, both)

        def silu_half(out, x, t, *w):
            o = act(t, x, ACT.Tanh, *w)
            return stt(out, t, 1.0, x, ALU.add, ALU.mult, o)

        def even(m):
            phase()
            QKV, GT = tiles(12, ST), tiles(4, ST)
            MIXb = alloc(8 * ST)
            H = [MIXb[:, f * ST:(f + 1) * ST] for f in range(8)]
            RAW = tiles(4, ST)
            AB = alloc(6 * 32)
            mark = pos[0]
            tmp, rst = Ring(tiles(2, S)), alloc(S)
            hw = pre2(0, m, "gpm", 0, 1, H, tmp, rst, True)
            pads = Ring(tiles(2, 776))
            cw = small(60)
            ocw = ts(cw, Pm["gconv"], 0.5, None, ALU.mult, None)
            z = []
            for sl in pads.slots:
                for lo in (0, 514, 516, 774):
                    z.append(memset(sl.ap[:, lo:lo + 2], 0.0))
            qw = [None] * 12
            rw = [[] for _ in range(4)]
            gw = [[] for _ in range(4)]
            l2 = Ring([rst, tmp.slots[1].ap])
            tmp1 = Ring([tmp.slots[0].ap])
            cur = {}

            def ev(mt, lo, n, ps, o):
                if mt >= 16:
                    o = act(RAW[mt - 16][:, lo:lo + n], ps, ACT.Copy, o)
                    rw[mt - 16].append(o)
                    return o
                if mt >= 12:
                    g = GT[mt - 12][:, lo:lo + n]
                    q = act(g, ps, ACT.Tanh, o, scale=0.5)
                    q = stt(g, g, 1.0, ps, ALU.add, ALU.mult, q)
                    gw[mt - 12].append(q)
                    return q
                if lo == 0:
                    cur["p"] = pads.take()
                    cur["q"] = []
                pd = cur["p"]
                off = 2 if lo == 0 else 518
                o = act(pd.ap[:, off:off + n], ps, ACT.Copy, o, pd.free, z)
                x = QKV[mt][:, lo:lo + n]
                w = lambda j: cw[:, j * 12 + mt:j * 12 + mt + 1]
                q = ts(x, pd.ap[:, off - 2:off - 2 + n], w(0), None, ALU.mult, None, o, ocw)
                for j in range(1, 5):
                    q = stt(x, pd.ap[:, off - 2 + j:off - 2 + j + n], w(j), x, ALU.mult, ALU.add, q)
                q = silu_half(x, x, pd.ap[:, off:off + n], q)
                cur["q"].append(q)
                if lo:
                    pd.free = list(cur["q"])
                    qw[mt] = list(cur["q"])
                return o

            linear("e_in", 20, 8, H, BOTH, ev, hw)
            bs = bank_slots.take()
            for blk in range(6):
                pass
            b6 = [bs] + [bank_slots.take() for _ in range(5)]
            for k in range(8):
                t, tw = W.take("e_in")
                for blk in range(6):
                    o = mm(b6[blk].ap[:, 0:32], H[k][:, blk * 128:(blk + 1) * 128], t[:, 0:32], k == 0, k == 7, tw, hw[k],
                           b6[blk].free if k == 0 else None)
                W.used(o)
            for blk in range(6):
                q = act(AB[:, blk * 32:(blk + 1) * 32], b6[blk].ap[:, 0:32], ACT.Copy, o)
                b6[blk].free = [q]
            Q.barrier()
            for f in range(8):
                for lo, n in BOTH:
                    x = QKV[f][:, lo:lo + n]
                    t = l2.take()
                    o = norm_stat([x], n, 1.0, tmp1, t.ap[:, 0:n], [[qw[f], t.free]], key="bd64")
                    o = tt(x, x, t.ap[:, 0:n], ALU.mult, o)
                    t.free = [o]
                    if f < 4:
                        ts(x, x, 0.125, None, ALU.mult, None, o, eng="g")
            Q.barrier()
            load(spill, XREG)
            Q.barrier()
            pos[0] = mark
            mla(RAW, MIXb)
            Q.barrier()
            pos[0] = mark - 6 * 32 - 4 * ST
            ab = alloc(192)
            gdn(QKV, GT, MIXb[:, 0:4 * ST], AB, ab)
            phase_keep = MIXb
            MIX = [QKV[f] for f in range(4)] + [MIXb[:, (4 + f) * ST:(5 + f) * ST] for f in range(4)]
            Q.barrier()
            pos[0] = mark - 6 * 32 - 4 * ST
            Y = tiles(8, ST)
            yw = [[] for _ in range(8)]
            tmp, rst = Ring(tiles(2, S)), alloc(S)

            def evy(mt, lo, n, ps, o):
                o = act(Y[mt][:, lo:lo + n], ps, ACT.Copy, o)
                yw[mt].append(o)
                return o

            load(XREG, spill)
            linear("e_out", 8, 8, MIX, BOTH, evy, [None] * 8)
            Q.barrier()
            post2(0, m, "gqm", 2, Y, yw, tmp, rst, True)

        def mla(RAW, MIXb):
            QD, KVD, KPE = RAW[0:2], RAW[2], RAW[3]
            OUT = [MIXb[:, (4 + f) * ST:(5 + f) * ST] for f in range(4)]
            VT = [MIXb[:, b * 512:(b + 1) * 512] for b in range(6)]
            save = pos[0]
            tmp, rst = Ring(tiles(1, S)), alloc(S)
            for lo, n in BOTH:
                o = norm_stat([q[:, lo:lo + n] for q in QD], n, 256.0, tmp, rst[:, 0:n], [None, None])
                for j in range(2):
                    x = QD[j][:, lo:lo + n]
                    q = stt(x, x, Pm["mqn"][:, j:j + 1], rst[:, 0:n], ALU.mult, ALU.mult, o)
                    ts(x, x, 96.0 ** -0.5, None, ALU.mult, None, q, eng="g")
                Q.barrier()
                o = norm_stat([KVD[:, lo:lo + n]], n, 128.0, tmp, rst[:, 0:n], [None])
                stt(KVD[:, lo:lo + n], KVD[:, lo:lo + n], Pm["mkn"], rst[:, 0:n], ALU.mult, ALU.mult, o)
                Q.barrier()
            rope(KPE, S, K["cosM"], K["sinM"], tmp, None, key="rot32", lo=64, hi=96)
            Q.barrier()
            t, tw = W.take("kvv", 4)
            for b in range(6):
                bk = bank_slots.take()
                o = mm(bk.ap, KVD[:, b * 128:(b + 1) * 128], t, True, True, tw, bk.free)
                bk.free = [act(VT[b], bk.ap, ACT.Copy, o)]
            W.used(o)
            pos[0] = save
            QK = [[(XREG[:, a:a + ST], XREG[:, a + ST:a + 2 * ST]) for a in (4 * ST * y, 4 * ST * y + 2 * ST)]
                  for y in range(2)]
            for y in range(2):
                for hh in range(2):
                    okp = cp(QK[y][hh][1][64:96, :], KPE[64:96, :], eng="g")
            rt = Ring(tiles(2, S))
            Q.barrier()
            qk_ready = {}

            def project(p, hh, ring):
                h = 2 * p + hh
                qh, kh = QK[p % 2][hh]
                bsq = [ring.take() for _ in BOTH]
                for k in range(2):
                    t, tw = W.take("qup")
                    for (lo, n), b in zip(BOTH, bsq):
                        o = mm(b.ap[0:96, 0:n], t[:, 0:96], QD[k][:, lo:lo + n], k == 0, k == 1, tw,
                               b.free if k == 0 else None)
                    W.used(o)
                for (lo, n), b in zip(BOTH, bsq):
                    oq = act(qh[0:96, lo:lo + n], b.ap[0:96, 0:n], ACT.Copy, o)
                    b.free = [oq]
                bsk = [ring.take() for _ in BOTH]
                t, tw = W.take("kvk")
                for (lo, n), b in zip(BOTH, bsk):
                    o = mm(b.ap[0:64, 0:n], t[:, 0:64], KVD[:, lo:lo + n], True, True, tw, b.free)
                W.used(o)
                for (lo, n), b in zip(BOTH, bsk):
                    ok = act(kh[0:64, lo:lo + n], b.ap[0:64, 0:n], ACT.Copy, o)
                    b.free = [ok]
                orp = rope(qh, S, K["cosM"], K["sinM"], rt, [oq], key="rot32", lo=64, hi=96, ring=ring)
                qk_ready[h] = [oq, ok, orp, okp]

            for hh in range(2):
                project(0, hh, bank_slots)

            def hook(i, ring):
                p, r = divmod(i, 12)
                if p < 3 and r in (4, 8):
                    project(p + 1, r // 4 - 1, ring)

            attention(4, 6,
                      lambda h, b: QK[(h // 2) % 2][h % 2][0][0:96, b * 128:(b + 1) * 128],
                      lambda h, b, l, n: QK[(h // 2) % 2][h % 2][1][0:96, (0 if b < 4 else S) + l:(0 if b < 4 else S) + l + n],
                      lambda h, b, j: (VT[(0 if b < 4 else 4) + j][:, h * 64:h * 64 + 64], None),
                      lambda b: ST if b < 4 else C, lambda h, b: None,
                      lambda p: OUT[p], lambda h: qk_ready[h], hook)

        def gdn(QKV, GT, Ob, AB0, AB):
            QT, KT, VT_ = QKV[0:4], QKV[4:8], QKV[8:12]
            O = [Ob[:, b * 512:(b + 1) * 512] for b in range(6)]
            o = cp(AB, AB0)
            Q.barrier()
            G, B = alloc(96), alloc(96)
            z, z2, mx, spx = alloc(96), alloc(96), alloc(96), alloc(96)
            ea = alloc(16)
            v3 = lambda a: a.rearrange("p (b c) -> p b c", b=6)
            o = tt(v3(spx), v3(AB)[:, :, 0:16], Pm["dtb"].unsqueeze(1).broadcast_to([128, 6, 16]), ALU.add)
            o = softplus(G, spx, 1.0, z, z2, mx, o)
            o2 = act(ea, Pm["alog"], ACT.Exp)
            o = stt(v3(G), v3(G), -1.0, ea.unsqueeze(1).broadcast_to([128, 6, 16]), ALU.mult, ALU.mult, o, o2)
            o = act(v3(B), v3(AB)[:, :, 16:32], ACT.Tanh, scale=0.5)
            o = ts(B, B, 0.5, 0.5, ALU.mult, ALU.add, o)
            Q.barrier()
            NG, EG, FT, GL, GLP = alloc(96), alloc(96), alloc(96), alloc(96), alloc(48)
            bg, bt = bank_slots.take(), bank_slots.take()
            for c in range(6):
                for d, tri in enumerate(("triF", "triB")):
                    j = c * 16 + d * 8
                    mm(bg.ap[:, j:j + 8], K[tri], G[:, j:j + 8], True, True, bg.free)
                    o = mm(bt.ap[:, j:j + 8], ones, G[:, j:j + 8], True, True, bt.free)
            o1 = act(NG, bg.ap[:, 0:96], ACT.Copy, o, scale=-1.0)
            o2 = act(EG, bg.ap[:, 0:96], ACT.Exp, o)
            o3 = act(GL, bt.ap[:, 0:96], ACT.Exp, o)
            q = tt(FT, bt.ap[:, 0:96], NG, ALU.add, o1, o3)
            bg.free, bt.free = [o2], [o3, q]
            act(FT, FT, ACT.Exp, q)
            gl2 = GL.rearrange("p (x two) -> p x two", two=2)
            cp(GLP[0:64, :], gl2[0:64, :, 0], o3)
            cp(GLP[64:128, :], gl2[64:128, :, 1], o3)
            ST_ = tiles(2, 256)
            BE = alloc(96)
            tt(BE, B, EG, ALU.mult, o2)
            for d in range(2):
                memset(ST_[d], 0.0)
            for b in range(6):
                memset(O[b], 0.0)
            Q.barrier()
            KTOK, VTOK, U, WT, KD = (tiles(2, 512) for _ in range(5))
            AT = tiles(2, 1024)
            work = [XREG[:, i * 512:(i + 1) * 512] for i in range(12)] + tiles(4, 512)
            D, DT, MT, Y = work[0:4], work[4:8], work[8:12], work[12:16]
            h3 = lambda a: a.rearrange("p (h d) -> p h d", d=64)
            g3 = lambda a: a.rearrange("p (h d) -> p h d", d=128)
            two = lambda a, y: a.rearrange("p (x two c) -> p x two c", two=2, c=64)[:, :, y, :]
            bc = lambda a, n: a.unsqueeze(2).broadcast_to([128, a.shape[1], n])
            rep = lambda a: a.unsqueeze(1).broadcast_to([128, 4, 128])
            par = lambda y: slice(64 * y, 64 * y + 64)
            col = lambda x, w=128: slice(x * w, (x + 1) * w)
            tok = (4, 5, 0, 1, 2, 3), (5, 4, 3, 2, 1, 0)
            grp = [(d, y) for d in range(2) for y in range(2)]
            none = lambda n: [[] for _ in range(n)]
            kt_free, vt_free, kd_free, at_free, u_free, wt_free = (none(2) for _ in range(6))
            y_free, dt_free, s_op = none(4), none(4), none(2)
            o_op = none(6)
            for step in range(6):
                cs = [tok[d][step] for d in range(2)]
                kb, vb, kd = [None] * 2, [None] * 2, [None] * 2
                for d in range(2):
                    cl, j0 = col(cs[d]), cs[d] * 16 + d * 8
                    ev = []
                    for src, dst, free in ((KT, KTOK[d], kt_free[d]), (VT_, VTOK[d], vt_free[d])):
                        b = bank_slots.take()
                        for f in range(4):
                            o = tr(b.ap[:, col(f)], src[f][:, cl], ident, b.free)
                        ev.append(act(dst, b.ap, ACT.Copy, o, free))
                        b.free = [ev[-1]]
                    kd[d] = tt(h3(KD[d]), h3(KTOK[d]), bc(FT[:, j0:j0 + 8], 64), ALU.mult, ev[0], kd_free[d])
                    vb[d] = tt(h3(VTOK[d]), h3(VTOK[d]), bc(B[:, j0:j0 + 8], 64), ALU.mult, ev[1], eng="g")
                    kb[d] = tt(h3(KTOK[d]), h3(KTOK[d]), bc(BE[:, j0:j0 + 8], 64), ALU.mult, ev[0], kd[d], eng="g")
                mt_op, d_op, dt_op, at_op = [None] * 4, [None] * 4, [None] * 4, [None] * 4
                for gi, (d, y) in enumerate(grp):
                    cl, j0 = col(cs[d]), cs[d] * 16 + d * 8
                    tri, neg = (("triF", "negF"), ("triB", "negB"))[d]
                    gcol = [j0 + 2 * x + y for x in range(4)]
                    b, bk, bq, bb = (bank_slots.take() for _ in range(4))
                    for x, j in enumerate(gcol):
                        o = mm(b.ap[:, col(x)], G[:, j:j + 1].broadcast_to([128, 128]), K[tri], True, True, b.free)
                    o = tt(g3(Y[gi]), g3(b.ap), rep(K[neg]), ALU.add, o, y_free[gi])
                    b.free = [o]
                    for x, j in enumerate(gcol):
                        od = act(Y[gi][:, col(x)], Y[gi][:, col(x)], ACT.Exp, o, bias=NG[:, j:j + 1])
                    for x, j in enumerate(gcol):
                        k_, q_ = KT[x][par(y), cl], QT[x][par(y), cl]
                        mm(bk.ap[:, col(x)], k_, k_, True, True, bk.free)
                        mm(bq.ap[:, col(x)], k_, q_, True, True, bq.free)
                    for x, j in enumerate(gcol):
                        o = mm(bb.ap[:, col(x)], B[:, j:j + 1].broadcast_to([128, 128]), ident, True, True, bb.free)
                    av = AT[d].rearrange("p (x two c) -> p x two c", two=2, c=128)[:, :, y, :]
                    at_op[gi] = tt(av, g3(bq.ap), g3(Y[gi]), ALU.mult, o, od, at_free[d])
                    a2 = tt(MT[gi], bk.ap, Y[gi], ALU.mult, o, od, y_free[gi])
                    mt_op[gi] = tt(MT[gi], bb.ap, MT[gi], ALU.mult, a2)
                    y_free[gi] = [at_op[gi], a2]
                    bq.free, bk.free, bb.free = [at_op[gi]], [a2], [mt_op[gi]]
                    m0 = K[("lvB", "lvF")[d]][:, 0:128]
                    o = tt(g3(DT[gi]), g3(MT[gi]), rep(m0), ALU.mult, mt_op[gi], dt_free[gi], eng="g")
                    dt_op[gi] = tt(g3(DT[gi]), rep(ident), g3(DT[gi]), ALU.subtract, o, eng="g")
                for gi in range(4):
                    b = bank_slots.take()
                    for x in range(4):
                        o = tr(b.ap[:, col(x)], DT[gi][:, col(x)], ident, dt_op[gi], b.free)
                    d_op[gi] = act(D[gi], b.ap, ACT.Copy, o)
                    b.free = [d_op[gi]]
                for lv in range(1, 7):
                    oy, oz = [None] * 4, [None] * 4
                    for gi, (d, y) in enumerate(grp):
                        b = bank_slots.take()
                        for x in range(4):
                            o = mm(b.ap[:, col(x)], MT[gi][:, col(x)], D[gi][:, col(x)], True, True, mt_op[gi], d_op[gi],
                                   b.free)
                        oy[gi] = tt(g3(Y[gi]), g3(b.ap), rep(K[("lvF", "lvB")[d]][:, col(lv)]), ALU.mult, o, y_free[gi])
                        b.free = [oy[gi]]
                    for gi in range(4):
                        b = bank_slots.take()
                        if lv < 6:
                            bz = bank_slots.take()
                            for x in range(4):
                                oz[gi] = mm(bz.ap[:, col(x)], DT[gi][:, col(x)], Y[gi][:, col(x)], True, True, oy[gi],
                                            dt_op[gi], bz.free)
                        for x in range(4):
                            o = mm(b.ap[:, col(x)], Y[gi][:, col(x)], DT[gi][:, col(x)], True, True, oy[gi], dt_op[gi],
                                   b.free)
                        y_free[gi] = [o]
                        if lv < 6:
                            d_op[gi] = tt(D[gi], D[gi], bz.ap, ALU.subtract, oz[gi], d_op[gi])
                            bz.free = [d_op[gi]]
                        dt_op[gi] = tt(DT[gi], DT[gi], b.ap, ALU.subtract, o)
                        b.free = [dt_op[gi]]
                u_op, w_op = [None] * 2, [None] * 2
                for d in range(2):
                    b, b2 = bank_slots.take(), bank_slots.take()
                    for h in range(8):
                        t_ = DT[2 * d + h % 2][:, col(h // 2)]
                        o = mm(b.ap[:, col(h, 64)], t_, VTOK[d][:, col(h, 64)], True, True, b.free, vb[d],
                               dt_op[2 * d:2 * d + 2])
                    u_op[d] = act(U[d], b.ap, ACT.Copy, o, u_free[d])
                    vt_free[d] = [o]
                    for h in range(8):
                        t_ = DT[2 * d + h % 2][:, col(h // 2)]
                        o = mm(b2.ap[par(h % 2), col(h // 2)], KTOK[d][:, col(h, 64)], t_, True, True, b2.free, kb[d])
                    w_op[d] = act(WT[d], b2.ap, ACT.Copy, o, wt_free[d])
                    kt_free[d] = [o]
                    dt_free[2 * d] = dt_free[2 * d + 1] = [o]
                    b.free, b2.free = [u_op[d]], [w_op[d]]
                nv, qs = [[], []], [[], []]
                for d in range(2):
                    cl, j0 = col(cs[d]), cs[d] * 16 + d * 8
                    for y in range(2):
                        b = bank_slots.take()
                        for x in range(4):
                            s_ = ST_[d][par(y), col(x, 64)]
                            mm(b.ap[:, col(x, 64)], WT[d][par(y), col(x)], s_, True, True, b.free, w_op[d], s_op[d])
                            o = mm(b.ap[:, 256 + x * 64:256 + (x + 1) * 64], QT[x][par(y), cl], s_, True, True)
                        nv[d].append(tt(two(U[d], y), two(U[d], y), h3(b.ap[:, 0:256]), ALU.subtract, o, u_op[d]))
                        eg = EG[:, j0:j0 + 8].rearrange("p (x two) -> p x two", two=2)[:, :, y]
                        qs[d].append(tt(two(VTOK[d], y), h3(b.ap[:, 256:512]), bc(eg, 64), ALU.mult, o, vt_free[d]))
                        b.free = [nv[d][-1], qs[d][-1]]
                    wt_free[d] = [o]
                for d in range(2):
                    j0 = cs[d] * 16 + d * 8
                    if step < 5:
                        b = bank_slots.take()
                        for h in range(8):
                            o = mm(b.ap[par(h % 2), col(h // 2, 64)], KD[d][:, col(h, 64)], U[d][:, col(h, 64)], True,
                                   True, nv[d], kd[d], b.free)
                        kd_free[d] = [o]
                        q = tt(h3(ST_[d]), h3(ST_[d]), bc(GLP[:, j0 // 2:j0 // 2 + 4], 64), ALU.mult, wt_free[d])
                        q = tt(ST_[d], ST_[d], b.ap[:, 0:256], ALU.add, q, o)
                        b.free = s_op[d] = [q]
                    bo = bank_slots.take()
                    for h in range(8):
                        o = mm(bo.ap[:, col(h, 64)], AT[d][:, col(h)], U[d][:, col(h, 64)], True, True, nv[d], at_op,
                               bo.free)
                    at_free[d] = u_free[d] = [o]
                    q = tt(VTOK[d], VTOK[d], bo.ap, ALU.add, qs[d], o)
                    bo.free = [q]
                    c = cs[d]
                    q = tt(O[c], O[c], VTOK[d], ALU.add, q, o_op[c], eng="g")
                    o_op[c] = vt_free[d] = [q]
            Q.barrier()
            hg_ = small(1)
            oh = ts(hg_, Pm["onorm"], 0.5, None, ALU.mult, None)
            sq = Ring([U[0], KTOK[0]])
            rr = Ring([WT[0][:, 0:8], WT[0][:, 8:16]])
            for b in range(6):
                t, r = sq.take(), rr.take()
                o = act(t.ap, O[b], ACT.Square, t.free)
                o = red(r.ap, h3(t.ap), ALU.add, o, r.free)
                t.free = [o]
                o = act(r.ap, r.ap, ACT.Ln, o, scale=1.0 / 64, bias=K["eps"])
                o = act(r.ap, r.ap, ACT.Exp, o, scale=-0.5)
                o = tt(h3(O[b]), h3(O[b]), bc(r.ap, 64), ALU.mult, o)
                r.free = [o]
                bk = bank_slots.take()
                for f in range(4):
                    q = tr(bk.ap[:, f * 128:(f + 1) * 128], O[b][:, f * 128:(f + 1) * 128], ident, o, bk.free)
                for f in range(4):
                    sl = slice(b * 128, (b + 1) * 128)
                    q2 = stt(QKV[f][:, sl], bk.ap[:, f * 128:(f + 1) * 128], hg_, GT[f][:, sl], ALU.mult, ALU.mult, q, oh)
                bk.free = [q2]

        def odd(m):
            phase()
            H = tiles(8, ST)
            NQ, NK_, NV = tiles(4, S), tiles(4, ST), tiles(6, 512)
            GQ, GK, GV = tiles(4, S), tiles(2, ST), tiles(6, 128)
            RP = tiles(2, S)
            lr = load(RP[0], d_rope[:, 2 * S:3 * S]), load(RP[1], d_rope[:, 3 * S:4 * S])
            Q.barrier("a")
            tmp, rst = Ring(tiles(1, S)), Ring(tiles(2, S))
            mark = pos[0]
            hw = pre2(1, m, "gpm", 0, 1, H, tmp, rst.slots[0].ap, True)
            rst.slots[0].free = [hw]

            def ev(mt, lo, n, ps, o):
                if mt < 4:
                    return act(NQ[mt], ps, ACT.Copy, o, scale=0.125)
                if mt < 8:
                    return act(NK_[mt - 4][:, lo:lo + n], ps, ACT.Copy, o)
                x = GQ[mt - 8] if mt < 12 else GK[mt - 12][:, lo:lo + n]
                o = act(x, ps, ACT.Copy, o)
                w = head_norm(x, n, Pm["gqn" if mt < 12 else "gkn"], 0.125 if mt < 12 else 1.0, tmp, rst, o)
                if lo == 0:
                    rope(x, S, RP[0], RP[1], tmp, [w, lr])
                return o

            linear("o_in", 4, 8, H, LAT, ev, hw)
            linear("o_in", 4, 8, H, BOTH, lambda mt, *a: ev(mt + 4, *a), hw)
            linear("o_in", 4, 8, H, LAT, lambda mt, *a: ev(mt + 8, *a), hw)
            linear("o_in", 2, 8, H, BOTH, lambda mt, *a: ev(mt + 12, *a), hw)
            for name, n, dst in (("nav", 4, NV), ("gv", 1, GV)):
                b6 = [bank_slots.take() for _ in range(6)]
                for k in range(8):
                    t, tw = W.take(name, n)
                    for b in range(6):
                        o = mm(b6[b].ap[:, 0:n * 128], H[k][:, b * 128:(b + 1) * 128], t, k == 0, k == 7, tw, hw[k],
                               b6[b].free if k == 0 else None)
                    W.used(o)
                for b in range(6):
                    b6[b].free = [act(dst[b], b6[b].ap[:, 0:n * 128], ACT.Copy, o)]
            Q.barrier()
            OUT = tiles(8, 512) if False else [H[f][:, 0:S] for f in range(8)]
            pos[0] = mark
            TB = Ring(tiles(2, 896))
            base = pos[0]
            for p in range(4):
                pos[0] = base
                tb, tw = [], []
                for hh in range(2):
                    t = TB.slots[hh].ap
                    Q.barrier("a")
                    l = load(t, d_rpb[2 * p + hh, :, :])
                    t3 = t.rearrange("p (e k) -> p e k", k=64)
                    tw.append(tt(t3, t3, K["namask"].unsqueeze(1).broadcast_to([128, 14, 64]), ALU.add, l, eng="g"))
                    tb.append(t)
                attention(1, 4,
                          lambda h, b: NQ[p][64 * h:64 * h + 64, b * 128:(b + 1) * 128],
                          lambda h, b, l, n: NK_[p][64 * h:64 * h + 64, l:l + n],
                          lambda h, b, j: (NV[j][:, (2 * p + h) * 64:(2 * p + h) * 64 + 64], None),
                          lambda b: ST,
                          lambda h, b: (512, tb[h][:, (6 - 2 * b) * 64:(14 - 2 * b) * 64], tw[h]),
                          lambda _: OUT[p], lambda h: None)
            pos[0] = mark
            attention(4, 4,
                      lambda h, b: GQ[h // 2][64 * (h % 2):64 * (h % 2) + 64, b * 128:(b + 1) * 128],
                      lambda h, b, l, n: GK[h // 4][64 * (h % 2):64 * (h % 2) + 64, l:l + n],
                      lambda h, b, j: (GV[j][:, (h // 4) * 64:(h // 4) * 64 + 64], None),
                      lambda b: ST, lambda h, b: None,
                      lambda p: OUT[4 + p], lambda h: None)
            pos[0] = mark
            Y = [a for a in NK_] + [alloc(S)[:, 0:S] for _ in range(4)]
            Y = [y[:, 0:S] for y in Y]
            yw = [None] * 8
            tmp, rst = Ring(tmp.slots[0:1] and [tmp.slots[0].ap]), rst.slots[0].ap

            def evy(mt, lo, n, ps, o):
                yw[mt] = act(Y[mt], ps, ACT.Copy, o)
                return yw[mt]

            linear("o_out", 8, 8, OUT, LAT, evy, [None] * 8)
            post2(1, m, "gqm", 2, Y, yw, tmp, rst, False)

        def body():
            def xdump():
                dump([(X[f], 128, S) for f in range(8)] + [(XC[f], 128, C) for f in range(8)])

            rglru(MOD1[:, 0:48])
            if stop == 1:
                return xdump()
            ffn1(0, MOD1[:, 0:48])
            if stop == 2:
                return xdump()
            dsa(MOD1[:, 48:96])
            if stop == 3:
                return xdump()
            ffn1(1, MOD1[:, 48:96])
            if stop == 4:
                return xdump()
            for i in range(2):
                m = [(part(MOD2[:, 96 * i:96 * i + 96], s, 2, 0), part(MOD2[:, 96 * i:96 * i + 96], s, 2, 1))
                     for s in range(6)]
                if i == 0:
                    even(m)
                else:
                    odd(m)
                if stop == 5 + 2 * i:
                    return xdump()
                ffn2(i, m, i == 0)
                if stop == 6 + 2 * i:
                    return xdump()
            Q.barrier("a")
            for f in range(8):
                load(d_out[f, :, :], X[f])

        body()

        sems = {e: es.enter_context(nc.semaphore(f"s_{n}")) for e, n in
                zip("pvagsd", ("tensor", "vector", "scalar", "gpsimd", "sync", "none"))}
        dsems = {e: [es.enter_context(nc.semaphore(f"d_{e}{i}")) for i in range(Q.NDMA)] for e in "as"}
        Q.number(sems, dsems)
        block = es.enter_context(nc.Block())

        @block.sync
        def _(e):
            Q.emit("s", e)

        @block.scalar
        def _(e):
            Q.emit("a", e)

        @block.tensor
        def _(e):
            Q.emit("p", e)

        @block.vector
        def _(e):
            Q.emit("v", e)

        @block.gpsimd
        def _(e):
            Q.emit("g", e)


def pack_weights(a):
    def pad(w, m):
        return np.pad(w, ((0, 0), (0, m - w.shape[1])))

    b, e, o = a["b_w_in"][0], a["w_in_even_2"][0], a["w_in_odd_2"][0]
    up, kv = a["mla_w_q_up_2"][0], a["mla_w_kv_up_2"][0].reshape(128, 8, 128)
    mats = {
        "a_in": a["a_w_in"][0], "a_out": a["a_w_out"][0],
        "gr": a["a_gate_r_w"][0].reshape(1280, 256), "gi": a["a_gate_i_w"][0].reshape(1280, 256),
        "b_in": np.concatenate([b[:, 0:1024], b[:, 1024:1088], b[:, 1024:1088], b[:, 1152:1664], b[:, 1664:1728],
                                b[:, 1664:1728], pad(np.concatenate([b[:, 1088:1152], b[:, 1728:1736]], 1), 128)], 1),
        "b_out": a["b_w_out"][0],
        "e_in": np.concatenate([e[:, 0:2048], e[:, 2080:2464], np.pad(e[:, 2464:2496], ((0, 0), (64, 32))),
                                pad(e[:, 2048:2080], 128)], 1),
        "e_out": a["w_out_even_2"][0],
        "kvv": kv[:, :, 64:].reshape(128, 512),
        "kvk": np.pad(kv[:, :, :64], ((0, 0), (0, 0), (0, 64))).reshape(128, 1024),
        "qup": np.pad(up.reshape(256, 8, 96), ((0, 0), (0, 0), (0, 32))).reshape(256, 1024),
        "o_in": np.concatenate([o[:, 0:1024], o[:, 1536:2048], o[:, 2048:2112], o[:, 2048:2112], o[:, 2112:2176],
                                o[:, 2112:2176]], 1),
        "nav": o[:, 1024:1536], "gv": o[:, 2176:2304], "o_out": a["w_out_odd_2"][0],
    }
    for i in range(2):
        mats[f"f1_{i}"], mats[f"f2_{i}"] = a["ffn_w1"][i], a["ffn_w2"][i]
        mats[f"g_{i}"], mats[f"u_{i}"], mats[f"d_{i}"] = (a["w_ffn_gate_2"][i], a["w_ffn_up_2"][i],
                                                          a["w_ffn_down_2"][i])
    plan = weight_plan()
    npanel = -(-len(plan) // PANEL)
    w = np.zeros((npanel, 128, PANEL, 128), np.float32)
    for i, t in enumerate(plan):
        if t is not None:
            name, k, m = t
            w[i // PANEL, :, i % PANEL, :] = mats[name][k * 128:(k + 1) * 128, m * 128:(m + 1) * 128]
    return w.reshape(npanel, 128, PANEL * 128)


def pack_modulation(a):
    m = np.concatenate([a["ada_w"], a["w_mod_2"]]).reshape(4, 8, 128, 12, 512)
    return np.ascontiguousarray(m.transpose(0, 3, 2, 1, 4)).reshape(48, 128, 4096)


def pack_params(a):
    def cols(v):
        return np.asarray(v).reshape(-1, 128).T

    def rows(v):
        return np.broadcast_to(np.asarray(v).reshape(1, -1), (128, v.size))

    def two(v):
        return np.concatenate([v, v]).reshape(128, 1)

    p = {
        "gmix": cols(a["norm_mix_g"]), "gffn": cols(a["norm_ffn_g"]), "ada_b": cols(a["ada_b"]),
        "convw": cols(a["a_conv_w"]), "convb": cols(a["a_conv_b"]), "rb": cols(a["a_gate_r_b"]),
        "ib": cols(a["a_gate_i_b"]), "lam": cols(a["a_lambda"]), "qg": two(a["b_q_norm_g"][0]),
        "kg": two(a["b_k_norm_g"][0]), "c1": cols(a["c"]),
        "c2": np.stack([cols(a["c_2"]), cols(a["c_ctx_2"])], 2).reshape(128, 16),
        "mod_b": cols(a["b_mod_2"]), "gpm": cols(a["g_pre_mix_2"]), "gqm": cols(a["g_post_mix_2"]),
        "gpf": cols(a["g_pre_ffn_2"]), "gqf": cols(a["g_post_ffn_2"]), "gconv": cols(a["gdn_conv_2"]),
        "alog": rows(a["gdn_a_log_2"]), "dtb": rows(a["gdn_dt_bias_2"]), "onorm": two(a["gdn_out_norm_2"][0]),
        "mqn": cols(a["mla_q_norm_2"]), "mkn": cols(a["mla_kv_norm_2"]), "gqn": two(a["gqa_q_norm_2"][0]),
        "gkn": two(a["gqa_k_norm_2"][0]),
    }
    return np.ascontiguousarray(np.concatenate([p[n] for n in PARAMS], 1))


def pack_rpb(rpb):
    t = np.pad(rpb, ((0, 0), (0, 0), (48, 48)))
    out = np.empty((8, 2, 64, 14, 64), np.float32)
    for rr in range(2):
        for col in range(64):
            out[:, rr, col] = t[:, 1 - rr:15 - rr, 63 - col:127 - col]
    return out.reshape(8, 128, 896)


def arrays_of(a):
    cst, ropes = constants()
    return {
        "in_w": pack_weights(a), "in_ada": pack_modulation(a), "in_const": cst, "in_rope": ropes, "in_par": pack_params(a),
        "in_rpb": pack_rpb(a["na_rpb_2"][0]),
        "in_x": np.ascontiguousarray(a["x"][0].T.reshape(8, 128, S)),
        "in_ctx": np.ascontiguousarray(a["ctx_2"][0].T.reshape(8, 128, C)),
    }


def build(nc, arrays, stop=None):
    aps = [nc.dram_tensor(n, list(v.shape), F32, kind="ExternalInput").ap() for n, v in arrays.items()]
    out = nc.dram_tensor("out_y", [8, 128, S], F32, kind="ExternalOutput").ap()
    dbg = nc.dram_tensor("dbg", [16, 128, ST], F32, kind="ExternalOutput").ap() if stop else None
    program(nc, *aps, out, dbg, stop)


def kernel(**inputs):
    import concourse.bacc as bacc
    from concourse.bass_utils import run_bass_kernel_spmd as run

    arrays = arrays_of({k: np.asarray(v) for k, v in inputs.items()})
    nc = bacc.Bacc("TRN2", target_bir_lowering=False, num_devices=1)
    build(nc, arrays)
    r = run(nc, [arrays], core_ids=[0])
    y = r.results[0]["out_y"]
    return np.ascontiguousarray(y.reshape(1024, S).T).reshape(1, S, 1024)
```

```python
from contextlib import ExitStack

import numpy as np

import concourse.bass as bass
from concourse import mybir

F32 = mybir.dt.float32
F32R = mybir.dt.float32r
ALU = mybir.AluOpType
ACT = mybir.ActivationFunctionType
AXX = mybir.AxisListType.X

S, C, ST = 512, 256, 768
NEG = -1.0e30
GONE = -3.0e38
PANEL = 32
SBW = 53000
GROUP = 8
FF2 = ((0, 4), (4, 8), (8, 12), (12, 16), (16, 19), (19, 22))


def weight_plan():
    plan = []

    def stat(name, nmt, nkt, mt0=0):
        for m in range(mt0, mt0 + nmt):
            plan.extend((name, k, m) for k in range(nkt))

    def mov(name, nkt, mt0, n):
        while len(plan) % n:
            plan.append(None)
        for k in range(nkt):
            plan.extend((name, k, mt0 + j) for j in range(n))

    def ffn1(i):
        while len(plan) % GROUP:
            plan.append(None)
        for q in range(4):
            stat(f"f1_{i}", 8, 8, 8 * q)
            for m in range(8):
                plan.extend((f"f2_{i}", 8 * q + k, m) for k in range(8))

    stat("a_in", 10, 8)
    for n in range(5):
        for d in range(2):
            for g in ("gr", "gi"):
                plan.extend((g, 2 * n + k, d) for k in range(2))
    stat("a_in", 10, 8, 10)
    stat("a_out", 8, 10)
    ffn1(0)
    stat("b_in", 6, 8, 9)
    stat("b_in", 9, 8)
    stat("b_out", 8, 8)
    ffn1(1)
    stat("e_in", 20, 8)
    stat("e_in", 1, 8, 20)
    mov("kvv", 1, 0, 4)
    for h in range(8):
        stat("qup", 1, 2, h)
        stat("kvk", 1, 1, h)
    stat("e_out", 8, 8)
    for i in range(2):
        if i:
            stat("o_in", 14, 8)
            mov("nav", 8, 0, 4)
            stat("gv", 1, 8)
            stat("o_out", 8, 8)
        while len(plan) % GROUP:
            plan.append(None)
        for a, b in FF2:
            for m in range(a, b):
                stat(f"g_{i}", 1, 8, m)
                stat(f"u_{i}", 1, 8, m)
            for m in range(8):
                plan.extend((f"d_{i}", k, m) for k in range(a, b))
    return plan


CONSTS = {}
for _n, _w in (("ident", 128), ("ones", 128), ("bd64", 128), ("rot64", 128), ("rot32", 128),
               ("triF", 128), ("triB", 128), ("negF", 128), ("negB", 128),
               ("lvF", 896), ("lvB", 896), ("causal", 128), ("namask", 64),
               ("cosM", 512), ("sinM", 512), ("eps", 1)):
    CONSTS[_n] = (sum(w for _, w in CONSTS.values()), _w)
NCONST = sum(w for _, w in CONSTS.values())
PARAMS = {}
for _n, _w in (("gmix", 16), ("gffn", 16), ("ada_b", 96), ("convw", 40), ("convb", 10), ("rb", 10), ("ib", 10),
               ("lam", 10), ("qg", 1), ("kg", 1), ("c1", 8), ("c2", 16), ("mod_b", 96), ("gpm", 16), ("gqm", 16),
               ("gpf", 16), ("gqf", 16), ("gconv", 60), ("alog", 16), ("dtb", 16), ("onorm", 1), ("mqn", 2),
               ("mkn", 1), ("gqn", 1), ("gkn", 1)):
    PARAMS[_n] = (sum(w for _, w in PARAMS.values()), _w)
NPARAM = sum(w for _, w in PARAMS.values())


def constants():
    p = np.arange(128)
    c = {"ident": np.eye(128), "ones": np.ones((128, 128)), "eps": np.full((128, 1), 1e-6)}
    c["bd64"] = (p[:, None] // 64 == p[None] // 64)

    def rot(base, head, half, n=128):
        m = np.zeros((128, 128))
        for o in range(base, n, head):
            for j in range(half):
                m[o + half + j, o + j] = -1.0
                m[o + j, o + half + j] = 1.0
        return m

    c["rot64"] = rot(0, 64, 32)
    c["rot32"] = rot(64, 64, 16, 96)
    c["triF"] = p[:, None] <= p[None]
    c["triB"] = p[:, None] >= p[None]
    c["negF"] = np.where(c["triF"], 0.0, NEG)
    c["negB"] = np.where(c["triB"], 0.0, NEG)
    lv = []
    for k in range(7):
        s = 1 << k
        i, j = p[:, None] // s, p[None] // s
        lv.append((i // 2 == j // 2) & (i == j + 1))
    c["lvF"] = np.concatenate(lv, 1)
    c["lvB"] = np.concatenate([m.T for m in lv], 1)
    c["causal"] = np.where(p[None] <= p[:, None], 0.0, NEG)
    col = p % 64
    cs = np.clip(col - 8, 0, 48)
    kc = np.arange(64)
    c["namask"] = np.where((kc[None] >= cs[:, None]) & (kc[None] < cs[:, None] + 16), 0.0, NEG)
    t = np.arange(S)

    def axial(rot_dim):
        n = rot_dim // 4
        inv = (np.float32(10000.0) ** (-np.arange(n, dtype=np.float32) / np.float32(n))).astype(np.float32)
        row, cl = (t // 64).astype(np.float32), (t % 64).astype(np.float32)
        return np.concatenate([row[:, None] * inv, cl[:, None] * inv], -1).astype(np.float32)

    a = axial(32).T
    c["cosM"] = np.zeros((128, S))
    c["sinM"] = np.zeros((128, S))
    c["cosM"][64:96] = np.cos(np.concatenate([a, a], 0))
    c["sinM"][64:96] = np.sin(np.concatenate([a, a], 0))
    inv = (np.float32(10000.0) ** (-np.arange(0, 64, 2, dtype=np.float32) / np.float32(64))).astype(np.float32)
    ang = (t.astype(np.float32)[:, None] * inv[None]).astype(np.float32).T
    ropes = []
    for a in (ang, axial(64).T):
        a4 = np.concatenate([a] * 4, 0)
        ropes += [np.cos(a4), np.sin(a4)]
    cst = np.concatenate([np.asarray(c[n], np.float32).reshape(128, w) for n, (_, w) in CONSTS.items()], 1)
    return np.ascontiguousarray(cst), np.ascontiguousarray(np.concatenate(ropes, 1).astype(np.float32))


class Op:
    __slots__ = ("eng", "fn", "waits", "marked", "sem", "val", "dma")

    def __init__(self, eng, fn, waits, dma):
        self.eng, self.fn, self.waits, self.dma = eng, fn, waits, dma
        self.marked = False
        self.sem = self.val = None


def flat(ws):
    for w in ws:
        if w is None:
            continue
        if isinstance(w, Op):
            yield w
        else:
            yield from flat(w)


class Queues:

    NDMA = 12

    def __init__(self):
        self.q = {e: [] for e in "pvagsd"}
        self.fence = {e: [] for e in self.q}

    def op(self, eng, fn, *waits, dma=False):
        ws = list(flat(waits)) + self.fence[eng]
        self.fence[eng] = []
        for w in ws:
            w.marked = True
        o = Op(eng, fn, ws, dma)
        self.q[eng].append(o)
        return o

    def barrier(self, engines="pvag"):
        last = [next((o for o in reversed(self.q[e]) if not o.dma), None) for e in "pvag"]
        last = [o for o in last if o]
        last += [o for o in self.q["a"][-40:] if o.dma]
        self.last = last
        for e in engines:
            self.fence[e] = [o for o in last if o.eng != e or o.dma] + [o for o in last if o.eng == e]

    def number(self, sems, dsems):
        for e, ops in self.q.items():
            n = d = 0
            for o in ops:
                if o.dma:
                    o.sem, o.val = dsems[e][d % self.NDMA], 16 * (d // self.NDMA + 1)
                    d += 1
                elif o.marked:
                    n += 1
                    o.sem, o.val = sems[e], n

    def emit(self, e, eng):
        seen = {}

        def wait(sem, val):
            if seen.get(id(sem), 0) < val:
                eng.wait_ge(sem, val)
                seen[id(sem)] = val

        for o in self.q[e]:
            for w in o.waits:
                wait(w.sem, w.val)
            if o.dma:
                if o.val > 16:
                    wait(o.sem, o.val - 16)
                o.fn(eng).then_inc(o.sem, 16)
            else:
                ins = o.fn(eng)
                if o.marked:
                    ins.then_inc(o.sem, 1)
        last = {}
        for o in self.q[e]:
            if o.dma:
                last[id(o.sem)] = o
        for o in last.values():
            wait(o.sem, o.val)


class Slot:
    def __init__(self, ap):
        self.ap, self.free = ap, []


class Ring:

    def __init__(self, aps):
        self.slots, self.n = [Slot(a) for a in aps], 0

    def take(self):
        s = self.slots[self.n % len(self.slots)]
        self.n += 1
        return s


def program(nc, d_w, d_ada, d_const, d_rope, d_par, d_rpb, d_x, d_ctx, d_out):
    plan = weight_plan()
    npanel = -(-len(plan) // PANEL)
    Q = Queues()
    with ExitStack() as es:
        with nc.sbuf_tensor("SB", [128, SBW], F32) as SB:
            pass
        PSB = es.enter_context(nc.psum_tensor("PSB", [128, 8 * 512], F32))
        pos = [0]

        def alloc(n):
            a = SB[:, pos[0]:pos[0] + n]
            pos[0] += n
            assert pos[0] <= SBW, pos[0]
            return a

        def pairs(n, w):
            width, blocks = rounded[w == ST]
            out = []
            for _ in range(n):
                at = (pos[0] - arena0) % width
                if at + 2 * w > width:
                    pos[0] += width - at
                    at = 0
                t = blocks[(pos[0] - arena0) // width]
                alloc(2 * w)
                out.append((t[:, at:at + w].bitcast(F32), t[:, at:at + w], t[:, at + w:at + 2 * w]))
            return out

        def tiles(n, w):
            a = alloc(n * w)
            return [a[:, i * w:(i + 1) * w] for i in range(n)]

        cst, par = alloc(NCONST), alloc(NPARAM)
        K = {n: cst[:, o:o + w] for n, (o, w) in CONSTS.items()}
        Pm = {n: par[:, o:o + w] for n, (o, w) in PARAMS.items()}
        ident, ones = K["ident"], K["ones"]
        x0 = pos[0]
        X = tiles(8, S)
        XC = tiles(8, C)
        XREG = SB[:, x0:x0 + 8 * ST]
        spill = nc.dram_tensor("spill", [128, 8 * ST], F32, kind="Internal").ap()
        NSLOT = 2
        wslot = tiles(NSLOT, PANEL * 128)
        RX = alloc(ST)
        MOD1 = alloc(96)
        MOD2 = alloc(192)
        SMALL = alloc(1200)
        spos = [0]

        def small(n):
            a = SMALL[:, spos[0]:spos[0] + n]
            spos[0] += n
            assert spos[0] <= 1200
            return a

        banks = [PSB[:, i * 512:(i + 1) * 512] for i in range(8)]
        bank_slots = Ring(banks)

        def mm(out, lhsT, rhs, start, stop_, *w):
            return Q.op("p", lambda e: e.matmul(out, lhsT, rhs, start=start, stop=stop_), *w)

        def tr(out, in_, idn, *w):
            return Q.op("p", lambda e: e.transpose(out, in_, idn), *w)

        def act(out, in_, f, *w, scale=1.0, bias=0.0, accum=None):
            kw = {} if accum is None else {"accum_out": accum}
            if f == ACT.Copy:
                return Q.op("a", lambda e: e.activation(out, in_, f, scale=scale, **kw), *w)
            return Q.op("a", lambda e: e.activation(out, in_, f, bias=bias, scale=scale, **kw), *w)

        def tt(out, a, b, op, *w, eng="v"):
            return Q.op(eng, lambda e: e.tensor_tensor(out, a, b, op), *w)

        def ts(out, a, s1, s2, o0, o1, *w, eng="v"):
            if o1 is None:
                return Q.op(eng, lambda e: e.tensor_scalar(out, a, s1, None, o0), *w)
            return Q.op(eng, lambda e: e.tensor_scalar(out, a, s1, s2, o0, o1), *w)

        def stt(out, a, s, b, o0, o1, *w):
            return Q.op("v", lambda e: e.scalar_tensor_tensor(out=out, in0=a, scalar=s, in1=b, op0=o0, op1=o1), *w)

        def cp(out, a, *w, eng="v"):
            return Q.op(eng, lambda e: e.tensor_copy(out, a), *w)

        def rec(out, a, *w):
            return Q.op("v", lambda e: e.reciprocal(out, a), *w)

        def red(out, a, op, *w, negate=False):
            return Q.op("v", lambda e: e.tensor_reduce(out, a, AXX, op, negate=negate), *w)

        def ttr_max(out, a, b, first, mx, *w):
            return Q.op("v", lambda e: e.tensor_tensor_reduce(out, a, b, 1.0, first, ALU.add, ALU.max, mx), *w)

        def memset(out, v, *w, eng="g"):
            return Q.op(eng, lambda e: e.memset(out, v), *w)

        def load(out, src, *w, eng="a"):
            return Q.op(eng, lambda e: e.dma_start(out, src), *w, dma=True)

        class Stream:
            i = 0
            loads = {}
            last = {}

            def fetch(self, p):
                if p < npanel:
                    self.loads[p] = Q.op("s", lambda e: e.dma_start(wslot[p % NSLOT], d_w[p, :, :]),
                                         self.last.get(p - NSLOT), dma=True)

            def take(self, name, n=1):
                while self.i % n or plan[self.i] is None:
                    assert plan[self.i] is None, (name, plan[self.i])
                    self.i += 1
                assert name is None or plan[self.i][0] == name, (name, plan[self.i])
                p, j = divmod(self.i, PANEL)
                assert j + n <= PANEL
                while max(self.loads) < p + NSLOT - 1 and max(self.loads) < npanel - 1:
                    self.fetch(max(self.loads) + 1)
                self.p = p
                self.i += n
                return wslot[p % NSLOT][:, j * 128:(j + n) * 128], self.loads[p]

            def used(self, op):
                self.last[self.p] = op

        W = Stream()

        def linear(name, nmt, nkt, xs, chunks, evac, xw, m=128, each=None):
            for mt in range(nmt):
                if each:
                    each(mt)
                bs = [bank_slots.take() for _ in chunks]
                for k in range(nkt):
                    t, tw = W.take(name)
                    for (lo, n), b in zip(chunks, bs):
                        o = mm(b.ap[0:m, 0:n], t[:, 0:m], xs[k][:, lo:lo + n], k == 0, k == nkt - 1,
                               tw, xw[k], b.free if k == 0 else None)
                    W.used(o)
                for (lo, n), b in zip(chunks, bs):
                    b.free = [evac(mt, lo, n, b.ap[0:m, 0:n], o)]

        class Split:

            def __init__(self, groups, bufs):
                self.ring, self.left, self.depth = Ring(bufs), groups, len(bufs)
                self.ready, self.j, self.cur = [], 0, None
                self.more()

            def prime(self):
                for _ in range(self.depth - 1):
                    self.more()

            def more(self):
                if self.left:
                    self.left -= 1
                    sl = self.ring.take()
                    hf, hr, lr = sl.ap
                    t, tw = W.take(None, GROUP)
                    o = act(hr, t, ACT.Copy, tw, sl.free)
                    o = tt(lr, t, hf, ALU.subtract, o, tw, eng="g")
                    W.used(o)
                    self.ready.append((sl, o))

            def take(self):
                j = self.j % GROUP
                if j == 0:
                    if self.cur:
                        self.cur[0].free = [self.op]
                        self.more()
                    self.cur = self.ready.pop(0)
                self.j += 1
                sl, o = self.cur
                c = slice(j * 128, (j + 1) * 128)
                return sl.ap[1][:, c], sl.ap[2][:, c], o

        def linear3(sp, nmt, nkt, xs, chunks, evac, xw, each=None):
            for mt in range(nmt):
                if each:
                    each(mt)
                bs = [bank_slots.take() for _ in chunks]
                for k in range(nkt):
                    wh, wl, tw = sp.take()
                    _, xh, xl = xs[k]
                    for (lo, n), b in zip(chunks, bs):
                        c = slice(lo, lo + n)
                        mm(b.ap[:, 0:n], wh, xh[:, c], k == 0, False, tw, xw[k], b.free if k == 0 else None)
                        mm(b.ap[:, 0:n], wh, xl[:, c], False, False)
                    for (lo, n), b in zip(chunks, bs):
                        sp.op = mm(b.ap[:, 0:n], wl, xh[:, lo:lo + n], False, k == nkt - 1)
                for (lo, n), b in zip(chunks, bs):
                    b.free = [evac(mt, lo, n, b.ap[:, 0:n], sp.op)]

        def split(dst, lo, n, t, *w):
            hf, hr, lr = (a[:, lo:lo + n] for a in dst)
            o = act(hr, t, ACT.Copy, *w)
            return tt(lr, t, hf, ALU.subtract, o)

        LAT, BOTH = [(0, S)], [(0, S), (S, C)]

        l0 = [load(cst, d_const), load(par, d_par)]
        l0 += [load(X[f], d_x[f, :, :]) for f in range(8)]
        Q.barrier()
        for e in "pvag":
            Q.fence[e] = list(l0)
        for o in l0:
            o.marked = True
        arena0 = pos[0] = -(-pos[0] // 64) * 64
        es.enter_context(nc.sbuf_tensor("kept", [128, arena0], F32))
        rounded = []
        for width in (4096, 3072):
            with ExitStack() as blocks:
                rounded.append((width, [blocks.enter_context(nc.sbuf_tensor(f"R{width}_{j}", [128, width], F32R))
                                        for j in range((SBW - arena0) // width)]))
        lxc = []

        def phase():
            Q.barrier()
            pos[0] = arena0

        cond1, cond2, ctmp = small(8), small(16), small(16)
        o = act(ctmp[:, 0:8], Pm["c1"], ACT.Tanh, scale=0.5)
        o = stt(ctmp[:, 0:8], ctmp[:, 0:8], 1.0, Pm["c1"], ALU.add, ALU.mult, o)
        oc1 = ts(cond1, ctmp[:, 0:8], 0.5, None, ALU.mult, None, o)
        o = act(ctmp, Pm["c2"], ACT.Tanh, oc1, scale=0.5)
        o = stt(ctmp, ctmp, 1.0, Pm["c2"], ALU.add, ALU.mult, o)
        oc2 = ts(cond2, ctmp, 0.5, None, ALU.mult, None, o)

        class Filler:

            def begin(self, jobs):
                self.jobs, self.left, self.ready = list(jobs), [], None
                self.ring = Ring(tiles(2, 2048))
                self.acc = [Ring(tiles(2, 512)) for _ in range(max(j[2] for j in jobs))]
                self.at, self.part, self.loaded, self.fence = 0, 0, [], Q.last
                self.load()

            def load(self):
                if self.at < len(self.jobs):
                    for half in range(2):
                        sl = self.ring.take()
                        src = d_ada[self.jobs[self.at][0], :, half * 2048:(half + 1) * 2048]
                        o = Q.op("s", (lambda d, x: lambda e: e.dma_start(d, x))(sl.ap, src), sl.free, self.fence,
                                 dma=True)
                        self.loaded.append((sl, o))
                    self.at += 1

            def sums(self):
                if self.ready is None:
                    return
                (_, cond, m, bias, MOD, key), accs, last = self.ready
                self.ready = None
                b = bank_slots.take()
                for j in range(4):
                    for v in range(m):
                        o = mm(b.ap[:, j * m + v:j * m + v + 1], accs[v].ap[:, j * 128:(j + 1) * 128], ones[:, 0:1], True,
                               True, last, b.free)
                for v in range(m):
                    accs[v].free = [o]
                v3 = lambda a: a.rearrange("p (j m) -> p j m", m=m)
                o = tt(v3(MOD), v3(b.ap[:, 0:4 * m]), bias.unsqueeze(2).broadcast_to([128, 4, m]), ALU.add, o)
                b.free = [o]
                mod_ready.setdefault(key, []).append(o)

            def step(self):
                if self.part == 1:
                    self.sums()
                if not self.loaded:
                    return
                job = self.jobs[self.at - 1]
                m, cond = job[2], job[1]
                if self.part == 0:
                    self.now = [self.acc[v].take() for v in range(m)], [None] * m
                accs, last = self.now
                sl, l = self.loaded.pop(0)
                for k in range(4):
                    w = sl.ap[:, k * 512:(k + 1) * 512]
                    for v in range(m):
                        c = cond[:, (4 * self.part + k) * m + v:(4 * self.part + k) * m + v + 1]
                        if self.part == k == 0:
                            last[v] = ts(accs[v].ap, w, c, None, ALU.mult, None, l, accs[v].free, oc1, oc2)
                        else:
                            last[v] = stt(accs[v].ap, w, c, accs[v].ap, ALU.mult, ALU.add, last[v], l)
                sl.free = list(last)
                if self.part == 1:
                    self.ready = job, accs, last
                    self.load()
                self.part ^= 1

            def flush(self):
                while self.loaded:
                    self.step()
                self.sums()

        fill = Filler()
        mod_ready = {}

        def mod_jobs(i, first=0, end=12):
            cond, m = (cond1, 1) if i < 2 else (cond2, 2)
            MOD = MOD1[:, 48 * i:48 * i + 48] if i < 2 else MOD2[:, 96 * (i - 2):96 * (i - 2) + 96]
            bias = Pm["ada_b"][:, 48 * i:48 * i + 48] if i < 2 else Pm["mod_b"][:, 48 * (i - 2):48 * (i - 2) + 48]
            return [(12 * i + q, cond, m, bias[:, 4 * q:4 * q + 4], MOD[:, 4 * q * m:4 * (q + 1) * m], i)
                    for q in range(first, end)]

        def part(MOD, s, m=1, which=0):
            v = MOD.rearrange("p (s f m) -> p s f m", f=8, m=m)
            return v[:, s, :, which]

        def scaled_gain(g, sc, w):
            gs = small(8)
            return gs, stt(gs, sc, 1.0, g, ALU.add, ALU.mult, w)

        def norm_stat(xs, n, count, tmp, out, w, lhs=None, key="ones", rows=128):
            b = bank_slots.take()
            for f, x in enumerate(xs):
                t = tmp.take()
                o = act(t.ap[0:rows, 0:n], x, ACT.Square, w[f], t.free)
                o = mm(b.ap[0:rows, 0:n], K[key][0:rows, 0:rows], t.ap[0:rows, 0:n], f == 0, f == len(xs) - 1, o,
                       b.free if f == 0 else None)
                t.free = [o]
            o = act(out, b.ap[0:rows, 0:n], ACT.Ln, o, scale=1.0 / count, bias=K["eps"][0:rows, :])
            b.free = [o]
            return act(out, out, ACT.Exp, o, scale=-0.5)

        class SumSq:

            def __init__(self, acc, tmp):
                self.acc, self.tmp, self.last = acc, tmp, {}

            def add(self, x, lo, n, *w):
                a = self.acc[:, lo:lo + n]
                if lo not in self.last:
                    self.last[lo] = act(a, x, ACT.Square, *w)
                else:
                    t = self.tmp.take()
                    o = act(t.ap[:, 0:n], x, ACT.Square, w, t.free)
                    self.last[lo] = tt(a, a, t.ap[:, 0:n], ALU.add, o, self.last[lo])
                    t.free = [self.last[lo]]

            def rms(self, lo, n, *w):
                b = bank_slots.take()
                o = mm(b.ap[:, 0:n], ones, self.acc[:, lo:lo + n], True, True, self.last[lo], b.free)
                return inv_rms(b, lo, n, o, *w)

        def inv_rms(b, lo, n, *w):
            r = RX[:, lo:lo + n]
            o = act(r, b.ap[:, 0:n], ACT.Ln, *w, scale=1.0 / 1024, bias=K["eps"])
            b.free = [o]
            return act(r, r, ACT.Exp, o, scale=-0.5)

        def norm_mod(xs, n, H, lo, gs, sh, w, tmp):
            rst, o = RX[:, lo:lo + n], w
            out = []
            for f in range(8):
                if isinstance(H[f], tuple):
                    t = tmp.take()
                    hf, hr, lr = (a[:, lo:lo + n] for a in H[f])
                    q = stt(t.ap[:, 0:n], xs[f], gs[:, f:f + 1], rst[:, 0:n], ALU.mult, ALU.mult, o, t.free)
                    q = act(hr, t.ap[:, 0:n], ACT.Identity, q, bias=sh[:, f:f + 1])
                    q = stt(lr, t.ap[:, 0:n], sh[:, f:f + 1], hf, ALU.add, ALU.subtract, q)
                    t.free = [q]
                    out.append(q)
                    continue
                h = H[f][:, lo:lo + n]
                q = stt(h, xs[f], gs[:, f:f + 1], rst[:, 0:n], ALU.mult, ALU.mult, o)
                out.append(act(h, h, ACT.Identity, q, bias=sh[:, f:f + 1]))
            return out

        class Later:

            def __init__(self):
                self.todo, self.n = [], 0

            def put(self, delay, fn):
                self.todo.append((self.n + delay, fn))

            def tick(self, *_):
                self.n += 1
                due = [f for d, f in self.todo if d <= self.n]
                self.todo = [x for x in self.todo if x[0] > self.n]
                for f in due:
                    f()

            def flush(self):
                while self.todo:
                    self.tick()

        def residual(X, gate, w=None, sums=None):
            def evac(mt, lo, n, ps, o):
                q = stt(X[mt][:, 0:n], ps, gate[:, mt:mt + 1], X[mt][:, 0:n], ALU.mult, ALU.add, o, w)
                if sums:
                    sums.add(X[mt][:, 0:n], 0, n, q)
                return q
            return evac

        def ffn1(i, mod):
            phase()
            H, HID, WS = pairs(8, S), pairs(8, S), pairs(3, GROUP * 128)
            tmp = Ring(tiles(3, S))
            sums = SumSq(alloc(ST), tmp)
            fill.begin(mod_jobs(1) + mod_jobs(2, 0, 6) if i == 0 else mod_jobs(2, 6) + mod_jobs(3))
            sp = Split(64, WS)
            gs, og = scaled_gain(Pm["gffn"][:, 8 * i:8 * i + 8], part(mod, 4), None)
            hw = norm_mod(X, S, H, 0, gs, part(mod, 3), og, tmp)
            sp.prime()
            if i == 1:
                for f in range(8):
                    sums.add(XC[f], S, C, lxc)
            hid = [None] * 8

            def relu2(mt, lo, n, ps, o):
                r, t = tmp.take(), tmp.take()
                q = act(r.ap, ps, ACT.Relu, o, r.free)
                q2 = tt(t.ap, r.ap, r.ap, ALU.mult, q, t.free)
                hid[mt] = split(HID[mt], 0, S, t.ap, q2)
                r.free, t.free = [q2], [hid[mt]]
                return q

            for q in range(4):
                linear3(sp, 8, 8, H, LAT, relu2, hw, each=lambda mt: fill.step() if mt < 7 else None)
                linear3(sp, 8, 8, HID, LAT, residual(X, part(mod, 5), None, sums if q == 3 else None), hid,
                        each=lambda mt: fill.step() if mt % 2 else None)
            fill.flush()
            if i == 1:
                sums.rms(S, C)
            sums.rms(0, S)

        def rglru(mod):
            phase()
            H = tiles(8, S)
            tmp = Ring(tiles(2, S))
            XB = tiles(10, S + 3)
            XCV, HS, M = tiles(10, S), tiles(10, S), tiles(10, S)
            A = [x[:, 0:S] for x in XB]
            fill.begin(mod_jobs(0))
            for p in range(NSLOT):
                W.fetch(p)
            on = norm_stat(X, S, 1024.0, tmp, RX[:, 0:S], [None] * 8)
            for _ in range(8):
                fill.step()
            fill.sums()
            gs, og = scaled_gain(Pm["gmix"][:, 0:8], part(mod, 1), mod_ready[0])
            hw = norm_mod(X, S, H, 0, gs, part(mod, 0), [og, on], tmp)
            xcw = [None] * 10
            c4, z, z2, s, m_ = small(10), small(10), small(10), small(10), small(10)
            hb = small(20)
            o1 = ts(hb[:, 0:10], Pm["rb"], 0.5, None, ALU.mult, None)
            o1 = ts(hb[:, 10:20], Pm["ib"], 0.5, None, ALU.mult, None, o1)
            osp = softplus(s, Pm["lam"], -1.0, z, z2, m_, o1)
            o4 = ts(c4, s, -4.0, None, ALU.mult, None, osp)
            n4 = small(10)
            o4 = ts(n4, s, 4.0, None, ALU.mult, None, o4)

            def conv(mt, lo, n, ps, o):
                xb = XB[mt]
                z0 = memset(xb[:, 0:3], 0.0)
                o = act(xb[:, 3:3 + S], ps, ACT.Copy, o)
                w = lambda j: Pm["convw"][:, j * 10 + mt:j * 10 + mt + 1]
                x = XCV[mt]
                q = ts(x, xb[:, 0:S], w(0), Pm["convb"][:, mt:mt + 1], ALU.mult, ALU.add, o, z0)
                for j in range(1, 4):
                    q = stt(x, xb[:, j:j + S], w(j), x, ALU.mult, ALU.add, q)
                xcw[mt] = q
                return o

            linear("a_in", 10, 8, H, LAT, conv, hw, each=lambda mt: fill.step())
            lxc.extend(load(XC[f], d_ctx[f, :, :]) for f in range(8))
            ops = [None] * 10
            for n in range(5):
                for d in range(2):
                    f = 2 * n + d
                    got = []
                    for g, half in (("gr", hb[:, f:f + 1]), ("gi", hb[:, 10 + f:11 + f])):
                        b = bank_slots.take()
                        for k in range(2):
                            t, tw = W.take(g)
                            o = mm(b.ap, t, XCV[2 * n + k], k == 0, k == 1, tw, xcw[2 * n + k],
                                   b.free if k == 0 else None)
                            W.used(o)
                        dst = A[f] if g == "gr" else M[f]
                        o = act(dst, b.ap, ACT.Tanh, o, o1, scale=0.5, bias=half)
                        b.free = [o]
                        got.append(o)
                    o = stt(HS[f], M[f], 1.0, XCV[f], ALU.add, ALU.mult, got[1])
                    o2 = act(M[f], A[f], ACT.Tanh, got[0], o, o4, scale=n4[:, f:f + 1], bias=n4[:, f:f + 1])
                    o3 = act(A[f], A[f], ACT.Exp, o2, scale=c4[:, f:f + 1], bias=c4[:, f:f + 1])
                    ops[f] = [o, o2, o3]
            for f in range(10):
                o, o2, o3 = ops[f]
                t = tmp.take()
                q = tt(t.ap, A[f], A[f], ALU.mult, o3, t.free, eng="g")
                q = stt(M[f], t.ap, 1.0, M[f], ALU.add, ALU.mult, q, o2)
                t.free = [q]
                ops[f] = [o, o3, q]
            for f in range(10):
                o, o3, q = ops[f]
                q = act(M[f], M[f], ACT.Sqrt, q)
                q = stt(M[f], M[f], 0.5, HS[f], ALU.mult, ALU.mult, q, o)
                ops[f] = Q.op("v", (lambda f: lambda e: e.tensor_tensor_scan(HS[f], A[f], M[f], 0.0, ALU.mult,
                                                                             ALU.add))(f), q, o3)
            yw = [None] * 10

            def gelu(mt, lo, n, ps, o):
                t, u = A[mt], XCV[mt]
                q0 = act(u, ps, ACT.Copy, o, ops[mt])
                q = tt(t, u, u, ALU.mult, q0, ops[mt], eng="g")
                q = ts(t, t, 0.044715, 1.0, ALU.mult, ALU.add, q, eng="g")
                q = tt(t, t, u, ALU.mult, q, eng="g")
                q = act(t, t, ACT.Tanh, q, scale=0.7978845608028654)
                q = stt(t, t, 1.0, u, ALU.add, ALU.mult, q)
                yw[mt] = stt(HS[mt], t, 0.5, HS[mt], ALU.mult, ALU.mult, q)
                return q0

            linear("a_in", 10, 8, H, LAT, gelu, hw, each=lambda mt: fill.step())
            fill.flush()
            sums = SumSq(H[0], Ring(H[1:3]))
            linear("a_out", 8, 10, HS, LAT, residual(X, part(mod, 2), mod_ready[0], sums), yw)
            sums.rms(0, S)

        def softplus(out, x, sign, z, z2, mx, *w):
            o = ts(mx, x, sign, 0.0, ALU.mult, ALU.max, *w)
            o2 = ts(z, x, -1.0, None, ALU.mult, None, o)
            o2 = tt(z, z, x, ALU.min, o2)
            o = act(z, z, ACT.Exp, o2)
            o = ts(z2, z, 2.0, None, ALU.add, None, o)
            o = rec(z2, z2, o)
            o = tt(z, z, z2, ALU.mult, o)
            o = tt(z2, z, z, ALU.mult, o)
            n = 9
            o = ts(out, z2, 1.0 / (2 * n + 1), 1.0 / (2 * n - 1), ALU.mult, ALU.add, o)
            for k in range(n - 1, 0, -1):
                o = tt(out, out, z2, ALU.mult, o)
                o = ts(out, out, 1.0 / (2 * k - 1), None, ALU.add, None, o)
            o = tt(out, out, z, ALU.mult, o)
            return stt(out, out, 2.0, mx, ALU.mult, ALU.add, o)

        def rope(x, n, cos, sin, tmp, w, key="rot64", lo=0, hi=128, ring=None):
            b = (ring or bank_slots).take()
            o = mm(b.ap[0:hi, 0:n], K[key][0:hi, 0:hi], x[0:hi, 0:n], True, True, w, b.free)
            t = tmp.take()
            q = tt(t.ap[lo:hi, 0:n], b.ap[lo:hi, 0:n], sin[lo:hi, 0:n], ALU.mult, o, t.free)
            b.free = [q]
            r = tt(x[lo:hi, 0:n], x[lo:hi, 0:n], cos[lo:hi, 0:n], ALU.mult, o, w, eng="g")
            r = tt(x[lo:hi, 0:n], x[lo:hi, 0:n], t.ap[lo:hi, 0:n], ALU.add, q, r, eng="g")
            t.free = [r]
            return r

        def attention(pairs, nqb, qT, kT, V, nkeys, mask, out, wq, hook=None):
            held = [x.free for x in bank_slots.slots]
            nk_max = max(nkeys(b) for b in range(nqb))
            wide = nk_max > 512
            sring = Ring([PSB[:, 0:1024], PSB[:, 1024:2048]] if wide else banks[0:4])
            for j, x in enumerate(sring.slots):
                x.free = held[2 * j:2 * j + 2] if wide else held[j]
            tring, oring = Ring(banks[4:6]), Ring(banks[6:8])
            for j in range(2):
                tring.slots[j].free, oring.slots[j].free = held[4 + j], held[6 + j]
            sb, pt, st = Ring(tiles(3, nk_max)), Ring(tiles(2, nk_max)), Ring(tiles(6, 8))
            ov = Ring(tiles(2, 128 * nqb))
            items = [(p, hh, b) for p in range(pairs) for hh in range(2) for b in range(nqb)]
            state, pair, done = {}, {}, []

            def scores(i):
                p, hh, b = items[i]
                h, nk = 2 * p + hh, nkeys(b)
                s = sring.take()
                o = None
                for lo in range(0, nk, 512):
                    n = min(512, nk - lo)
                    o = mm(s.ap[:, lo:lo + n], qT(h, b), kT(h, b, lo, n), True, True, wq(h), s.free)
                pb, sc = sb.take(), st.take()
                mx, m2, s1, s2, rc = (sc.ap[:, j:j + 1] for j in range(5))
                masked = mask(h, b)
                free = [pb.free, sc.free]
                if masked is None:
                    o = red(mx, s.ap[:, 0:nk], ALU.max, o, free, negate=True)
                    e_ = act(pb.ap[:, 0:nk], s.ap[:, 0:nk], ACT.Exp, o, bias=mx, accum=s1)
                    s.free = [e_]
                    o = rec(rc, s1, e_)
                else:
                    n, m_, mw = masked
                    first = -3.0e38
                    if n < nk:
                        o = red(m2, s.ap[:, n:nk], ALU.max, o, free)
                        first = m2
                    o = ttr_max(pb.ap[:, 0:n], s.ap[:, 0:n], m_, first, mx, o, mw, free)
                    om = o
                    o = ts(mx, mx, -1.0, None, ALU.mult, None, o)
                    e_ = act(pb.ap[:, 0:n], pb.ap[:, 0:n], ACT.Exp, o, bias=mx, accum=s1)
                    s.free = [om]
                    if n < nk:
                        e2 = act(pb.ap[:, n:nk], s.ap[:, n:nk], ACT.Exp, o, bias=mx, accum=s2)
                        s.free = [om, e2]
                        o = tt(s1, s1, s2, ALU.add, e_, e2)
                        e_ = [e_, e2]
                    else:
                        o = e_
                    o = rec(rc, s1, o)
                state[i] = pb, sc, rc, e_, o

            def transposed(i):
                p, hh, b = items[i]
                nk = nkeys(b)
                pb, sc, rc, e_, o = state[i]
                ptb = pt.take()
                evs = []
                for lo in range(0, nk, 512):
                    n = min(512, nk - lo)
                    t = tring.take()
                    for j in range(0, n, 128):
                        q = tr(t.ap[:, j:j + 128], pb.ap[:, lo + j:lo + j + 128], ident, e_, t.free)
                    ev = act(ptb.ap[:, lo:lo + n], t.ap[:, 0:n], ACT.Copy, q, ptb.free)
                    t.free = [ev]
                    evs.append(ev)
                pb.free = [q]
                state[i] = sc, rc, o, ptb, evs

            def values(i):
                p, hh, b = items[i]
                h = 2 * p + hh
                sc, rc, orc, ptb, evs = state.pop(i)
                if p not in pair:
                    pair[p] = ov.take(), []
                osb, ops = pair[p]
                ob = oring.take()
                nt = nkeys(b) // 128
                for j in range(nt):
                    vap, vw = V(h, b, j)
                    q = mm(ob.ap[:, 0:64], ptb.ap[:, j * 128:j * 128 + 128], vap, j == 0, j == nt - 1, evs, vw, ob.free)
                ptb.free = [q]
                at = b * 128 + hh * 64
                o = ts(osb.ap[:, at:at + 64], ob.ap[:, 0:64], rc, None, ALU.mult, None, q, orc, osb.free)
                ob.free = sc.free = [o]
                ops.append(o)

            def gathered(p):
                osb, ops = pair.pop(p)
                for b0 in range(0, nqb, 4):
                    t, nb = tring.take(), min(4, nqb - b0)
                    for b in range(nb):
                        q = tr(t.ap[:, b * 128:(b + 1) * 128], osb.ap[:, (b0 + b) * 128:(b0 + b + 1) * 128], ident, ops,
                               t.free)
                    o = act(out(p)[:, b0 * 128:(b0 + nb) * 128], t.ap[:, 0:nb * 128], ACT.Copy, q)
                    t.free = [o]
                    done.append(o)
                osb.free = [q]

            n = len(items)
            for i in range(n + 4):
                if hook:
                    hook(i, tring)
                if i < n:
                    scores(i)
                if 1 <= i <= n:
                    transposed(i - 1)
                if 2 <= i <= n + 1:
                    values(i - 2)
                if i >= 4 and (i - 3) % (2 * nqb) == 0:
                    gathered((i - 3) // (2 * nqb) - 1)
            for x in bank_slots.slots:
                x.free = []
            Q.barrier()
            return done

        def head_norm(x, chunks, count, gcol, sq, rst, later, w, then, delay=2):
            t = sq.take()
            parts = [(x[:, lo:lo + n], t.ap[:, lo:lo + n], n) for lo, n in chunks]
            sqs = [act(tp, xp, ACT.Square, w, t.free) for xp, tp, n in parts]

            def rest():
                r = rst.take()
                free, last, done = r.free, [], []
                for (lo, n), (xp, tp, _), o in zip(chunks, parts, sqs):
                    b = bank_slots.take()
                    o = mm(b.ap[:, 0:n], K["bd64"], tp, True, True, o, b.free)
                    last.append(o)
                    rp = r.ap[:, lo:lo + n]
                    o = act(rp, b.ap[:, 0:n], ACT.Ln, o, free, scale=1.0 / count, bias=K["eps"])
                    b.free = [o]
                    o = act(rp, rp, ACT.Exp, o, scale=-0.5)
                    done.append(stt(xp, xp, gcol, rp, ALU.mult, ALU.mult, o, w))
                t.free, r.free = last, done
                then(done)

            later.put(delay, rest)

        def dsa(mod):
            phase()
            H = tiles(8, S)
            QT, QI, KK, KI = tiles(8, S), tiles(4, S), alloc(S), alloc(S)
            VW = tiles(4, 72)
            RP = tiles(2, S)
            AO = tiles(8, S)
            MK = [alloc(128 * (b + 1)) for b in range(4)]
            SC = [alloc(128 * (b + 1)) for b in range(4)]
            m8 = alloc(8)
            tmp, rst, sq = Ring(tiles(2, S)), Ring(tiles(2, S)), Ring(tiles(3, S))
            lt = Ring(tiles(3, S))
            lr = load(RP[0], d_rope[:, 0:S]), load(RP[1], d_rope[:, S:2 * S])
            gs, og = scaled_gain(Pm["gmix"][:, 8:16], part(mod, 1), None)
            hw = norm_mod(X, S, H, 0, gs, part(mod, 0), og, tmp)
            g8 = small(1)
            og8 = ts(g8, Pm["qg"], 0.125, None, ALU.mult, None)
            dst = QT + [KK] + QI + [KI]
            rdy = [None] * 14
            later = Later()

            def ev(mt, lo, n, ps, o):
                o = act(dst[mt], ps, ACT.Copy, o)

                def turn(w):
                    rdy[mt] = rope(dst[mt], S, RP[0], RP[1], tmp, [w, lr])

                if mt > 8:
                    later.put(2, lambda: turn(o))
                else:
                    head_norm(dst[mt], LAT, 64.0, g8 if mt < 8 else Pm["kg"], sq, rst, later, [o, og8],
                              lambda w: later.put(1, lambda: turn(w)))
                return o

            linear("b_in", 5, 8, H, LAT, lambda mt, *a: ev(mt + 9, *a), hw, each=later.tick)
            later.tick()
            bs = [bank_slots.take() for _ in range(4)]
            for k in range(8):
                t, tw = W.take("b_in")
                for b in range(4):
                    o = mm(bs[b].ap[:, 0:72], H[k][:, b * 128:(b + 1) * 128], t[:, 0:72], k == 0, k == 7, tw, hw[k],
                           bs[b].free if k == 0 else None)
                W.used(o)
            vw = []
            for b in range(4):
                o1 = act(VW[b], bs[b].ap[:, 0:72], ACT.Copy, o)
                bs[b].free = [o1]
                o1 = ts(VW[b][:, 64:72], VW[b][:, 64:72], 8.0 ** -0.5, None, ALU.mult, None, o1, eng="g")
                vw.append(o1)
            later.flush()
            mk = {0: cp(MK[0], K["causal"])}

            def index():
                ready = {}
                for b in range(1, 4):
                    nk = 128 * (b + 1)
                    sc = SC[b]
                    prev = None
                    for h in range(8):
                        bk = bank_slots.take()
                        r = 64 * (h % 2)
                        o = mm(bk.ap[:, 0:nk], QI[h // 2][r:r + 64, b * 128:(b + 1) * 128], KI[r:r + 64, 0:nk], True,
                               True, rdy[9 + h // 2], rdy[13], bk.free)
                        l = lt.take()
                        o = act(l.ap[:, 0:nk], bk.ap[:, 0:nk], ACT.Relu, o, l.free, scale=0.125)
                        bk.free = [o]
                        wcol = VW[b][:, 64 + h:65 + h]
                        if h == 0:
                            prev = ts(sc, l.ap[:, 0:nk], wcol, None, ALU.mult, None, o, vw[b])
                        else:
                            prev = stt(sc, l.ap[:, 0:nk], wcol, sc, ALU.mult, ALU.add, o, prev)
                        l.free = [prev]
                    ready[b] = tt(sc[:, nk - 128:nk], sc[:, nk - 128:nk], K["causal"], ALU.add, prev)
                    yield
                for b in range(1, 4):
                    nk = 128 * (b + 1)
                    cur, nxt, o = SC[b], MK[b], ready[b]
                    for r in range(16):
                        o = Q.op("v", (lambda a: lambda e: e.max(m8, a))(cur), o)
                        o = Q.op("v", (lambda a, z: lambda e: e.match_replace(z, m8, a, GONE))(cur, nxt), o)
                        cur, nxt = nxt, cur
                        if r == 7:
                            yield
                    mk[b] = ts(MK[b], cur, 0.5 * GONE, NEG, ALU.is_gt, ALU.mult, o)
                    yield

            parts = index()

            def beside(mt):
                later.tick()
                next(parts, None)

            linear("b_in", 9, 8, H, LAT, ev, hw, each=beside)
            later.flush()
            for _ in parts:
                pass

            done = attention(8, 4,
                      lambda h, b: QT[h // 2][64 * (h % 2):64 * (h % 2) + 64, b * 128:(b + 1) * 128],
                      lambda h, b, lo, n: KK[64 * (h % 2):64 * (h % 2) + 64, lo:lo + n],
                      lambda h, b, j: (VW[j][:, 0:64], vw[j]),
                      lambda b: 128 * (b + 1),
                      lambda h, b: (128 * (b + 1), MK[b], mk[b]),
                      lambda p: AO[p], lambda h: [rdy[h // 2], rdy[8]])
            sums = SumSq(H[0], Ring(H[1:3]))
            linear("b_out", 8, 8, AO, LAT, residual(X, part(mod, 2), None, sums), done)
            sums.rms(0, S)


        def pre2(i, m, gname, s_sh, s_sc, H, tmp, both):
            gl, o1 = scaled_gain(Pm[gname][:, 8 * i:8 * i + 8], m[s_sc][0], None)
            hw = norm_mod(X, S, H, 0, gl, m[s_sh][0], o1, tmp)
            hw = [[w] for w in hw]
            if both:
                gc, o2 = scaled_gain(Pm[gname][:, 8 * i:8 * i + 8], m[s_sc][1], None)
                hc = norm_mod(XC, C, H, S, gc, m[s_sh][1], o2, tmp)
                hw = [a + [b] for a, b in zip(hw, hc)]
            return hw

        def post2(i, m, gname, s_gt, Y, sums, both, more=True, w=None):
            todo = [(0, S, X, 0), (S, C, XC, 1)][:2 if both else 1]
            rms = [sums.rms(lo, n) for lo, n, _, _ in todo]
            last = []
            for (lo, n, xs, which), o in zip(todo, rms):
                gg = small(8)
                og = tt(gg, m[s_gt][which], Pm[gname][:, 8 * i:8 * i + 8], ALU.mult)
                b = bank_slots.take()
                for f in range(8):
                    y = Y[f][:, lo:lo + n]
                    q = stt(y, y, gg[:, f:f + 1], RX[:, lo:lo + n], ALU.mult, ALU.mult, o, og)
                    q = tt(xs[f], xs[f], y, ALU.add, q, w, eng="g" if f % 2 else "v")
                    last.append(q)
                    if more:
                        q = act(y, xs[f], ACT.Square, q)
                        q = mm(b.ap[:, 0:n], ones, y, f == 0, f == 7, q, b.free if f == 0 else None)
                if more:
                    inv_rms(b, lo, n, q)
            return last

        def ffn2(i, m, both):
            phase()
            chunks = BOTH if both else LAT
            wdt = ST if both else S
            H, HID, WS = pairs(8, wdt), pairs(4, wdt), pairs(2 if both else 3, GROUP * 128)
            Y = tiles(8, wdt)
            tmp = Ring(tiles(3, S))
            sums = SumSq(alloc(wdt), tmp)
            sp = Split(66, WS)
            hw = pre2(i, m, "gpf", 3, 4, H, tmp, both)
            sp.prime()
            for first, end in FF2:
                hid = [[] for _ in range(end - first)]
                for mt in range(end - first):
                    kept = []

                    def keep(_, lo, n, ps, o):
                        kept.append((lo, n, ps, o))
                        return o

                    slots = [bank_slots.slots[(bank_slots.n + j) % 8] for j in range(2 * len(chunks))]
                    linear3(sp, 1, 8, H, chunks, keep, hw)
                    linear3(sp, 1, 8, H, chunks, keep, hw)
                    for c, (lo, n) in enumerate(chunks):
                        pg, pu, o = kept[c][2], kept[len(chunks) + c][2], kept[-1][3]
                        t = tmp.take()
                        x = t.ap[:, 0:n]
                        q = act(x, pg, ACT.Tanh, o, t.free, scale=0.5)
                        q = stt(x, x, 1.0, pg, ALU.add, ALU.mult, q)
                        slots[c].free = [q]
                        q = stt(x, x, 0.5, pu, ALU.mult, ALU.mult, q)
                        slots[len(chunks) + c].free = [q]
                        q = split(HID[mt], lo, n, x, q)
                        t.free = [q]
                        hid[mt].append(q)

                def ev(mt, lo, n, ps, o):
                    y = Y[mt][:, lo:lo + n]
                    o = tt(y, y, ps, ALU.add, o) if first else act(y, ps, ACT.Copy, o)
                    if end == 22:
                        sums.add(y, lo, n, o)
                    return o

                linear3(sp, 8, end - first, HID, chunks, ev, hid)
            return post2(i, m, "gqf", 5, Y, sums, both, more=i == 0)

        def silu_half(out, x, t, *w):
            o = act(t, x, ACT.Tanh, *w)
            return stt(out, t, 1.0, x, ALU.add, ALU.mult, o)

        def even(m):
            phase()
            for e in "pvag":
                Q.fence[e] += lxc
            sp = load(spill, XREG)
            QKV, GT = tiles(12, ST), tiles(4, ST)
            MIXb = alloc(8 * ST)
            H = [MIXb[:, f * ST:(f + 1) * ST] for f in range(8)]
            RAW = tiles(4, ST)
            AB = alloc(6 * 32)
            mark = pos[0]
            tmp, rst = Ring(tiles(2, S)), alloc(S)
            hw = pre2(0, m, "gpm", 0, 1, H, tmp, True)
            pads = Ring(tiles(2, 776))
            cw = small(60)
            ocw = ts(cw, Pm["gconv"], 0.5, None, ALU.mult, None)
            z = []
            for sl in pads.slots:
                for lo in (0, 514, 516, 774):
                    z.append(memset(sl.ap[:, lo:lo + 2], 0.0))
            rw = [[] for _ in range(4)]
            gw = [[] for _ in range(4)]
            sq, l2 = Ring(tiles(3, ST)), Ring(tiles(2, ST))
            later = Later()
            cur = {}

            def ev(mt, lo, n, ps, o):
                if mt >= 16:
                    o = act(RAW[mt - 16][:, lo:lo + n], ps, ACT.Copy, o)
                    rw[mt - 16].append(o)
                    return o
                if mt >= 12:
                    g = GT[mt - 12][:, lo:lo + n]
                    q = act(g, ps, ACT.Tanh, o, scale=0.5)
                    q = stt(g, g, 1.0, ps, ALU.add, ALU.mult, q)
                    gw[mt - 12].append(q)
                    return q
                if lo == 0:
                    cur["p"] = pads.take()
                    cur["q"] = []
                pd = cur["p"]
                off = 2 if lo == 0 else 518
                o = act(pd.ap[:, off:off + n], ps, ACT.Copy, o, pd.free, z)
                x = QKV[mt][:, lo:lo + n]
                w = lambda j: cw[:, j * 12 + mt:j * 12 + mt + 1]
                q = ts(x, pd.ap[:, off - 2:off - 2 + n], w(0), None, ALU.mult, None, o, ocw)
                for j in range(1, 5):
                    q = stt(x, pd.ap[:, off - 2 + j:off - 2 + j + n], w(j), x, ALU.mult, ALU.add, q)
                q = silu_half(x, x, pd.ap[:, off:off + n], q)
                cur["q"].append(q)
                if lo:
                    pd.free = list(cur["q"])
                    if mt < 8:
                        head_norm(QKV[mt], BOTH, 1.0, 0.125 if mt < 4 else 1.0, sq, l2, later, list(cur["q"]),
                                  lambda w: None, 3)
                return o

            linear("e_in", 20, 8, H, BOTH, ev, hw, each=later.tick)
            later.flush()
            b6 = [bank_slots.take() for _ in range(6)]
            for k in range(8):
                t, tw = W.take("e_in")
                for blk in range(6):
                    o = mm(b6[blk].ap[:, 0:32], H[k][:, blk * 128:(blk + 1) * 128], t[:, 0:32], k == 0, k == 7, tw, hw[k],
                           b6[blk].free if k == 0 else None)
                W.used(o)
            for blk in range(6):
                q = act(AB[:, blk * 32:(blk + 1) * 32], b6[blk].ap[:, 0:32], ACT.Copy, o)
                b6[blk].free = [q]
            Q.barrier()
            for e in "pvag":
                Q.fence[e].append(sp)
            pos[0] = mark
            mla(RAW, MIXb)
            Q.barrier()
            pos[0] = mark - 6 * 32 - 4 * ST
            ab = alloc(192)
            gdn(QKV, GT, MIXb[:, 0:4 * ST], AB, ab)
            MIX = [QKV[f] for f in range(4)] + [MIXb[:, (4 + f) * ST:(5 + f) * ST] for f in range(4)]
            Q.barrier()
            pos[0] = mark - 6 * 32 - 4 * ST
            Y = tiles(8, ST)
            sums = SumSq(alloc(ST), Ring(tiles(2, S)))

            def evy(mt, lo, n, ps, o):
                o = act(Y[mt][:, lo:lo + n], ps, ACT.Copy, o)
                sums.add(Y[mt][:, lo:lo + n], lo, n, o)
                return o

            back = load(XREG, spill)
            linear("e_out", 8, 8, MIX, BOTH, evy, [None] * 8)
            post2(0, m, "gqm", 2, Y, sums, True, w=back)

        def mla(RAW, MIXb):
            QD, KVD, KPE = RAW[0:2], RAW[2], RAW[3]
            OUT = [MIXb[:, (4 + f) * ST:(5 + f) * ST] for f in range(4)]
            VT = [MIXb[:, b * 512:(b + 1) * 512] for b in range(6)]
            save = pos[0]
            tmp, rq, rk = Ring(tiles(3, S)), alloc(ST), alloc(ST)
            for lo, n in BOTH:
                rst = rq[:, lo:lo + n]
                o = norm_stat([q[:, lo:lo + n] for q in QD], n, 256.0, tmp, rst[:, 0:n], [None, None])
                for j in range(2):
                    x = QD[j][:, lo:lo + n]
                    q = stt(x, x, Pm["mqn"][:, j:j + 1], rst[:, 0:n], ALU.mult, ALU.mult, o)
                    ts(x, x, 96.0 ** -0.5, None, ALU.mult, None, q, eng="g")
                rst = rk[:, lo:lo + n]
                o = norm_stat([KVD[:, lo:lo + n]], n, 128.0, tmp, rst[:, 0:n], [None])
                stt(KVD[:, lo:lo + n], KVD[:, lo:lo + n], Pm["mkn"], rst[:, 0:n], ALU.mult, ALU.mult, o)
            Q.barrier()
            rope(KPE, S, K["cosM"], K["sinM"], tmp, None, key="rot32", lo=64, hi=96)
            Q.barrier()
            t, tw = W.take("kvv", 4)
            for b in range(6):
                bk = bank_slots.take()
                o = mm(bk.ap, KVD[:, b * 128:(b + 1) * 128], t, True, True, tw, bk.free)
                bk.free = [act(VT[b], bk.ap, ACT.Copy, o)]
            W.used(o)
            pos[0] = save
            QK = [[(XREG[:, a:a + ST], XREG[:, a + ST:a + 2 * ST]) for a in (4 * ST * y, 4 * ST * y + 2 * ST)]
                  for y in range(2)]
            for y in range(2):
                for hh in range(2):
                    okp = cp(QK[y][hh][1][64:96, :], KPE[64:96, :], eng="g")
            rt = Ring(tiles(2, S))
            Q.barrier()
            qk_ready = {}

            def project(p, hh, ring):
                h = 2 * p + hh
                qh, kh = QK[p % 2][hh]
                bsq = [ring.take() for _ in BOTH]
                for k in range(2):
                    t, tw = W.take("qup")
                    for (lo, n), b in zip(BOTH, bsq):
                        o = mm(b.ap[0:96, 0:n], t[:, 0:96], QD[k][:, lo:lo + n], k == 0, k == 1, tw,
                               b.free if k == 0 else None)
                    W.used(o)
                for (lo, n), b in zip(BOTH, bsq):
                    oq = act(qh[0:96, lo:lo + n], b.ap[0:96, 0:n], ACT.Copy, o)
                    b.free = [oq]
                bsk = [ring.take() for _ in BOTH]
                t, tw = W.take("kvk")
                for (lo, n), b in zip(BOTH, bsk):
                    o = mm(b.ap[0:64, 0:n], t[:, 0:64], KVD[:, lo:lo + n], True, True, tw, b.free)
                W.used(o)
                for (lo, n), b in zip(BOTH, bsk):
                    ok = act(kh[0:64, lo:lo + n], b.ap[0:64, 0:n], ACT.Copy, o)
                    b.free = [ok]
                orp = rope(qh, S, K["cosM"], K["sinM"], rt, [oq], key="rot32", lo=64, hi=96, ring=ring)
                qk_ready[h] = [oq, ok, orp, okp]

            for hh in range(2):
                project(0, hh, bank_slots)

            def hook(i, ring):
                p, r = divmod(i, 12)
                if p < 3 and r in (4, 8):
                    project(p + 1, r // 4 - 1, ring)

            attention(4, 6,
                      lambda h, b: QK[(h // 2) % 2][h % 2][0][0:96, b * 128:(b + 1) * 128],
                      lambda h, b, l, n: QK[(h // 2) % 2][h % 2][1][0:96, (0 if b < 4 else S) + l:(0 if b < 4 else S) + l + n],
                      lambda h, b, j: (VT[(0 if b < 4 else 4) + j][:, h * 64:h * 64 + 64], None),
                      lambda b: ST if b < 4 else C, lambda h, b: None,
                      lambda p: OUT[p], lambda h: qk_ready[h], hook)

        def gdn(QKV, GT, Ob, AB0, AB):
            QT, KT, VT_ = QKV[0:4], QKV[4:8], QKV[8:12]
            O = [Ob[:, b * 512:(b + 1) * 512] for b in range(6)]
            o = cp(AB, AB0)
            Q.barrier()
            G, B = alloc(96), alloc(96)
            z, z2, mx, spx = alloc(96), alloc(96), alloc(96), alloc(96)
            ea = alloc(16)
            v3 = lambda a: a.rearrange("p (b c) -> p b c", b=6)
            o = tt(v3(spx), v3(AB)[:, :, 0:16], Pm["dtb"].unsqueeze(1).broadcast_to([128, 6, 16]), ALU.add)
            o = softplus(G, spx, 1.0, z, z2, mx, o)
            o2 = act(ea, Pm["alog"], ACT.Exp)
            o = stt(v3(G), v3(G), -1.0, ea.unsqueeze(1).broadcast_to([128, 6, 16]), ALU.mult, ALU.mult, o, o2)
            o = act(v3(B), v3(AB)[:, :, 16:32], ACT.Tanh, scale=0.5)
            o = ts(B, B, 0.5, 0.5, ALU.mult, ALU.add, o)
            Q.barrier()
            NG, EG, FT, GL, GLP = alloc(96), alloc(96), alloc(96), alloc(96), alloc(48)
            bg, bt = bank_slots.take(), bank_slots.take()
            for c in range(6):
                for d, tri in enumerate(("triF", "triB")):
                    j = c * 16 + d * 8
                    mm(bg.ap[:, j:j + 8], K[tri], G[:, j:j + 8], True, True, bg.free)
                    o = mm(bt.ap[:, j:j + 8], ones, G[:, j:j + 8], True, True, bt.free)
            o1 = act(NG, bg.ap[:, 0:96], ACT.Copy, o, scale=-1.0)
            o2 = act(EG, bg.ap[:, 0:96], ACT.Exp, o)
            o3 = act(GL, bt.ap[:, 0:96], ACT.Exp, o)
            q = tt(FT, bt.ap[:, 0:96], NG, ALU.add, o1, o3)
            bg.free, bt.free = [o2], [o3, q]
            act(FT, FT, ACT.Exp, q)
            gl2 = GL.rearrange("p (x two) -> p x two", two=2)
            cp(GLP[0:64, :], gl2[0:64, :, 0], o3)
            cp(GLP[64:128, :], gl2[64:128, :, 1], o3)
            ST_ = tiles(2, 256)
            BE = alloc(96)
            tt(BE, B, EG, ALU.mult, o2)
            for d in range(2):
                memset(ST_[d], 0.0)
            for b in range(6):
                memset(O[b], 0.0)
            Q.barrier()
            KTOK, VTOK, U, WT, KD = (tiles(2, 512) for _ in range(5))
            AT = tiles(2, 1024)
            work = [XREG[:, i * 512:(i + 1) * 512] for i in range(12)] + tiles(4, 512)
            D, DT, MT, Y = work[0:4], work[4:8], work[8:12], work[12:16]
            h3 = lambda a: a.rearrange("p (h d) -> p h d", d=64)
            g3 = lambda a: a.rearrange("p (h d) -> p h d", d=128)
            two = lambda a, y: a.rearrange("p (x two c) -> p x two c", two=2, c=64)[:, :, y, :]
            bc = lambda a, n: a.unsqueeze(2).broadcast_to([128, a.shape[1], n])
            rep = lambda a: a.unsqueeze(1).broadcast_to([128, 4, 128])
            par = lambda y: slice(64 * y, 64 * y + 64)
            col = lambda x, w=128: slice(x * w, (x + 1) * w)
            tok = (4, 5, 0, 1, 2, 3), (5, 4, 3, 2, 1, 0)
            grp = [(d, y) for d in range(2) for y in range(2)]
            none = lambda n: [[] for _ in range(n)]
            kt_free, vt_free, kd_free, at_free, u_free, wt_free = (none(2) for _ in range(6))
            y_free, dt_free, s_op = none(4), none(4), none(2)
            o_op = none(6)
            for step in range(6):
                cs = [tok[d][step] for d in range(2)]
                kb, vb, kd = [None] * 2, [None] * 2, [None] * 2
                for d in range(2):
                    cl, j0 = col(cs[d]), cs[d] * 16 + d * 8
                    ev = []
                    for src, dst, free in ((KT, KTOK[d], kt_free[d]), (VT_, VTOK[d], vt_free[d])):
                        b = bank_slots.take()
                        for f in range(4):
                            o = tr(b.ap[:, col(f)], src[f][:, cl], ident, b.free)
                        ev.append(act(dst, b.ap, ACT.Copy, o, free))
                        b.free = [ev[-1]]
                    kd[d] = tt(h3(KD[d]), h3(KTOK[d]), bc(FT[:, j0:j0 + 8], 64), ALU.mult, ev[0], kd_free[d])
                    vb[d] = tt(h3(VTOK[d]), h3(VTOK[d]), bc(B[:, j0:j0 + 8], 64), ALU.mult, ev[1], eng="g")
                    kb[d] = tt(h3(KTOK[d]), h3(KTOK[d]), bc(BE[:, j0:j0 + 8], 64), ALU.mult, ev[0], kd[d], eng="g")
                mt_op, d_op, dt_op, at_op = [None] * 4, [None] * 4, [None] * 4, [None] * 4
                for gi, (d, y) in enumerate(grp):
                    cl, j0 = col(cs[d]), cs[d] * 16 + d * 8
                    tri, neg = (("triF", "negF"), ("triB", "negB"))[d]
                    gcol = [j0 + 2 * x + y for x in range(4)]
                    b, bk, bq, bb = (bank_slots.take() for _ in range(4))
                    for x, j in enumerate(gcol):
                        o = mm(b.ap[:, col(x)], G[:, j:j + 1].broadcast_to([128, 128]), K[tri], True, True, b.free)
                    o = tt(g3(Y[gi]), g3(b.ap), rep(K[neg]), ALU.add, o, y_free[gi])
                    b.free = [o]
                    for x, j in enumerate(gcol):
                        od = act(Y[gi][:, col(x)], Y[gi][:, col(x)], ACT.Exp, o, bias=NG[:, j:j + 1])
                    for x, j in enumerate(gcol):
                        k_, q_ = KT[x][par(y), cl], QT[x][par(y), cl]
                        mm(bk.ap[:, col(x)], k_, k_, True, True, bk.free)
                        mm(bq.ap[:, col(x)], k_, q_, True, True, bq.free)
                    for x, j in enumerate(gcol):
                        o = mm(bb.ap[:, col(x)], B[:, j:j + 1].broadcast_to([128, 128]), ident, True, True, bb.free)
                    av = AT[d].rearrange("p (x two c) -> p x two c", two=2, c=128)[:, :, y, :]
                    at_op[gi] = tt(av, g3(bq.ap), g3(Y[gi]), ALU.mult, o, od, at_free[d])
                    a2 = tt(MT[gi], bk.ap, Y[gi], ALU.mult, o, od, y_free[gi])
                    mt_op[gi] = tt(MT[gi], bb.ap, MT[gi], ALU.mult, a2)
                    y_free[gi] = [at_op[gi], a2]
                    bq.free, bk.free, bb.free = [at_op[gi]], [a2], [mt_op[gi]]
                    m0 = K[("lvB", "lvF")[d]][:, 0:128]
                    beside = "v" if gi == 3 else "g"
                    o = tt(g3(DT[gi]), g3(MT[gi]), rep(m0), ALU.mult, mt_op[gi], dt_free[gi], eng=beside)
                    dt_op[gi] = tt(g3(DT[gi]), rep(ident), g3(DT[gi]), ALU.subtract, o, eng=beside)
                for gi in range(4):
                    b = bank_slots.take()
                    for x in range(4):
                        o = tr(b.ap[:, col(x)], DT[gi][:, col(x)], ident, dt_op[gi], b.free)
                    d_op[gi] = act(D[gi], b.ap, ACT.Copy, o)
                    b.free = [d_op[gi]]
                for lv in range(1, 6):
                    oy = [None] * 4
                    for gi, (d, y) in enumerate(grp):
                        b = bank_slots.take()
                        for x in range(4):
                            o = mm(b.ap[:, col(x)], MT[gi][:, col(x)], D[gi][:, col(x)], True, True, mt_op[gi], d_op[gi],
                                   b.free)
                        oy[gi] = tt(g3(Y[gi]), g3(b.ap), rep(K[("lvF", "lvB")[d]][:, col(lv)]), ALU.mult, o, y_free[gi])
                        b.free = [oy[gi]]
                    for gi in range(4):
                        b = bank_slots.take()
                        for x in range(4):
                            o = mm(b.ap[:, col(x)], DT[gi][:, col(x)], Y[gi][:, col(x)], True, True, oy[gi], dt_op[gi],
                                   b.free)
                        d_op[gi] = tt(D[gi], D[gi], b.ap, ALU.subtract, o, d_op[gi])
                        b.free = [d_op[gi]]
                        y_free[gi] = [o]
                    for gi in range(4):
                        b = bank_slots.take()
                        for x in range(4):
                            o = tr(b.ap[:, col(x)], D[gi][:, col(x)], ident, d_op[gi], b.free)
                        dt_op[gi] = act(DT[gi], b.ap, ACT.Copy, o)
                        b.free = [dt_op[gi]]
                oy = [None] * 4
                for gi, (d, y) in enumerate(grp):
                    r, c = par(1 - d), par(d)
                    b = bank_slots.take()
                    for x in range(4):
                        o = mm(b.ap[r, col(x, 64)], g3(MT[gi])[c, x, r], g3(D[gi])[c, x, c], True, True, mt_op[gi],
                               d_op[gi], b.free)
                    oy[gi] = act(g3(Y[gi])[r, :, c], h3(b.ap[r, 0:256]), ACT.Copy, o, y_free[gi])
                    b.free = [oy[gi]]
                for gi, (d, y) in enumerate(grp):
                    r, c = par(1 - d), par(d)
                    b = bank_slots.take()
                    for x in range(4):
                        o = mm(b.ap[c, col(x, 64)], g3(Y[gi])[r, x, c], g3(DT[gi])[r, x, r], True, True, oy[gi],
                               dt_op[gi], b.free)
                    t_ = g3(DT[gi])[c, :, r]
                    dt_op[gi] = tt(t_, t_, h3(b.ap[c, 0:256]), ALU.subtract, o, dt_op[gi])
                    b.free = [dt_op[gi]]
                    y_free[gi] = [o]
                u_op, w_op = [None] * 2, [None] * 2
                for d in range(2):
                    b, b2 = bank_slots.take(), bank_slots.take()
                    for h in range(8):
                        t_ = DT[2 * d + h % 2][:, col(h // 2)]
                        o = mm(b.ap[:, col(h, 64)], t_, VTOK[d][:, col(h, 64)], True, True, b.free, vb[d],
                               dt_op[2 * d:2 * d + 2])
                    u_op[d] = act(U[d], b.ap, ACT.Copy, o, u_free[d])
                    vt_free[d] = [o]
                    for h in range(8):
                        t_ = DT[2 * d + h % 2][:, col(h // 2)]
                        o = mm(b2.ap[par(h % 2), col(h // 2)], KTOK[d][:, col(h, 64)], t_, True, True, b2.free, kb[d])
                    w_op[d] = act(WT[d], b2.ap, ACT.Copy, o, wt_free[d])
                    kt_free[d] = [o]
                    dt_free[2 * d] = dt_free[2 * d + 1] = [o]
                    b.free, b2.free = [u_op[d]], [w_op[d]]
                nv, qs = [[], []], [[], []]
                for d in range(2):
                    cl, j0 = col(cs[d]), cs[d] * 16 + d * 8
                    for y in range(2):
                        b = bank_slots.take()
                        for x in range(4):
                            s_ = ST_[d][par(y), col(x, 64)]
                            mm(b.ap[:, col(x, 64)], WT[d][par(y), col(x)], s_, True, True, b.free, w_op[d], s_op[d])
                            o = mm(b.ap[:, 256 + x * 64:256 + (x + 1) * 64], QT[x][par(y), cl], s_, True, True)
                        nv[d].append(tt(two(U[d], y), two(U[d], y), h3(b.ap[:, 0:256]), ALU.subtract, o, u_op[d]))
                        eg = EG[:, j0:j0 + 8].rearrange("p (x two) -> p x two", two=2)[:, :, y]
                        qs[d].append(tt(two(VTOK[d], y), h3(b.ap[:, 256:512]), bc(eg, 64), ALU.mult, o, vt_free[d]))
                        b.free = [nv[d][-1], qs[d][-1]]
                    wt_free[d] = [o]
                for d in range(2):
                    j0 = cs[d] * 16 + d * 8
                    if step < 5:
                        b = bank_slots.take()
                        for h in range(8):
                            o = mm(b.ap[par(h % 2), col(h // 2, 64)], KD[d][:, col(h, 64)], U[d][:, col(h, 64)], True,
                                   True, nv[d], kd[d], b.free)
                        kd_free[d] = [o]
                        q = tt(h3(ST_[d]), h3(ST_[d]), bc(GLP[:, j0 // 2:j0 // 2 + 4], 64), ALU.mult, wt_free[d])
                        q = tt(ST_[d], ST_[d], b.ap[:, 0:256], ALU.add, q, o)
                        b.free = s_op[d] = [q]
                    bo = bank_slots.take()
                    for h in range(8):
                        o = mm(bo.ap[:, col(h, 64)], AT[d][:, col(h)], U[d][:, col(h, 64)], True, True, nv[d], at_op,
                               bo.free)
                    at_free[d] = u_free[d] = [o]
                    q = tt(VTOK[d], VTOK[d], bo.ap, ALU.add, qs[d], o)
                    bo.free = [q]
                    c = cs[d]
                    q = tt(O[c], O[c], VTOK[d], ALU.add, q, o_op[c], eng="g")
                    o_op[c] = vt_free[d] = [q]
            Q.barrier()
            hg_ = small(1)
            oh = ts(hg_, Pm["onorm"], 0.5, None, ALU.mult, None)
            sq = Ring([U[0], KTOK[0]])
            rr = WT[0][:, 0:48]
            rs = []
            for b in range(6):
                t = sq.take()
                o = act(t.ap, O[b], ACT.Square, t.free)
                rs.append(red(rr[:, 8 * b:8 * b + 8], h3(t.ap), ALU.add, o))
                t.free = [rs[-1]]
            o = act(rr, rr, ACT.Ln, rs, scale=1.0 / 64, bias=K["eps"])
            orr = act(rr, rr, ACT.Exp, o, scale=-0.5)
            for b in range(6):
                o = tt(h3(O[b]), h3(O[b]), bc(rr[:, 8 * b:8 * b + 8], 64), ALU.mult, orr)
                bk = bank_slots.take()
                for f in range(4):
                    q = tr(bk.ap[:, f * 128:(f + 1) * 128], O[b][:, f * 128:(f + 1) * 128], ident, o, bk.free)
                for f in range(4):
                    sl = slice(b * 128, (b + 1) * 128)
                    q2 = stt(QKV[f][:, sl], bk.ap[:, f * 128:(f + 1) * 128], hg_, GT[f][:, sl], ALU.mult, ALU.mult, q, oh)
                bk.free = [q2]

        def odd(m):
            phase()
            H = tiles(8, ST)
            NQ, NK_, NV = tiles(4, S), tiles(4, ST), tiles(6, 512)
            GQ, GK, GV = tiles(4, S), tiles(2, ST), tiles(6, 128)
            RP = tiles(2, S)
            lr = load(RP[0], d_rope[:, 2 * S:3 * S]), load(RP[1], d_rope[:, 3 * S:4 * S])
            Q.barrier("a")
            mark = pos[0]
            tmp, rst, sq = Ring(tiles(2, S)), Ring(tiles(2, ST)), Ring(tiles(3, ST))
            later = Later()
            g8 = small(1)
            og8 = ts(g8, Pm["gqn"], 0.125, None, ALU.mult, None)
            hw = pre2(1, m, "gpm", 0, 1, H, tmp, True)

            def ev(mt, lo, n, ps, o):
                if mt < 4:
                    return act(NQ[mt], ps, ACT.Copy, o, scale=0.125)
                if mt < 8:
                    return act(NK_[mt - 4][:, lo:lo + n], ps, ACT.Copy, o)
                x = GQ[mt - 8] if mt < 12 else GK[mt - 12]
                o = act(x[:, lo:lo + n], ps, ACT.Copy, o)
                done.setdefault(mt, []).append(o)
                chunks = LAT if mt < 12 else BOTH
                if len(done[mt]) == len(chunks):
                    head_norm(x, chunks, 64.0, g8 if mt < 12 else Pm["gkn"], sq, rst, later, [done[mt], og8],
                              lambda w: later.put(1, lambda: rope(x, S, RP[0], RP[1], tmp, [w, lr])))
                return o

            done = {}
            linear("o_in", 4, 8, H, LAT, ev, hw)
            linear("o_in", 4, 8, H, BOTH, lambda mt, *a: ev(mt + 4, *a), hw)
            linear("o_in", 4, 8, H, LAT, lambda mt, *a: ev(mt + 8, *a), hw, each=later.tick)
            linear("o_in", 2, 8, H, BOTH, lambda mt, *a: ev(mt + 12, *a), hw, each=later.tick)
            later.tick()
            for name, n, dst in (("nav", 4, NV), ("gv", 1, GV)):
                b6 = [bank_slots.take() for _ in range(6)]
                for k in range(8):
                    t, tw = W.take(name, n)
                    for b in range(6):
                        o = mm(b6[b].ap[:, 0:n * 128], H[k][:, b * 128:(b + 1) * 128], t, k == 0, k == 7, tw, hw[k],
                               b6[b].free if k == 0 else None)
                    W.used(o)
                for b in range(6):
                    b6[b].free = [act(dst[b], b6[b].ap[:, 0:n * 128], ACT.Copy, o)]
                later.flush()
            Q.barrier()
            OUT = [H[f][:, 0:S] for f in range(8)]
            pos[0] = mark
            TB = tiles(4, 896)
            tw = {}

            def bias(p, *w):
                for h in (2 * p, 2 * p + 1):
                    l = load(TB[h % 4], d_rpb[h, :, :], *w, eng="s")
                    t3 = TB[h % 4].rearrange("p (e k) -> p e k", k=64)
                    tw[h] = tt(t3, t3, K["namask"].unsqueeze(1).broadcast_to([128, 14, 64]), ALU.add, l, eng="g")

            fenced = Q.last
            for p in range(2):
                bias(p, fenced)

            def hook(i, ring):
                if i in (9, 17):
                    bias(i // 8 + 1, Q.q["v"][-1])

            def half(a, h):
                return a[64 * (h % 2):64 * (h % 2) + 64, :]

            attention(8, 4,
                      lambda h, b: half(NQ[h // 2] if h < 8 else GQ[h // 2 - 4], h)[:, b * 128:(b + 1) * 128],
                      lambda h, b, l, n: half(NK_[h // 2] if h < 8 else GK[(h - 8) // 4], h)[:, l:l + n],
                      lambda h, b, j: (NV[j][:, h * 64:h * 64 + 64] if h < 8 else
                                       GV[j][:, ((h - 8) // 4) * 64:((h - 8) // 4) * 64 + 64], None),
                      lambda b: ST,
                      lambda h, b: (512, TB[h % 4][:, (6 - 2 * b) * 64:(14 - 2 * b) * 64], tw[h]) if h < 8 else None,
                      lambda p: OUT[p], lambda h: None, hook)
            pos[0] = mark
            Y = [a for a in NK_] + [alloc(S)[:, 0:S] for _ in range(4)]
            Y = [y[:, 0:S] for y in Y]
            sums = SumSq(alloc(S), Ring(tiles(2, S)))

            def evy(mt, lo, n, ps, o):
                o = act(Y[mt], ps, ACT.Copy, o)
                sums.add(Y[mt], 0, S, o)
                return o

            linear("o_out", 8, 8, OUT, LAT, evy, [None] * 8)
            post2(1, m, "gqm", 2, Y, sums, False)

        def body():
            rglru(MOD1[:, 0:48])
            ffn1(0, MOD1[:, 0:48])
            dsa(MOD1[:, 48:96])
            ffn1(1, MOD1[:, 48:96])
            for i in range(2):
                m = [(part(MOD2[:, 96 * i:96 * i + 96], s, 2, 0), part(MOD2[:, 96 * i:96 * i + 96], s, 2, 1))
                     for s in range(6)]
                if i == 0:
                    even(m)
                else:
                    odd(m)
                ffn2(i, m, i == 0)
            Q.barrier("a")
            for f in range(8):
                load(d_out[f, :, :], X[f])

        body()

        sems = {e: es.enter_context(nc.semaphore(f"s_{n}")) for e, n in
                zip("pvagsd", ("tensor", "vector", "scalar", "gpsimd", "sync", "none"))}
        dsems = {e: [es.enter_context(nc.semaphore(f"d_{e}{i}")) for i in range(Q.NDMA)] for e in "as"}
        Q.number(sems, dsems)
        block = es.enter_context(nc.Block())

        @block.sync
        def _(e):
            Q.emit("s", e)

        @block.scalar
        def _(e):
            Q.emit("a", e)

        @block.tensor
        def _(e):
            Q.emit("p", e)

        @block.vector
        def _(e):
            Q.emit("v", e)

        @block.gpsimd
        def _(e):
            Q.emit("g", e)


def pack_weights(a):
    def pad(w, m):
        return np.pad(w, ((0, 0), (0, m - w.shape[1])))

    b, e, o = a["b_w_in"][0], a["w_in_even_2"][0], a["w_in_odd_2"][0]
    up, kv = a["mla_w_q_up_2"][0], a["mla_w_kv_up_2"][0].reshape(128, 8, 128)
    mats = {
        "a_in": a["a_w_in"][0], "a_out": a["a_w_out"][0],
        "gr": a["a_gate_r_w"][0].reshape(1280, 256), "gi": a["a_gate_i_w"][0].reshape(1280, 256),
        "b_in": np.concatenate([b[:, 0:1024], b[:, 1024:1088], b[:, 1024:1088], b[:, 1152:1664], b[:, 1664:1728],
                                b[:, 1664:1728], pad(np.concatenate([b[:, 1088:1152], b[:, 1728:1736]], 1), 128)], 1),
        "b_out": a["b_w_out"][0],
        "e_in": np.concatenate([e[:, 0:2048], e[:, 2080:2464], np.pad(e[:, 2464:2496], ((0, 0), (64, 32))),
                                pad(e[:, 2048:2080], 128)], 1),
        "e_out": a["w_out_even_2"][0],
        "kvv": kv[:, :, 64:].reshape(128, 512),
        "kvk": np.pad(kv[:, :, :64], ((0, 0), (0, 0), (0, 64))).reshape(128, 1024),
        "qup": np.pad(up.reshape(256, 8, 96), ((0, 0), (0, 0), (0, 32))).reshape(256, 1024),
        "o_in": np.concatenate([o[:, 0:1024], o[:, 1536:2048], o[:, 2048:2112], o[:, 2048:2112], o[:, 2112:2176],
                                o[:, 2112:2176]], 1),
        "nav": o[:, 1024:1536], "gv": o[:, 2176:2304], "o_out": a["w_out_odd_2"][0],
    }
    for i in range(2):
        mats[f"f1_{i}"], mats[f"f2_{i}"] = a["ffn_w1"][i], a["ffn_w2"][i]
        mats[f"g_{i}"], mats[f"u_{i}"], mats[f"d_{i}"] = (a["w_ffn_gate_2"][i], a["w_ffn_up_2"][i],
                                                          a["w_ffn_down_2"][i])
    plan = weight_plan()
    npanel = -(-len(plan) // PANEL)
    w = np.zeros((npanel, 128, PANEL, 128), np.float32)
    for i, t in enumerate(plan):
        if t is not None:
            name, k, m = t
            w[i // PANEL, :, i % PANEL, :] = mats[name][k * 128:(k + 1) * 128, m * 128:(m + 1) * 128]
    return w.reshape(npanel, 128, PANEL * 128)


def pack_modulation(a):
    m = np.concatenate([a["ada_w"], a["w_mod_2"]]).reshape(4, 8, 128, 12, 512)
    return np.ascontiguousarray(m.transpose(0, 3, 2, 1, 4)).reshape(48, 128, 4096)


def pack_params(a):
    def cols(v):
        return np.asarray(v).reshape(-1, 128).T

    def rows(v):
        return np.broadcast_to(np.asarray(v).reshape(1, -1), (128, v.size))

    def two(v):
        return np.concatenate([v, v]).reshape(128, 1)

    p = {
        "gmix": cols(a["norm_mix_g"]), "gffn": cols(a["norm_ffn_g"]), "ada_b": cols(a["ada_b"]),
        "convw": cols(a["a_conv_w"]), "convb": cols(a["a_conv_b"]), "rb": cols(a["a_gate_r_b"]),
        "ib": cols(a["a_gate_i_b"]), "lam": cols(a["a_lambda"]), "qg": two(a["b_q_norm_g"][0]),
        "kg": two(a["b_k_norm_g"][0]), "c1": cols(a["c"]),
        "c2": np.stack([cols(a["c_2"]), cols(a["c_ctx_2"])], 2).reshape(128, 16),
        "mod_b": cols(a["b_mod_2"]), "gpm": cols(a["g_pre_mix_2"]), "gqm": cols(a["g_post_mix_2"]),
        "gpf": cols(a["g_pre_ffn_2"]), "gqf": cols(a["g_post_ffn_2"]), "gconv": cols(a["gdn_conv_2"]),
        "alog": rows(a["gdn_a_log_2"]), "dtb": rows(a["gdn_dt_bias_2"]), "onorm": two(a["gdn_out_norm_2"][0]),
        "mqn": cols(a["mla_q_norm_2"]), "mkn": cols(a["mla_kv_norm_2"]), "gqn": two(a["gqa_q_norm_2"][0]),
        "gkn": two(a["gqa_k_norm_2"][0]),
    }
    return np.ascontiguousarray(np.concatenate([p[n] for n in PARAMS], 1))


def pack_rpb(rpb):
    t = np.pad(rpb, ((0, 0), (0, 0), (48, 48)))
    out = np.empty((8, 2, 64, 14, 64), np.float32)
    for rr in range(2):
        for col in range(64):
            out[:, rr, col] = t[:, 1 - rr:15 - rr, 63 - col:127 - col]
    return out.reshape(8, 128, 896)


def arrays_of(a):
    cst, ropes = constants()
    return {
        "in_w": pack_weights(a), "in_ada": pack_modulation(a), "in_const": cst, "in_rope": ropes, "in_par": pack_params(a),
        "in_rpb": pack_rpb(a["na_rpb_2"][0]),
        "in_x": np.ascontiguousarray(a["x"][0].T.reshape(8, 128, S)),
        "in_ctx": np.ascontiguousarray(a["ctx_2"][0].T.reshape(8, 128, C)),
    }


def build(nc, arrays):
    aps = [nc.dram_tensor(n, list(v.shape), F32, kind="ExternalInput").ap() for n, v in arrays.items()]
    out = nc.dram_tensor("out_y", [8, 128, S], F32, kind="ExternalOutput").ap()
    program(nc, *aps, out)


def kernel(**inputs):
    import concourse.bacc as bacc
    from concourse.bass_utils import run_bass_kernel_spmd as run

    arrays = arrays_of({k: np.asarray(v) for k, v in inputs.items()})
    nc = bacc.Bacc("TRN2", target_bir_lowering=False, num_devices=1)
    build(nc, arrays)
    r = run(nc, [arrays], core_ids=[0])
    y = r.results[0]["out_y"]
    return np.ascontiguousarray(y.reshape(1024, S).T).reshape(1, S, 1024)
```
